# Optimizing a Trainium2 kernel written in Bass

```python
import functools
import jax, jax.numpy as jnp
from jax import lax
import numpy as np

D_MODEL = 1024
BATCH = 1
SEQ = 512
DEPTH = 2
DEC_BATCH = 8
DEC_SEQ = 4
PAST_LEN = 2048
PAGE_SIZE = 128

MIX_WIDTH = D_MODEL
HEAD_DIM = 64
GLA_HEADS = 4
GLA_DV = (MIX_WIDTH // 2) // GLA_HEADS
GLA_DK = GLA_DV // 2
GLA_QK_W = GLA_HEADS * GLA_DK
GLA_V_W = GLA_HEADS * GLA_DV
GATE_RANK = 16
GATE_NORM = 16.0
GLA_CHUNK = 64
SWA_HEADS = (MIX_WIDTH - GLA_V_W) // HEAD_DIM
SWA_KV_HEADS = 2
SWA_GROUP = SWA_HEADS // SWA_KV_HEADS
SWA_Q_W = SWA_HEADS * HEAD_DIM
SWA_KV_W = SWA_KV_HEADS * HEAD_DIM
WINDOW = 128
ROT_DIM = HEAD_DIM // 4
ROPE_THETA = 500000.0
D_FF = 2816
EPS = 1e-6
IN_SPLITS = (GLA_QK_W, GLA_QK_W, GLA_V_W, GLA_V_W, GATE_RANK, SWA_Q_W, SWA_KV_W, SWA_KV_W)
IN_WIDTH = 2 * GLA_QK_W + 2 * GLA_V_W + GATE_RANK + SWA_Q_W + 2 * SWA_KV_W

kernel_name = 'hymba_gla_swa_macaron_step'

def rmsnorm(x, g):
    xf = x.astype(jnp.float32)
    y = xf * lax.rsqrt(jnp.mean(xf * xf, axis=-1, keepdims=True) + EPS)
    return (y * g.astype(jnp.float32)).astype(x.dtype)

def swiglu(h, w_gu, w_down):
    gate, up = jnp.split(h @ w_gu, 2, axis=-1)
    return (jax.nn.silu(gate) * up) @ w_down

def rope_partial(x, pos):
    half = ROT_DIM // 2
    inv = jnp.power(jnp.float32(ROPE_THETA), -jnp.arange(half, dtype=jnp.float32) * (2.0 / ROT_DIM))
    ang = pos.astype(jnp.float32)[:, None] * inv[None, :]
    cos = jnp.cos(ang)[None, :, None, :].astype(x.dtype)
    sin = jnp.sin(ang)[None, :, None, :].astype(x.dtype)
    x1 = x[..., :half]
    x2 = x[..., half:ROT_DIM]
    return jnp.concatenate([x1 * cos - x2 * sin, x2 * cos + x1 * sin, x[..., ROT_DIM:]], axis=-1)

def gla_chunked(q, k, v, g, s0):
    B, L, H, _ = q.shape
    C = min(GLA_CHUNK, L)
    n = -(-L // C)
    pad = n * C - L

    def blocks(t):
        t = jnp.pad(t.astype(jnp.float32), ((0, 0), (0, pad), (0, 0), (0, 0)))
        return t.reshape(B, n, C, H, t.shape[-1]).transpose(1, 0, 3, 2, 4)

    causal = jnp.tril(jnp.ones((C, C), dtype=bool))

    def step(S, inp):
        qc, kc, vc, gc = inp
        b = jnp.cumsum(gc, axis=-2)
        b_last = b[..., -1:, :]
        qb = qc * jnp.exp(b)
        att = jnp.where(causal, jnp.einsum('bhid,bhjd->bhij', qb, kc * jnp.exp(-b)), 0.0)
        o = jnp.einsum('bhij,bhjv->bhiv', att, vc) + jnp.einsum('bhid,bhdv->bhiv', qb, S)
        S = jnp.exp(b_last[..., 0, :])[..., None] * S + jnp.einsum('bhjd,bhjv->bhdv', kc * jnp.exp(b_last - b), vc)
        return S, o

    S, o = lax.scan(step, s0.astype(jnp.float32), (blocks(q), blocks(k), blocks(v), blocks(g)))
    o = o.transpose(1, 0, 3, 2, 4).reshape(B, n * C, H, -1)[:, :L]
    return o, S

def sink_attention(q, k, v, q_pos, k_pos, sinks):
    B, N, Q = q.shape[:3]
    qg = q.reshape(B, N, Q, SWA_KV_HEADS, SWA_GROUP, HEAD_DIM)
    s = jnp.einsum('bnqhgd,bnkhd->bnhgqk', qg, k, preferred_element_type=jnp.float32) * (HEAD_DIM ** -0.5)
    qp = q_pos[:, :, None]
    kp = k_pos[:, None, :]
    mask = (kp <= qp) & (kp > qp - WINDOW) & (kp >= 0)
    s = jnp.where(mask[None, :, None, None], s, -jnp.inf)
    sink = sinks.astype(jnp.float32).reshape(SWA_KV_HEADS, SWA_GROUP)[:, :, None, None]
    m = jnp.maximum(jnp.max(s, axis=-1, keepdims=True), sink)
    p = jnp.exp(s - m)
    probs = p / (jnp.sum(p, axis=-1, keepdims=True) + jnp.exp(sink - m))
    o = jnp.einsum('bnhgqk,bnkhd->bnqhgd', probs.astype(v.dtype), v)
    return o.reshape(B, N * Q, SWA_HEADS * HEAD_DIM)

def swa_prompt(q, k, v, sinks):
    B, L = q.shape[:2]
    nb = L // WINDOW
    qb = q.reshape(B, nb, WINDOW, SWA_HEADS, HEAD_DIM)

    def ctx(t):
        tp = jnp.pad(t, ((0, 0), (WINDOW, 0), (0, 0), (0, 0))).reshape(B, nb + 1, WINDOW, SWA_KV_HEADS, HEAD_DIM)
        return jnp.concatenate([tp[:, :-1], tp[:, 1:]], axis=2)

    q_pos = jnp.arange(L).reshape(nb, WINDOW)
    k_pos = jnp.concatenate([q_pos - WINDOW, q_pos], axis=1)
    out = sink_attention(qb, ctx(k), ctx(v), q_pos, k_pos, sinks)
    wb = min(WINDOW, L)
    return out, k[:, L - wb:], v[:, L - wb:]

def swa_sample(q, k, v, sinks, *, k_buf, v_buf, pos):
    wb = k_buf.shape[1]
    k_all = jnp.concatenate([k_buf.astype(k.dtype), k], axis=1)
    v_all = jnp.concatenate([v_buf.astype(v.dtype), v], axis=1)
    k_pos = jnp.concatenate([PAST_LEN - wb + jnp.arange(wb), pos])[None]
    out = sink_attention(q[:, None], k_all[:, None], v_all[:, None], pos[None], k_pos, sinks)
    return out, k_all[:, -wb:], v_all[:, -wb:]

def layer(x, pos, gla_s0, swa_fn, p):
    (n1, ffn1_gu, ffn1_down, n_mix, w_in, w_a2, b_a, gla_g, sinks, swa_g, w_out, n2, ffn2_gu, ffn2_down) = p
    x = x + 0.5 * swiglu(rmsnorm(x, n1), ffn1_gu, ffn1_down)
    h = rmsnorm(x, n_mix)
    B, L, _ = h.shape
    offs = np.cumsum(IN_SPLITS)[:-1].tolist()
    qg, kg, vg, rg, a_low, qs, ks, vs = jnp.split(h @ w_in, offs, axis=-1)

    def heads(t, nh):
        return t.reshape(B, L, nh, -1)

    log_a = jax.nn.log_sigmoid((a_low @ w_a2 + b_a).astype(jnp.float32)) / GATE_NORM
    o_g, s_new = gla_chunked(heads(qg, GLA_HEADS) * (GLA_DK ** -0.5), heads(kg, GLA_HEADS),
                             heads(vg, GLA_HEADS), heads(log_a, GLA_HEADS), gla_s0)
    o_g = o_g * lax.rsqrt(jnp.mean(o_g * o_g, axis=-1, keepdims=True) + EPS)
    o_g = (o_g.reshape(B, L, GLA_V_W) * gla_g.astype(jnp.float32)
           * jax.nn.silu(rg.astype(jnp.float32))).astype(x.dtype)
    qs = rope_partial(heads(qs, SWA_HEADS), pos)
    ks = rope_partial(heads(ks, SWA_KV_HEADS), pos)
    vs = heads(vs, SWA_KV_HEADS)
    o_s, k_keep, v_keep = swa_fn(qs, ks, vs, sinks)
    o_s = rmsnorm(o_s, swa_g)
    x = x + jnp.concatenate([o_g, o_s.astype(x.dtype)], axis=-1) @ w_out
    x = x + 0.5 * swiglu(rmsnorm(x, n2), ffn2_gu, ffn2_down)
    return x, s_new.astype(gla_s0.dtype), k_keep, v_keep

def setup_inputs(seed: int = 0) -> dict:
    key = jax.random.key(seed)
    ks = jax.random.split(key, 24)
    f32 = jnp.float32
    win_buf = min(WINDOW, PAST_LEN)

    def nrm(k, shape, scale):
        return jax.random.normal(k, shape, f32) * scale

    def gain(k, shape):
        return 1.0 + 0.02 * jax.random.normal(k, shape, f32)

    return {
        'x_prompt': nrm(ks[0], (BATCH, SEQ, D_MODEL), 1.0),
        'x_sample': nrm(ks[1], (DEC_BATCH, DEC_SEQ, D_MODEL), 1.0),
        'state_gla': nrm(ks[2], (DEPTH, DEC_BATCH, GLA_HEADS, GLA_DK, GLA_DV), 0.5),
        'cache_swa_k': nrm(ks[3], (DEPTH, DEC_BATCH, win_buf, SWA_KV_HEADS, HEAD_DIM), 1.0),
        'cache_swa_v': nrm(ks[4], (DEPTH, DEC_BATCH, win_buf, SWA_KV_HEADS, HEAD_DIM), 1.0),
        'norm_ffn1': gain(ks[5], (DEPTH, D_MODEL)),
        'w_ffn1_gu': nrm(ks[6], (DEPTH, D_MODEL, 2 * D_FF), D_MODEL ** -0.5),
        'w_ffn1_down': nrm(ks[7], (DEPTH, D_FF, D_MODEL), D_FF ** -0.5),
        'norm_mix': gain(ks[8], (DEPTH, D_MODEL)),
        'w_in': nrm(ks[9], (DEPTH, D_MODEL, IN_WIDTH), D_MODEL ** -0.5),
        'w_gate_up': nrm(ks[10], (DEPTH, GATE_RANK, GLA_QK_W), GATE_RANK ** -0.5),
        'b_gate': nrm(ks[11], (DEPTH, GLA_QK_W), 0.1),
        'gla_norm': gain(ks[12], (DEPTH, GLA_V_W)),
        'attn_sinks': nrm(ks[13], (DEPTH, SWA_HEADS), 0.5),
        'swa_norm': gain(ks[14], (DEPTH, SWA_Q_W)),
        'w_out': nrm(ks[15], (DEPTH, MIX_WIDTH, D_MODEL), MIX_WIDTH ** -0.5),
        'norm_ffn2': gain(ks[16], (DEPTH, D_MODEL)),
        'w_ffn2_gu': nrm(ks[17], (DEPTH, D_MODEL, 2 * D_FF), D_MODEL ** -0.5),
        'w_ffn2_down': nrm(ks[18], (DEPTH, D_FF, D_MODEL), D_FF ** -0.5),
        'norm_final': gain(ks[19], (D_MODEL,)),
    }

def reference(x_prompt, x_sample, state_gla, cache_swa_k, cache_swa_v,
              norm_ffn1, w_ffn1_gu, w_ffn1_down, norm_mix, w_in, w_gate_up, b_gate,
              gla_norm, attn_sinks, swa_norm, w_out, norm_ffn2, w_ffn2_gu, w_ffn2_down,
              norm_final):
    def params(l):
        return (norm_ffn1[l], w_ffn1_gu[l], w_ffn1_down[l], norm_mix[l], w_in[l], w_gate_up[l],
                b_gate[l], gla_norm[l], attn_sinks[l], swa_norm[l], w_out[l], norm_ffn2[l],
                w_ffn2_gu[l], w_ffn2_down[l])

    pos_p = jnp.arange(SEQ)
    s0_p = jnp.zeros((BATCH, GLA_HEADS, GLA_DK, GLA_DV), state_gla.dtype)
    xp = x_prompt
    gla_p, k_p, v_p = [], [], []
    for l in range(DEPTH):
        xp, s, kk, vv = layer(xp, pos_p, s0_p, swa_prompt, params(l))
        gla_p.append(s)
        k_p.append(kk)
        v_p.append(vv)

    pos_s = PAST_LEN + jnp.arange(DEC_SEQ)
    xs = x_sample
    gla_s, k_s, v_s = [], [], []
    for l in range(DEPTH):
        swa_fn = functools.partial(swa_sample, k_buf=cache_swa_k[l], v_buf=cache_swa_v[l], pos=pos_s)
        xs, s, kk, vv = layer(xs, pos_s, state_gla[l], swa_fn, params(l))
        gla_s.append(s)
        k_s.append(kk)
        v_s.append(vv)

    y_prompt = rmsnorm(xp, norm_final)
    y_sample = rmsnorm(xs, norm_final)
    return (y_prompt, y_sample, jnp.stack(gla_p), jnp.stack(k_p), jnp.stack(v_p),
            jnp.stack(gla_s), jnp.stack(k_s), jnp.stack(v_s))


_drawn_inputs = setup_inputs


def setup_inputs(seed=0):
    import zlib

    import numpy as np

    out = dict(_drawn_inputs(seed))
    spreads = {}
    factors = {'norm_ffn1': 3.562,
     'gla_norm': 20.95,
     'attn_sinks': 4.601,
     'swa_norm': 12.931,
     'norm_ffn2': 6.334,
     'norm_final': 7.98}
    for name, (base, spread) in spreads.items():
        noise = np.random.default_rng([zlib.crc32(name.encode()), seed]).standard_normal(out[name].shape)
        drawn = base * np.exp(spread * noise) if base else spread * noise
        out[name] = __import__('jax').numpy.asarray(drawn.astype(out[name].dtype))
    for name, factor in factors.items():
        out[name] = (out[name] * factor).astype(out[name].dtype)
    return out
```

```python
from contextlib import ExitStack

import numpy as np

import concourse.bass as bass
from concourse import mybir

F32 = mybir.dt.float32
F32R = mybir.dt.float32r
I32 = mybir.dt.int32
ALU = mybir.AluOpType
ACT = mybir.ActivationFunctionType
AX_X = mybir.AxisListType.X

P = 128
D = 1024
DEPTH = 2
SEQ = 512
NB = 8
NT = 4
SAMP = NB * NT
T = SEQ + SAMP
TH = T // 2
KT = D // P
D_FF = 2816
FT = D_FF // P
WIN = 128
HD = 64
PAST = 2048
EPS = 1e-6
CHUNK = 64
NCHK = SEQ // CHUNK
NBLK = SEQ // WIN
GH = 4
DN_CH = -(-FT // KT)

CH_GU = 2 * FT
CH_FFN = CH_GU + KT * DN_CH
RING = 4
RAW = 2
IN_TILES = ["kS", "vS", "qS0", "qS1", "qS2", "qS3", "a", "kG0", "kG1", "qG0", "qG1",
            "vG0", "vG1", "vG2", "vG3", "rG0", "rG1", "rG2", "rG3"]
CH_IN = len(IN_TILES) + 1
CH_MIX = CH_IN + KT
CH_LAYER = 2 * CH_FFN + CH_MIX
CH_ALL = DEPTH * CH_LAYER + RING
assert CH_LAYER % RING == 0 and CH_IN % RING == 0

JOBS_FFN = 2 * FT + KT

IN_JOBS = ["kS", "vS", "qS0", "qS1", "qS2", "qS3", "a", "kG0", "z0", "z1", "kG1", "qG0", "qG1",
           "vG0", "vG1", "vG2", "vG3", "rG0", "rG1", "rG2", "rG3"]
UNITS = [(b, jj) for b in range(NBLK) for jj in range(2)]


def in_chunk(name):
    c = 0
    for n in IN_TILES:
        if n == name:
            return c
        c += 2 if n == "a" else 1
    raise KeyError(name)


def mixer_steps():
    steps = [("load", 0)]
    n = len(UNITS)
    for i, name in enumerate(IN_JOBS):
        steps.append(("in", i))
        if i == 0:
            steps.append(("norm", 0))
        steps.append(("evac", i))
        if 3 <= i < 8:
            steps.append(("rope", i - 3))
        if i == 3:
            steps.append(("vstr", 0))
        u = i - 7
        if u >= 0:
            steps += [("pv", u - 2)] * (0 <= u - 2 < n)
            steps += [("score", u)] * (0 <= u < n)
            steps += [("ptr", u - 1)] * (0 <= u - 1 < n)
            steps += [("nrm", u)] * (0 <= u < n)
        if i == 7:
            steps.append(("samp_q", 0))
        if name == "qG0":
            steps += [("gatef", 0), ("gate", 0)]
        if name == "qG1":
            steps += [("gatef", 1), ("gate", 1)]
        if name == "vG2":
            steps += [("samp_s", 0), ("nrm", n)]
        if name == "vG3":
            steps += [("samp_t", 0)]
        if name == "rG0":
            steps += [("samp_o", 0), ("load_s0", 0), ("vtr", 0), ("vtr", 1)]
        if name == "rG1":
            steps += [("vtr", 2), ("vtr", 3), ("vtr", 4)]
        if name == "rG2":
            steps += [("kltr", 0), ("kltr", 1)]
    steps += [("ssq", j) for j in range(4)]
    steps += [("snorm", 0), ("kv", 0), ("kv", 1), ("att", 0)]
    for tb in range(NBLK):
        if tb + 1 < NBLK:
            steps.append(("att", tb + 1))
        steps.append(("o", tb))
        if tb + 1 < NBLK:
            steps += [("kv", 2 * tb + 2), ("kv", 2 * tb + 3)]
    steps += [("gs_att", 0), ("gs_o", 0)]
    steps += [("gs_kv", b) for b in range(NB)]
    steps += [("store", 0)]
    steps += [("silu", j) for j in range(4)]
    steps += [("gsq", h) for h in range(GH)]
    steps += [("smix", j) for j in range(4)]
    steps += [("gsum", h) for h in range(GH)]
    steps += [("gmix", h) for h in range(GH)]
    return steps


def trunk(nc, xT, stream, gains, lparams, wa2, cos_t, sin_t, swa_mask, samp_mask, gla_mask,
          glas_mask, bmask, ident_d, s0_d, kc_d, vc_d, y_d, s_p_d, kv_p_d, s_s_d, k_s_d, v_s_d):
    U = T * 4
    base = -(-nc.sbuf_base // 64) * 64
    plan = {"at": base}

    def sb(name, shape, dt=F32, at=None):
        size = int(np.prod(shape[1:])) * 4
        if at is None:
            at = plan["at"]
            plan["at"] += -(-size // 64) * 64
        return nc.alloc_sbuf_tensor_at(name, list(shape), dt, offset=at)

    ctx = ExitStack()
    with ctx:
        x = sb("x", [P, KT, T])
        h_hi = sb("h_hi", [P, KT, T], F32R)
        h_lo = sb("h_lo", [P, KT, T], F32R)
        arena = plan["at"]
        act_hi = sb("act_hi", [P, FT, T], F32R)
        act_lo = sb("act_lo", [P, FT, T], F32R)
        w_raw = sb("w_raw", [P, RAW, KT * P])
        w_hi = sb("w_hi", [P, RING, KT * P], F32R)
        w_lo = sb("w_lo", [P, RING, KT * P], F32R)
        rs = sb("rs", [P, T])
        g_buf = sb("g_buf", [P, 2, T])
        a_buf = sb("a_buf", [P, 2, T])
        sq_buf = sb("sq_buf", [P, 2, T])
        ssum = sb("ssum", [P, T])
        s_ring = sb("s_ring", [P, 4, 2, P])
        ones = sb("ones", [P, P])
        ident = sb("ident", [P, P])
        lp = sb("lp", [P, 44])
        st = sb("st", [P, 2, 24])
        nsk = sb("nsk", [P, 10])
        eps = sb("eps", [P, 1])
        g_first = sb("g_first", [P, KT])
        ebl = sb("ebl", [P, 2, 16])
        bm = sb("bm", [P, NB])
        assert plan["at"] <= nc.sbuf_usable_end, plan["at"]
        LG, BG, GG, SG, SK, SKS = 0, 24, 26, 30, 34, 42

        def mx(name, shape, off, dt=F32):
            assert off + int(np.prod(shape[1:])) * 4 <= 2 * FT * U, name
            return sb(name, shape, dt, at=arena + off)

        mix_hi = mx("mix_hi", [P, KT, T], 0, F32R)
        mix_lo = mx("mix_lo", [P, KT, T], 8 * U, F32R)
        kG = mx("kG", [P, 2, T], 0)
        qG = mx("qG", [P, 2, T], 2 * U)
        aT = mx("aT", [P, T], 4 * U)
        kS = mx("kS", [P, T], 5 * U)
        vS = mx("vS", [P, T], 6 * U)
        cos_s = mx("cos_s", [P, T], 7 * U)
        sin_s = mx("sin_s", [P, T], 8 * U)
        shuf = mx("shuf", [P, T], 9 * U)
        klT = mx("klT", [P, 5, 2 * P], 7 * U)
        t1 = mx("t1", [P, T], 10 * U)
        t2 = mx("t2", [P, T], 11 * U)
        t3 = mx("t3", [P, T], 12 * U)
        kc = mx("kc", [P, NB, WIN], 13 * U)
        qz = mx("qz", [P, NB * (P + 16)], 15 * U)
        qc = mx("qc", [P, P], 15 * U + 4608)
        wa = mx("wa", [P, 2 * P], 15 * U + 5120)
        s0 = mx("s0", [P, NB, 2, P], 13 * U)
        qS = mx("qS", [P, 4, T], 18 * U)
        vG = mx("vG", [P, 4, T], 22 * U)
        oG = mx("oG", [P, 4, T], 22 * U)
        rG = mx("rG", [P, 4, T], 26 * U)
        off = 30 * U
        v_tok = mx("v_tok", [P, 5, 4 * P], off)
        off += 10240
        vs_tok = mx("vs_tok", [P, 5, P], off)
        off += 2560
        vc = mx("vc", [P, NB, P], off)
        attm = mx("attm", [P, 2, 2, 2, P], off)
        off += 4096
        m_swa = mx("m_swa", [P, 2 * WIN], off)
        off += 1024
        m_gla = mx("m_gla", [P, P], off, I32)
        off += 512
        m_samp = mx("m_samp", [P, WIN + SAMP], off)
        off += 640
        m_glas = mx("m_glas", [P, SAMP], off, I32)
        off += 128
        klm = mx("klm", [P, 2, 2 * P], off)
        off += 2048
        atts = mx("atts", [P, 2, 2, SAMP], off)
        off += 512

        ps = ctx.enter_context(nc.psum_tensor("ps", [P, 8, 512], F32))

        def pair(i):
            return ps[:, 2 * i:2 * i + 2, 0:TH]

        def halves(ap):
            return ap.rearrange("p (h n) -> p h n", h=2)

        def s_tile(u):
            return (g_buf, sq_buf)[u % 2][:, :, :].rearrange("p a n -> p (a n)")[:, 0:1024]

        def unit_rows(u):
            if u == len(UNITS):
                return [(g, slice(g * 512, g * 512 + WIN + SAMP)) for g in range(2)]
            return [(a, slice(a * 256 + (0 if UNITS[u][0] else WIN), (a + 1) * 256)) for a in range(4)]

        p_t = a_buf[:, :, :].rearrange("p a n -> p (a n)")

        def sq_tile(j):
            return (g_buf, sq_buf)[j // 2][:, j % 2, :]

        def sem(name):
            return ctx.enter_context(nc.semaphore(name))

        raw_loaded = [sem(f"raw_loaded{i}") for i in range(RAW)]
        hi_ready = sem("hi_ready")
        lo_ready = sem("lo_ready")
        chunk_done = sem("chunk_done")
        gate_scaled = sem("gate_scaled")
        silu_done = sem("silu_done")
        up_used = sem("up_used")
        act_ready = sem("act_ready")
        down_used = sem("down_used")
        x_ready = sem("x_ready")
        sq_ready = sem("sq_ready")
        h_ready = sem("h_ready")
        h_step = sem("h_step")
        ssum_ready = sem("ssum_ready")
        norm_summed = sem("norm_summed")
        norm_root = sem("norm_root")
        rs_ready = sem("rs_ready")
        lp_loaded = sem("lp_loaded")
        start_loaded = sem("start_loaded")
        ones_set = sem("ones_set")
        eps_set = sem("eps_set")
        y_ready = sem("y_ready")
        y_stored = sem("y_stored")
        caches_moved = sem("caches_moved")
        mixer_left = sem("mixer_left")
        m_names = ["loaded", "s0_loaded", "stored", "in_done", "in_used", "v_step", "a_step",
                   "roped", "vst_done", "vst_out", "score_done", "masked", "statted", "exped",
                   "normed", "ptr_done", "pt_out", "pv_done", "attn_out", "z_logged", "z_summed",
                   "z_exped", "kl_diff", "kl_exped", "kl_made", "kltr_done", "kl_out", "vtr_done",
                   "v_out", "ss_done", "q_set", "st_done", "st_out", "so_done", "so_out",
                   "att_done", "att_out", "kv_done", "state_made", "o_done", "o_out", "ga_done",
                   "ga_out", "go_done", "go_out", "klm_made", "gkv_done", "gkv_used", "r_silu",
                   "gsq", "gsum_done", "g_root", "ssq", "ssum_done", "s_root", "mix_ready", "kb_made"]
        m = {n: sem("m_" + n) for n in m_names}
        first, last = m[m_names[0]].num, m[m_names[-1]].num
        m_range = range(min(first, last), max(first, last) + 1)
        assert len(m_range) == len(m_names)

        STEPS = mixer_steps()
        B_STEPS = 2 * KT - 2
        N_LOADS = 9

        block = ctx.enter_context(nc.Block())

        @block.sync
        def _(sp):
            sp.dma_start(x[:, :, :], xT).then_inc(start_loaded, 16)
            sp.dma_start(ident[:, :], ident_d).then_inc(start_loaded, 16)
            sp.dma_start(bm[:, :], bmask).then_inc(start_loaded, 16)
            with sp.Fori(0, CH_ALL // RING) as i:
                for q in range(RING):
                    sp.wait_ge(lo_ready, i * RING + (q + 1 - RAW + RING))
                    sp.dma_start(w_raw[:, q % RAW, :], stream[i * RING + q]).then_inc(raw_loaded[q % RAW], 16)
            sp.wait_ge(y_ready, KT)
            sp.dma_start(y_d, x[:, :, :]).then_inc(y_stored, 16)
            sp.wait_ge(y_stored, 16)
            sp.wait_ge(caches_moved, DEPTH * 32)

        @block.gpsimd
        def _(pool):
            pool.memset(ones[:, :], 1.0).then_inc(ones_set, 1)
            pool.sem_inc(lo_ready, RING)
            for l in range(DEPTH):
                pool.dma_start(k_s_d[l, :, :, 0:WIN - NT], kc_d[l, :, :, NT:WIN]).then_inc(caches_moved, 16)
                pool.dma_start(v_s_d[l, 0:WIN - NT, :, :], vc_d[l, NT:WIN, :, :]).then_inc(caches_moved, 16)
            with pool.Fori(0, CH_ALL // RING) as i:
                for q in range(RING):
                    pool.wait_ge(hi_ready, i * RING + (q + 1))
                    pool.tensor_tensor(w_lo[:, q, :], w_raw[:, q % RAW, :], w_hi[:, q, :].bitcast(F32),
                                       ALU.subtract).then_inc(lo_ready, 1)

        @block.tensor
        def _(pe):
            pe.sem_inc(chunk_done, RING)

            def product(dst, slot, col, rhs_hi, rhs_lo, first, last):
                cols = slice(col, col + P)
                for w, r in ((w_hi, rhs_hi), (w_lo, rhs_hi), (w_hi, rhs_lo)):
                    for hf in range(2):
                        ins = pe.matmul(dst[:, hf, :], w[:, slot, cols], r[:, hf * TH:(hf + 1) * TH],
                                        start=first and w is w_hi and r is rhs_hi,
                                        stop=last and r is rhs_lo)
                return ins

            def model_tile(dst, chunk, slot, hb=None):
                pe.wait_ge(lo_ready, chunk + (1 + RING))
                for k in range(KT):
                    if hb is not None and k >= 5:
                        pe.wait_ge(h_ready, hb + (k + 1))
                    ins = product(dst, slot, k * P, h_hi[:, k, :], h_lo[:, k, :], k == 0, k == KT - 1)
                return ins

            def norm_sum(phase):
                pe.wait_ge(ssum_ready, phase + 1)
                for hf in range(2):
                    ins = pe.matmul(pair(3)[:, hf, :], ones[:, :], ssum[:, hf * TH:(hf + 1) * TH],
                                    start=True, stop=True)
                ins.then_inc(norm_summed, 1)

            def ffn_half(l, half):
                ch = l * CH_LAYER + half * (CH_FFN + CH_MIX)
                fb = l * (2 * FT) + half * FT
                hb = l * (3 * KT) + half * 2 * KT
                pe.wait_ge(h_ready, hb + 5)
                for q in range(4):
                    if q == 3:
                        pe.wait_ge(norm_root, l * 3 + (half * 2 + 1))
                    model_tile(pair(q), ch + q, q, hb if q == 0 else None).then_inc(chunk_done, 1)
                    if q == 0:
                        norm_sum(l * 3 + half * 2)
                with pe.Fori(1, FT // 2) as i:
                    for q in range(4):
                        pe.wait_ge(up_used if q % 2 else gate_scaled, i * 2 + (fb + (q // 2 - 1)))
                        model_tile(pair(q), i * 4 + (ch + q), q).then_inc(chunk_done, 1)
                with pe.Fori(0, KT // 4) as i:
                    for q in range(4):
                        pe.wait_ge(up_used if q % 2 else gate_scaled, fb + (FT - 1 + q // 2))
                        pe.wait_ge(down_used, i * 4 + (l * (2 * KT) + (half * KT + q + 1)))
                        for c in range(DN_CH):
                            s = (q * DN_CH + c) % RING
                            pe.wait_ge(lo_ready, i * (4 * DN_CH) + (ch + (CH_GU + q * DN_CH + c + 1 + RING)))
                            for k in range(c * KT, min(FT, (c + 1) * KT)):
                                if q == 0 and k >= FT - 4:
                                    pe.wait_ge(act_ready, fb + (k + 1))
                                ins = product(pair(q), s, (k - c * KT) * P, act_hi[:, k, :],
                                              act_lo[:, k, :], k == 0, k == FT - 1)
                            ins.then_inc(chunk_done, 1)

            def mixer(l):
                ch = l * CH_LAYER + CH_FFN
                hb = l * (3 * KT) + KT
                for step, i in STEPS:
                    if step == "in":
                        name = IN_JOBS[i]
                        if i == 0:
                            pe.wait_ge(h_ready, hb + 6)
                        if i >= 2:
                            pe.wait_ge(m["in_used"], i - 1)
                        dst = pair(i % 2)
                        if name[0] == "z":
                            pr = int(name[1])
                            pe.wait_ge(m["loaded"], 16 * N_LOADS)
                            pe.wait_ge(m["in_used"], IN_JOBS.index("a") + 1)
                            for hf in range(2):
                                ins = pe.matmul(dst[:, hf, :], wa[0:16, pr * P:(pr + 1) * P],
                                                aT[0:16, hf * TH:(hf + 1) * TH], start=True, stop=True)
                            ins.then_inc(m["in_done"], 1)
                            continue
                        c = in_chunk(name)
                        if name == "a":
                            for part in range(2):
                                pe.wait_ge(lo_ready, ch + (c + part + 1 + RING))
                                for k in range(4 * part, 4 * part + 4):
                                    ins = product(dst, (c + part) % RING, (k % 4) * P, h_hi[:, k, :],
                                                  h_lo[:, k, :], k == 0, k == KT - 1)
                                if part == 0:
                                    ins.then_inc(chunk_done, 1)
                        else:
                            ins = model_tile(dst, ch + c, c % RING, hb if i == 0 else None)
                        ins.then_inc(chunk_done, 1)
                    elif step == "norm":
                        norm_sum(l * 3 + 1)
                    elif step == "vstr":
                        pe.wait_ge(m["in_used"], 2)
                        pe.wait_ge(norm_root, l * 3 + 2)
                        for tb in range(5):
                            n = P if tb < 4 else SAMP
                            dst = ps[0:n, 6, tb * P:(tb + 1) * P] if tb < 4 else ps[0:n, 7, 0:P]
                            ins = pe.transpose(dst, vS[:, tb * P:tb * P + n], ident[:, :])
                        ins.then_inc(m["vst_done"], 1)
                    elif step == "score":
                        b, jj = UNITS[i]
                        pe.wait_ge(m["roped"], 2 * jj + 3)
                        if i >= 1:
                            pe.wait_ge(m["masked"], i)
                        k0 = max(b - 1, 0) * WIN
                        o = 0 if b else WIN
                        for g in range(2):
                            rows = slice(g * HD, (g + 1) * HD)
                            for uu in range(2):
                                ins = pe.matmul(ps[:, 4 + g, uu * 256 + o:(uu + 1) * 256],
                                                qS[rows, 2 * jj + uu, b * WIN:(b + 1) * WIN],
                                                kS[rows, k0:(b + 1) * WIN], start=True, stop=True)
                        ins.then_inc(m["score_done"], 1)
                    elif step == "ptr":
                        b, jj = UNITS[i]
                        pe.wait_ge(m["normed"], i + 1)
                        if i >= 1:
                            pe.wait_ge(m["attn_out"], i)
                        else:
                            pe.wait_ge(m["vst_out"], 2)
                        for a in range(4):
                            for kb in range(0 if b else 1, 2):
                                o = (a % 2) * 256 + kb * WIN
                                ins = pe.transpose(ps[:, 6 + a // 2, o:o + WIN],
                                                   s_tile(i)[:, a * 256 + kb * WIN:a * 256 + (kb + 1) * WIN],
                                                   ident[:, :])
                        ins.then_inc(m["ptr_done"], 1)
                    elif step == "pv":
                        b, jj = UNITS[i]
                        pe.wait_ge(m["pt_out"], i + 1)
                        for a in range(4):
                            g, uu = divmod(a, 2)
                            for kb in range(0 if b else 1, 2):
                                o = a * 256 + kb * WIN
                                ins = pe.matmul(ps[g * HD:(g + 1) * HD, 6, uu * WIN:(uu + 1) * WIN],
                                                vs_tok[:, b - 1 + kb, g * HD:(g + 1) * HD], p_t[:, o:o + WIN],
                                                start=kb == (0 if b else 1), stop=kb == 1)
                        ins.then_inc(m["pv_done"], 1)
                    elif step == "samp_s":
                        pe.wait_ge(m["loaded"], 16 * N_LOADS)
                        pe.wait_ge(m["masked"], len(UNITS))
                        pe.wait_ge(m["q_set"], 1)
                        for g in range(2):
                            rows = slice(g * HD, (g + 1) * HD)
                            for b in range(NB):
                                pe.matmul(ps[:, 4 + g, 0:WIN], qz[rows, b * P:(b + 1) * P], kc[rows, b, :],
                                          start=b == 0, stop=b == NB - 1)
                            ins = pe.matmul(ps[:, 4 + g, WIN:WIN + SAMP], qc[rows, :],
                                            kS[rows, SEQ:T], start=True, stop=True)
                        ins.then_inc(m["ss_done"], 1)
                    elif step == "samp_t":
                        pe.wait_ge(m["normed"], len(UNITS) + 1)
                        pe.wait_ge(m["attn_out"], len(UNITS))
                        src = s_tile(0)
                        for g in range(2):
                            pe.transpose(ps[:, 6, g * P:(g + 1) * P], src[:, g * 512:g * 512 + WIN],
                                         ident[:, :])
                            ins = pe.transpose(ps[0:SAMP, 6, (2 + g) * P:(3 + g) * P],
                                               src[:, g * 512 + WIN:g * 512 + WIN + SAMP], ident[:, :])
                        ins.then_inc(m["st_done"], 1)
                    elif step == "samp_o":
                        pe.wait_ge(m["st_out"], 2)
                        for g in range(2):
                            rows = slice(g * HD, (g + 1) * HD)
                            pe.matmul(ps[rows, 7, 0:P], vs_tok[0:SAMP, 4, rows],
                                      p_t[0:SAMP, (2 + g) * P:(3 + g) * P], start=True, stop=False)
                            for b in range(NB):
                                ins = pe.matmul(ps[rows, 7, b * 16:(b + 1) * 16], vc[:, b, rows],
                                                p_t[:, g * P + b * 16:g * P + b * 16 + 16],
                                                start=False, stop=b == NB - 1)
                        ins.then_inc(m["so_done"], 1)
                    elif step == "kltr":
                        pe.wait_ge(m["kl_made"], 2)
                        pe.wait_ge(m["masked"], len(UNITS) + 1)
                        if i:
                            pe.wait_ge(m["kl_out"], 2)
                        for tb in range(5):
                            n = P if tb < 4 else SAMP
                            dst = ps[0:n, 4, tb * P:(tb + 1) * P] if tb < 4 else ps[0:n, 5, 0:P]
                            ins = pe.transpose(dst, (aT, t1)[i][:, tb * P:tb * P + n], ident[:, :])
                        ins.then_inc(m["kltr_done"], 1)
                    elif step == "vtr":
                        n = P if i < 4 else SAMP
                        pe.wait_ge(m["in_used"], IN_JOBS.index("vG3") + 1)
                        pe.wait_ge(m["so_out"], 1)
                        if i >= 2:
                            pe.wait_ge(m["v_out"], i - 1)
                        for h in range(GH):
                            ins = pe.transpose(ps[0:n, 6 + i % 2, h * P:(h + 1) * P],
                                               vG[:, h, i * P:i * P + n], ident[:, :])
                        ins.then_inc(m["vtr_done"], 1)
                    elif step == "kv":
                        pe.wait_ge(m["kl_out"], 4)
                        pe.wait_ge(m["v_out"], 5)
                        if i >= 2:
                            pe.wait_ge(m["state_made"], i - 1)
                        else:
                            pe.wait_ge(m["in_used"], len(IN_JOBS))
                        rows = slice((i % 2) * CHUNK, (i % 2 + 1) * CHUNK)
                        for h in range(GH):
                            pr, hh = divmod(h, 2)
                            ins = pe.matmul(ps[hh * HD:(hh + 1) * HD, 2 + i % 2, pr * P:(pr + 1) * P],
                                            klT[rows, i // 2, h * HD:(h + 1) * HD],
                                            v_tok[rows, i // 2, h * P:(h + 1) * P], start=True, stop=True)
                        ins.then_inc(m["kv_done"], 1)
                    elif step == "att":
                        pe.wait_ge(m["kb_made"], 2)
                        if i >= 1:
                            pe.wait_ge(m["att_out"], i)
                        else:
                            pe.wait_ge(m["kl_out"], 4)
                        for h in range(GH):
                            pr, hh = divmod(h, 2)
                            rows = slice(hh * HD, (hh + 1) * HD)
                            ins = pe.matmul(ps[:, 4 + hh, pr * P:(pr + 1) * P], kG[rows, pr, i * P:(i + 1) * P],
                                            qG[rows, pr, i * P:(i + 1) * P], start=True, stop=True)
                        ins.then_inc(m["att_done"], 1)
                    elif step == "o":
                        pe.wait_ge(m["att_out"], i + 1)
                        pe.wait_ge(m["state_made"], 2 * i + 1)
                        if i >= 2:
                            pe.wait_ge(m["o_out"], i - 1)
                        else:
                            pe.wait_ge(m["v_out"], 5)
                            pe.wait_ge(m["s_root"], 1)
                        for h in range(GH):
                            pr, hh = divmod(h, 2)
                            at, bank = pr * P, (6, 0)[i % 2] + hh
                            pe.matmul(ps[:, bank, at:at + P], v_tok[:, i, h * P:(h + 1) * P],
                                      attm[:, i % 2, hh, pr, :], start=True, stop=False)
                            for c in (2 * i, 2 * i + 1):
                                if c == 0:
                                    continue
                                o = at + (c % 2) * CHUNK
                                ins = pe.matmul(ps[:, bank, o:o + CHUNK],
                                                s_ring[hh * HD:(hh + 1) * HD, c % 4, pr, :],
                                                qG[hh * HD:(hh + 1) * HD, pr, c * CHUNK:(c + 1) * CHUNK],
                                                start=False, stop=c == 2 * i + 1)
                        ins.then_inc(m["o_done"], 1)
                    elif step == "gs_att":
                        pe.wait_ge(m["att_out"], NBLK)
                        for h in range(GH):
                            pr, hh = divmod(h, 2)
                            rows = slice(hh * HD, (hh + 1) * HD)
                            ins = pe.matmul(ps[0:SAMP, 4 + hh, pr * SAMP:(pr + 1) * SAMP], kG[rows, pr, SEQ:T],
                                            qG[rows, pr, SEQ:T], start=True, stop=True)
                        ins.then_inc(m["ga_done"], 1)
                    elif step == "gs_o":
                        pe.wait_ge(m["ga_out"], 1)
                        pe.wait_ge(m["s0_loaded"], 16)
                        pe.wait_ge(m["o_out"], NBLK - 1)
                        for h in range(GH):
                            pr, hh = divmod(h, 2)
                            rows = slice(hh * HD, (hh + 1) * HD)
                            pe.matmul(ps[:, 6 + hh, pr * SAMP:(pr + 1) * SAMP],
                                      v_tok[0:SAMP, 4, h * P:(h + 1) * P], atts[0:SAMP, hh, pr, :],
                                      start=True, stop=False)
                            for b in range(NB):
                                o = pr * SAMP + b * NT
                                ins = pe.matmul(ps[:, 6 + hh, o:o + NT], s0[rows, b, pr, :],
                                                qG[rows, pr, SEQ + b * NT:SEQ + (b + 1) * NT],
                                                start=False, stop=b == NB - 1)
                        ins.then_inc(m["go_done"], 1)
                    elif step == "gs_kv":
                        pe.wait_ge(m["klm_made"], i + 1)
                        if i >= 2:
                            pe.wait_ge(m["gkv_used"], i - 1)
                        else:
                            pe.wait_ge(m["state_made"], NCHK)
                        for h in range(GH):
                            pr, hh = divmod(h, 2)
                            ins = pe.matmul(ps[hh * HD:(hh + 1) * HD, 2 + i % 2, pr * P:(pr + 1) * P],
                                            klm[0:SAMP, i % 2, h * HD:(h + 1) * HD],
                                            v_tok[0:SAMP, 4, h * P:(h + 1) * P], start=True, stop=True)
                        ins.then_inc(m["gkv_done"], 1)
                    elif step == "snorm":
                        pe.wait_ge(m["in_used"], len(IN_JOBS))
                        for j in range(4):
                            pe.wait_ge(m["ssq"], j + 1)
                            for hf in range(2):
                                ins = pe.matmul(pair(0)[:, hf, :], ones[:, :],
                                                sq_tile(j)[:, hf * TH:(hf + 1) * TH],
                                                start=j == 0, stop=j == 3)
                        ins.then_inc(m["ssum_done"], 1)
                    elif step == "gsum":
                        pe.wait_ge(m["gsq"], i + 1)
                        if i == 0:
                            pe.wait_ge(m["s_root"], 1)
                            pe.wait_ge(m["go_out"], 1)
                            pe.wait_ge(m["gkv_used"], NB)
                            pe.wait_ge(m["o_out"], NBLK)
                        for hf in range(2):
                            ins = pe.matmul(pair(i)[:, hf, :], ones[:, :],
                                            sq_tile(i)[:, hf * TH:(hf + 1) * TH], start=True, stop=True)
                        ins.then_inc(m["gsum_done"], 1)
                pe.wait_ge(m["g_root"], GH)
                for n in range(KT):
                    c = CH_IN + n
                    pe.wait_ge(lo_ready, ch + (c + 1 + RING))
                    if n >= 4:
                        pe.wait_ge(x_ready, l * (3 * KT) + (KT + n - 3))
                    for k in range(KT):
                        if n == 0:
                            pe.wait_ge(m["mix_ready"], k + 1)
                        ins = product(pair(n % 4), c % RING, k * P, mix_hi[:, k, :], mix_lo[:, k, :],
                                      k == 0, k == KT - 1)
                    ins.then_inc(chunk_done, 1)

            pe.wait_ge(ones_set, 1)
            pe.wait_ge(start_loaded, 48)
            with pe.Fori(0, DEPTH) as l:
                ffn_half(l, 0)
                mixer(l)
                ffn_half(l, 1)
            pe.wait_ge(h_ready, DEPTH * 3 * KT + KT)
            norm_sum(DEPTH * 3)

        @block.scalar
        def _(act):
            def high_part(g, q):
                act.wait_ge(raw_loaded[q % RAW], g[1])
                act.wait_ge(chunk_done, g[0] + 1)
                act.activation(w_hi[:, q % RING, :], w_raw[:, q % RAW, :], ACT.Copy).then_inc(hi_ready, 1)

            def chunk(l, c, i=None, per=0):
                n, r = l * CH_LAYER + c, l * (CH_LAYER // RAW * 16) + (c // RAW + 1) * 16
                if i is not None:
                    n, r = n + i * per, r + i * (per // RAW * 16)
                return n, r

            def square(l, p, n):
                act.wait_ge(x_ready, l * (3 * KT) + (p * KT + n + 1))
                dst = ssum[:, :] if n == 0 else sq_buf[:, n % 2, :]
                act.activation(dst, x[:, n, :], ACT.Square).then_inc(sq_ready, 1)

            def root(phase):
                act.wait_ge(norm_summed, phase + 1)
                act.activation(halves(rs[:, :]), pair(3), ACT.Sqrt, bias=eps[:, :],
                               scale=1.0 / D).then_inc(norm_root, 1)

            def ffn_half(l, half):
                c0 = half * (CH_FFN + CH_MIX)
                fb = l * (2 * FT) + half * FT
                high_part(chunk(l, c0 + RING), 0)
                root(l * 3 + half * 2)
                for q in range(1, 4):
                    high_part(chunk(l, c0 + RING + q), q)
                    if q % 2:
                        silu(fb + q // 2, q // 2)
                with act.Fori(1, FT // 2) as i:
                    for q in range(4):
                        high_part(chunk(l, c0 + RING + q, i, 4), q)
                        if q % 2:
                            silu(i * 2 + (fb + q // 2), q // 2)
                for n in range(KT):
                    for c in range(DN_CH):
                        high_part(chunk(l, c0 + CH_GU + n * DN_CH + c + RING), n * DN_CH + c)
                    square(l, half * 2, n)

            def silu(f, q):
                act.wait_ge(gate_scaled, f + 1)
                act.activation(g_buf[:, q, :], g_buf[:, q, :], ACT.Silu).then_inc(silu_done, 1)

            def mixer(l):
                c0 = CH_FFN
                steps = [0]

                def link(ins):
                    steps[0] += 1
                    ins.then_inc(m["a_step"], 1)
                    act.wait_ge(m["a_step"], steps[0])

                for step, i in STEPS:
                    if step == "load":
                        act.wait_ge(chunk_done, l * CH_LAYER + (CH_FFN + RING))
                        act.dma_start(cos_s[:, :], cos_t).then_inc(m["loaded"], 16)
                        act.dma_start(sin_s[:, :], sin_t).then_inc(m["loaded"], 16)
                        act.dma_start(m_swa[:, :], swa_mask).then_inc(m["loaded"], 16)
                        act.dma_start(m_samp[:, :], samp_mask).then_inc(m["loaded"], 16)
                        act.dma_start(m_gla[:, :], gla_mask).then_inc(m["loaded"], 16)
                        act.dma_start(m_glas[:, :], glas_mask).then_inc(m["loaded"], 16)
                        act.dma_start(wa[0:16, :], wa2[l]).then_inc(m["loaded"], 16)
                        act.dma_start(kc[:, :, :], kc_d[l]).then_inc(m["loaded"], 16)
                        act.dma_start(vc[:, :, :], vc_d[l]).then_inc(m["loaded"], 16)
                    elif step == "in":
                        name = IN_JOBS[i]
                        if name[0] != "z":
                            for part in range(2 if name == "a" else 1):
                                c = in_chunk(name) + part
                                high_part(chunk(l, c0 + c + RING), c)
                    elif step == "norm":
                        root(l * 3 + 1)
                    elif step == "vstr":
                        act.wait_ge(m["vst_done"], 1)
                        act.activation(vs_tok[:, 0:4, :], ps[:, 6, :].rearrange("p (b n) -> p b n", b=4),
                                       ACT.Copy).then_inc(m["vst_out"], 1)
                        act.activation(vs_tok[0:SAMP, 4, :], ps[0:SAMP, 7, 0:P],
                                       ACT.Copy).then_inc(m["vst_out"], 1)
                    elif step in ("score", "samp_s"):
                        u = i if step == "score" else len(UNITS)
                        act.wait_ge(m["statted"], u + 1)
                        for a, cols in unit_rows(u):
                            ap = s_tile(u)[:, cols]
                            act.activation(ap, ap, ACT.Exp, bias=st[:, u % 2, 4 + a:5 + a],
                                           accum_out=st[:, u % 2, 16 + a:17 + a])
                        n = len(unit_rows(u))
                        act.activation(st[:, u % 2, 12:12 + n], st[:, u % 2, 8:8 + n],
                                       ACT.Exp).then_inc(m["exped"], 1)
                    elif step == "ptr":
                        act.wait_ge(m["ptr_done"], i + 1)
                        if i >= 1:
                            act.wait_ge(m["pv_done"], i)
                        o = 0 if UNITS[i][0] else WIN
                        act.activation(p_t[:, 0:1024].rearrange("p (a n) -> p a n", a=4)[:, :, o:256],
                                       ps[:, 6:8, :].rearrange("p b n -> p (b n)")
                                       .rearrange("p (a n) -> p a n", a=4)[:, :, o:256],
                                       ACT.Copy).then_inc(m["pt_out"], 1)
                    elif step == "samp_t":
                        act.wait_ge(m["st_done"], 1)
                        act.wait_ge(m["pv_done"], len(UNITS))
                        act.activation(p_t[:, 0:256], ps[:, 6, 0:256], ACT.Copy).then_inc(m["st_out"], 1)
                        act.activation(p_t[0:SAMP, 256:512], ps[0:SAMP, 6, 256:512],
                                       ACT.Copy).then_inc(m["st_out"], 1)
                    elif step == "gatef":
                        z = (t1, shuf)[i]
                        act.wait_ge(m["in_used"], IN_JOBS.index(f"z{i}") + 1)
                        if i:
                            act.wait_ge(m["kb_made"], 1)
                        link(act.activation(t2[:, :], z[:, :], ACT.Abs))
                        link(act.activation(t2[:, :], t2[:, :], ACT.Exp, scale=-1.0))
                        act.activation(t2[:, :], t2[:, :], ACT.Ln, bias=1.0).then_inc(m["z_logged"], 1)
                    elif step == "gate":
                        z = (t1, shuf)[i]
                        act.wait_ge(m["z_summed"], i + 1)
                        act.activation(z[:, :], t3[:, :], ACT.Exp, scale=1.0 / 16)
                        act.activation(t2[:, :], t3[:, :], ACT.Exp, scale=-1.0 / 16).then_inc(m["z_exped"], 1)
                        act.wait_ge(m["kl_diff"], i + 1)
                        act.activation(z[:, :], z[:, :], ACT.Exp, scale=1.0 / 16).then_inc(m["kl_exped"], 1)
                    elif step == "vtr":
                        n = P if i < 4 else SAMP
                        act.wait_ge(m["vtr_done"], i + 1)
                        act.activation(v_tok[0:n, i, :], ps[0:n, 6 + i % 2, :], ACT.Copy).then_inc(m["v_out"], 1)
                    elif step == "kltr":
                        act.wait_ge(m["kltr_done"], i + 1)
                        act.activation(klT[:, 0:4, i * P:(i + 1) * P],
                                       ps[:, 4, :].rearrange("p (b n) -> p b n", b=4),
                                       ACT.Copy).then_inc(m["kl_out"], 1)
                        act.activation(klT[0:SAMP, 4, i * P:(i + 1) * P], ps[0:SAMP, 5, 0:P],
                                       ACT.Copy).then_inc(m["kl_out"], 1)
                    elif step == "load_s0":
                        act.wait_ge(m["ss_done"], 1)
                        act.dma_start(s0[:, :, :, :], s0_d[l]).then_inc(m["s0_loaded"], 16)
                    elif step == "silu":
                        act.wait_ge(m["in_used"], len(IN_JOBS))
                        act.activation(rG[:, i, :], rG[:, i, :], ACT.Silu).then_inc(m["r_silu"], 1)
                    elif step == "ssq":
                        act.wait_ge(m["so_out"], 1)
                        act.activation(sq_tile(i), qS[:, i, :], ACT.Square).then_inc(m["ssq"], 1)
                    elif step == "snorm":
                        act.wait_ge(m["in_used"], len(IN_JOBS))
                        act.wait_ge(m["ssum_done"], 1)
                        act.activation(halves(rs[:, :]), pair(0), ACT.Sqrt, bias=eps[:, :],
                                       scale=1.0 / (4 * P)).then_inc(m["s_root"], 1)
                    elif step == "o":
                        act.wait_ge(m["o_done"], i + 1)
                        for hh in range(2):
                            ins = act.activation(
                                oG[:, hh:4:2, i * P:(i + 1) * P],
                                ps[:, (6, 0)[i % 2] + hh, 0:256].rearrange("p (h n) -> p h n", h=2),
                                ACT.Copy)
                        ins.then_inc(m["o_out"], 1)
                    elif step == "gs_o":
                        act.wait_ge(m["go_done"], 1)
                        for hh in range(2):
                            ins = act.activation(oG[:, hh:4:2, SEQ:T],
                                                 ps[:, 6 + hh, 0:64].rearrange("p (h n) -> p h n", h=2),
                                                 ACT.Copy)
                        ins.then_inc(m["go_out"], 1)
                    elif step == "store":
                        act.wait_ge(m["roped"], 1)
                        act.dma_start(kv_p_d[l, 0], kS[:, SEQ - WIN:T]).then_inc(m["stored"], 16)
                        act.dma_start(kv_p_d[l, 1], vS[:, SEQ - WIN:T]).then_inc(m["stored"], 16)
                        act.wait_ge(m["state_made"], NCHK)
                        act.dma_start(s_p_d[l], s_ring[:, NCHK % 4, :, :]).then_inc(m["stored"], 16)
                        act.wait_ge(m["gkv_used"], NB)
                        act.dma_start(s_s_d[l], s0[:, :, :, :]).then_inc(m["stored"], 16)
                    elif step == "gsq":
                        act.wait_ge(m["o_out"], NBLK)
                        act.wait_ge(m["go_out"], 1)
                        act.wait_ge(m["ssum_done"], 1)
                        act.activation(sq_tile(i), oG[:, i, :], ACT.Square).then_inc(m["gsq"], 1)
                    elif step == "gsum":
                        act.wait_ge(m["gsum_done"], i + 1)
                        act.activation(halves(sq_tile(i)), pair(i), ACT.Sqrt, bias=eps[:, :],
                                       scale=1.0 / P).then_inc(m["g_root"], 1)
                for n in range(KT):
                    high_part(chunk(l, c0 + CH_IN + n + RING), n)
                    if n == KT - 1:
                        act.sem_inc(mixer_left, 1)
                    square(l, 1, n)

            for q in range(RING):
                act.wait_ge(raw_loaded[q % RAW], (q // RAW + 1) * 16)
                act.wait_ge(chunk_done, q + 1)
                act.activation(w_hi[:, q, :], w_raw[:, q % RAW, :], ACT.Copy).then_inc(hi_ready, 1)
            act.dma_start(g_first[:, :], gains).then_inc(lp_loaded, 16)
            act.wait_ge(start_loaded, 48)
            act.wait_ge(eps_set, 1)
            for n in range(KT):
                dst = ssum[:, :] if n == 0 else sq_buf[:, n % 2, :]
                if n >= 3:
                    act.wait_ge(h_step, 2 * n - 2)
                act.activation(dst, x[:, n, :], ACT.Square).then_inc(sq_ready, 1)
            with act.Fori(0, DEPTH) as l:
                act.wait_ge(h_ready, l * (3 * KT) + KT)
                act.dma_start(lp[:, :], lparams[l]).then_inc(lp_loaded, 16)
                ffn_half(l, 0)
                mixer(l)
                ffn_half(l, 1)
            root(DEPTH * 3)

        @block.vector
        def _(dve):
            def rope_swap():
                return [8 + i if i < 8 else i - 8 if i < 16 else i for i in range(32)]

            def new_h(n, gain, step, squares):
                dve.tensor_scalar(h_hi[:, n, :], x[:, n, :], gain, None, ALU.mult).then_inc(h_step, 1)
                k = n + max(n - 2, 0) + 1
                dve.wait_ge(h_step, step + k)
                dve.scalar_tensor_tensor(out=h_lo[:, n, :], in0=x[:, n, :], scalar=gain,
                                         in1=h_hi[:, n, :].bitcast(F32), op0=ALU.mult,
                                         op1=ALU.subtract).then_inc(h_ready, 1)
                if n >= 2:
                    add_square(n - 1, squares + n, h_step)
                if n == KT - 1:
                    dve.wait_ge(h_step, step + (k + 1))
                    add_square(n, squares + KT, ssum_ready)

            def add_square(n, squares, out_sem):
                dve.wait_ge(sq_ready, squares)
                dve.tensor_tensor(ssum[:, :], ssum[:, :], sq_buf[:, n % 2, :], ALU.add).then_inc(out_sem, 1)

            def scale_ready(phase):
                dve.wait_ge(norm_root, phase + 1)
                dve.reciprocal(rs[:, :], rs[:, :]).then_inc(rs_ready, 1)

            def boundary(l, p, evacuate):
                for n in range(KT):
                    evacuate(n)
                    dve.wait_ge(x_ready, l * (3 * KT) + (p * KT + n + 1))
                    if n == 0:
                        dve.wait_ge(lp_loaded, l * 16 + 32)
                    new_h(n, lp[:, LG + p * KT + n:LG + p * KT + n + 1], l * (3 * B_STEPS) + (p + 1) * B_STEPS,
                          l * (3 * KT) + (p + 1) * KT)

            def ffn_half(l, half):
                cb = l * CH_LAYER + half * (CH_FFN + CH_MIX)
                fb = l * (2 * FT) + half * FT
                scale_ready(l * 3 + half * 2)
                with dve.Fori(0, FT // 2) as i:
                    for q in range(2):
                        if q == 0:
                            dve.wait_ge(rs_ready, l * 3 + (half * 2 + 1))
                        dve.wait_ge(chunk_done, i * 4 + (cb + 2 * q + 1 + RING))
                        dve.tensor_tensor(halves(g_buf[:, q, :]), pair(2 * q), halves(rs[:, :]),
                                          ALU.mult).then_inc(gate_scaled, 1)
                        dve.wait_ge(chunk_done, i * 4 + (cb + 2 * q + 2 + RING))
                        dve.wait_ge(silu_done, i * 2 + (fb + q + 1))
                        dve.tensor_tensor(halves(act_hi[:, i * 2 + q, :]), pair(2 * q + 1),
                                          halves(g_buf[:, q, :]), ALU.mult)
                        dve.tensor_tensor(halves(a_buf[:, q, :]), pair(2 * q + 1),
                                          halves(g_buf[:, q, :]), ALU.mult).then_inc(up_used, 1)
                        dve.wait_ge(up_used, i * 2 + (fb + q + 1))
                        dve.tensor_tensor(act_lo[:, i * 2 + q, :], a_buf[:, q, :],
                                          act_hi[:, i * 2 + q, :].bitcast(F32),
                                          ALU.subtract).then_inc(act_ready, 1)

                def evacuate(n):
                    dve.wait_ge(chunk_done, cb + (CH_GU + DN_CH * (n + 1) + RING))
                    dve.scalar_tensor_tensor(out=halves(a_buf[:, n % 2, :]), in0=pair(n % 4), scalar=0.5,
                                             in1=halves(rs[:, :]), op0=ALU.mult,
                                             op1=ALU.mult).then_inc(down_used, 1)
                    dve.wait_ge(down_used, l * (2 * KT) + (half * KT + n + 1 + 4))
                    dve.tensor_tensor(x[:, n, :], x[:, n, :], a_buf[:, n % 2, :], ALU.add).then_inc(x_ready, 1)

                boundary(l, half * 2, evacuate)

            def mixer(l):
                cb = l * CH_LAYER + CH_FFN
                steps = [0]

                def link(ins):
                    steps[0] += 1
                    ins.then_inc(m["v_step"], 1)
                    dve.wait_ge(m["v_step"], steps[0])

                def stats(u, src, mask, n, w, o, sink):
                    s = s_tile(u).rearrange("p (a n) -> p a n", a=n)[:, :, o:o + w]
                    dve.scalar_tensor_tensor(out=s, in0=src, scalar=HD ** -0.5,
                                             in1=mask.unsqueeze(1).to_broadcast([P, n, w]),
                                             op0=ALU.mult, op1=ALU.add).then_inc(m["masked"], 1)
                    dve.wait_ge(m["masked"], u + 1)
                    q = st[:, u % 2, :]
                    link(dve.tensor_reduce(q[:, 0:n], s, AX_X, ALU.max, negate=True))
                    link(dve.tensor_tensor(q[:, 4:4 + n], q[:, 0:n], nsk[:, sink:sink + n], ALU.min))
                    dve.tensor_tensor(q[:, 8:8 + n], q[:, 4:4 + n], lp[:, SK + sink:SK + sink + n],
                                      ALU.add).then_inc(m["statted"], 1)

                def klm_mask(b):
                    if b >= 2:
                        dve.wait_ge(m["gkv_done"], b - 1)
                    dve.tensor_scalar(klm[0:SAMP, b % 2, :], klT[0:SAMP, 4, :], bm[0:SAMP, b:b + 1], None,
                                      ALU.mult).then_inc(m["klm_made"], 1)

                for step, i in STEPS:
                    if step == "load":
                        link(dve.tensor_scalar(nsk[:, :], lp[:, SK:SK + 10], -1.0, None, ALU.mult))
                        link(dve.memset(qz[:, :], 0.0))
                        link(dve.memset(atts[:, :, :, :], 0.0))
                    elif step == "norm":
                        scale_ready(l * 3 + 1)
                        dve.wait_ge(rs_ready, l * 3 + 2)
                        link(dve.memset(ssum[:, :], 1.0))
                        link(dve.memset(ssum[:, 0:SEQ].rearrange("p (c n) -> p c n", n=CHUNK)[:, :, 0:1], 0.0))
                        link(dve.memset(ssum[:, SEQ:T].rearrange("p (c n) -> p c n", n=NT)[:, :, 0:1], 0.0))
                    elif step == "evac":
                        name = IN_JOBS[i]
                        src = pair(i % 2)
                        if name[0] == "z":
                            pr = int(name[1])
                            dve.wait_ge(m["in_done"], pr + 1)
                            dve.tensor_scalar(halves((t1, shuf)[pr][:, :]), src, lp[:, BG + pr:BG + pr + 1],
                                              None, ALU.add).then_inc(m["in_used"], 1)
                            continue
                        c = in_chunk(name) + (1 if name == "a" else 0)
                        dst = {"kS": kS, "vS": vS, "a": aT}.get(name)
                        if dst is None:
                            t = {"kG": kG, "qG": qG, "vG": vG, "rG": rG, "qS": qS}[name[:2]]
                            dst = t[:, int(name[2]), :]
                        else:
                            dst = dst[:, :]
                        dve.wait_ge(chunk_done, cb + (c + 1 + RING))
                        dve.tensor_tensor(halves(dst), src, halves(rs[:, :]), ALU.mult)\
                           .then_inc(m["in_used"], 1)
                    elif step == "rope":
                        t = kS[:, :] if i == 0 else qS[:, i - 1, :]
                        dve.wait_ge(m["loaded"], 16 * N_LOADS)
                        dve.wait_ge(m["in_used"], (1, 3, 4, 5, 6)[i])
                        link(dve.stream_shuffle(shuf[:, :], t, rope_swap()))
                        link(dve.tensor_tensor(shuf[:, :], shuf[:, :], sin_s[:, :], ALU.mult))
                        link(dve.tensor_tensor(t, t, cos_s[:, :], ALU.mult))
                        dve.tensor_tensor(t, t, shuf[:, :], ALU.add).then_inc(m["roped"], 1)
                        dve.wait_ge(m["roped"], i + 1)
                    elif step == "samp_q":
                        for j in range(4):
                            src = qS[:, j, SEQ:T].rearrange("p (b t) -> p b t", t=NT)
                            dve.tensor_copy(qc[:, :].rearrange("p (b n) -> p b n", n=16)[:, :, j * NT:(j + 1) * NT], src)
                            ins = dve.tensor_copy(
                                qz[:, :].rearrange("p (b n) -> p b n", n=P + 16)[:, :, j * NT:(j + 1) * NT], src)
                        ins.then_inc(m["q_set"], 1)
                    elif step == "score":
                        b, jj = UNITS[i]
                        o = 0 if b else WIN
                        if i >= 2:
                            dve.wait_ge(m["ptr_done"], i - 1)
                        elif i == 0:
                            dve.wait_ge(m["loaded"], 16 * N_LOADS)
                        dve.wait_ge(m["score_done"], i + 1)
                        src = ps[:, 4:6, :].rearrange("p b n -> p (b n)").rearrange("p (a n) -> p a n", a=4)
                        stats(i, src[:, :, o:256], m_swa[:, o:256], 4, 256 - o, o, 4 * jj)
                    elif step == "samp_s":
                        dve.wait_ge(m["ptr_done"], len(UNITS) - 1)
                        dve.wait_ge(m["ss_done"], 1)
                        stats(len(UNITS), ps[:, 4:6, 0:WIN + SAMP], m_samp[:, :], 2, WIN + SAMP, 0, 8)
                    elif step == "nrm":
                        dve.wait_ge(m["exped"], i + 1)
                        s = st[:, i % 2, :]
                        rows = unit_rows(i)
                        n = len(rows)
                        link(dve.tensor_tensor(s[:, 20:20 + n], s[:, 16:16 + n], s[:, 12:12 + n], ALU.add))
                        link(dve.reciprocal(s[:, 20:20 + n], s[:, 20:20 + n]))
                        for a, cols in rows:
                            ap = s_tile(i)[:, cols]
                            ins = dve.tensor_scalar(ap, ap, s[:, 20 + a:21 + a], None, ALU.mult)
                        ins.then_inc(m["normed"], 1)
                    elif step == "pv":
                        b, jj = UNITS[i]
                        dve.wait_ge(m["pv_done"], i + 1)
                        dve.tensor_copy(qS[:, 2 * jj:2 * jj + 2, b * WIN:(b + 1) * WIN],
                                        ps[:, 6, 0:256].rearrange("p (u n) -> p u n", u=2))\
                           .then_inc(m["attn_out"], 1)
                    elif step == "samp_o":
                        dve.wait_ge(m["so_done"], 1)
                        for j in range(4):
                            ins = dve.tensor_copy(
                                qS[:, j, SEQ:T].rearrange("p (b t) -> p b t", t=NT),
                                ps[:, 7, 0:P].rearrange("p (b n) -> p b n", n=16)[:, :, j * NT:(j + 1) * NT])
                        ins.then_inc(m["so_out"], 1)
                    elif step == "gate":
                        z = (t1, shuf)[i]
                        chunks = ((z[:, 0:SEQ], t3[:, 0:SEQ], CHUNK, 0), (z[:, SEQ:T], t3[:, SEQ:T], NT, 8))
                        dve.wait_ge(m["z_logged"], i + 1)
                        link(dve.scalar_tensor_tensor(out=z[:, :], in0=z[:, :], scalar=0.0, in1=t2[:, :],
                                                      op0=ALU.min, op1=ALU.subtract))
                        dve.tensor_tensor_scan(t3[:, :], ssum[:, :], z[:, :], 0.0, ALU.mult, ALU.add)\
                           .then_inc(m["z_summed"], 1)
                        dve.wait_ge(m["z_summed"], i + 1)
                        dve.wait_ge(m["z_exped"], i + 1)
                        for zz, _, n, o in chunks:
                            dve.tensor_copy(ebl[:, i, o:o + 8].unsqueeze(2),
                                            zz.rearrange("p (c n) -> p c n", n=n)[:, :, n - 1:n])
                        link(dve.scalar_tensor_tensor(out=qG[:, i, :], in0=qG[:, i, :], scalar=HD ** -0.5,
                                                      in1=z[:, :], op0=ALU.mult, op1=ALU.mult))
                        for zz, bb, n, o in chunks:
                            b3 = bb.rearrange("p (c n) -> p c n", n=n)
                            ins = dve.tensor_tensor(zz.rearrange("p (c n) -> p c n", n=n),
                                                    b3[:, :, n - 1:n].to_broadcast([P, 8, n]), b3,
                                                    ALU.subtract)
                        ins.then_inc(m["kl_diff"], 1)
                        dve.wait_ge(m["kl_exped"], i + 1)
                        dve.tensor_tensor((aT, t1)[i][:, :], kG[:, i, :], z[:, :], ALU.mult)\
                           .then_inc(m["kl_made"], 1)
                        dve.wait_ge(m["kl_made"], i + 1)
                        dve.tensor_tensor(kG[:, i, :], kG[:, i, :], t2[:, :], ALU.mult).then_inc(m["kb_made"], 1)
                    elif step == "kv":
                        dve.wait_ge(m["kv_done"], i + 1)
                        if i >= 3:
                            dve.wait_ge(m["o_done"], (i - 3) // 2 + 1)
                        if i == 0:
                            ins = dve.tensor_copy(s_ring[:, 1, :, :].rearrange("p a b -> p (a b)"),
                                                  ps[:, 2, 0:256])
                        else:
                            dve.wait_ge(m["state_made"], i)
                            for pr in range(2):
                                ins = dve.scalar_tensor_tensor(
                                    out=s_ring[:, (i + 1) % 4, pr, :], in0=s_ring[:, i % 4, pr, :],
                                    scalar=ebl[:, pr, i:i + 1], in1=ps[:, 2 + i % 2, pr * P:(pr + 1) * P],
                                    op0=ALU.mult, op1=ALU.add)
                        ins.then_inc(m["state_made"], 1)
                    elif step == "att":
                        if i == 0:
                            dve.wait_ge(m["so_done"], 1)
                            link(dve.memset(attm[:, :, :, :, :], 0.0))
                        if i >= 2:
                            dve.wait_ge(m["o_done"], i - 1)
                        dve.wait_ge(m["att_done"], i + 1)
                        for hh in range(2):
                            ins = dve.copy_predicated(attm[:, i % 2, hh, :, :],
                                                      m_gla[:, :].unsqueeze(1).to_broadcast([P, 2, P]),
                                                      ps[:, 4 + hh, 0:256].rearrange("p (h n) -> p h n", h=2))
                        ins.then_inc(m["att_out"], 1)
                    elif step == "gs_att":
                        dve.wait_ge(m["ga_done"], 1)
                        for hh in range(2):
                            ins = dve.copy_predicated(
                                atts[0:SAMP, hh, :, :],
                                m_glas[0:SAMP, :].unsqueeze(1).to_broadcast([SAMP, 2, SAMP]),
                                ps[0:SAMP, 4 + hh, 0:64].rearrange("p (h n) -> p h n", h=2))
                        ins.then_inc(m["ga_out"], 1)
                    elif step == "gs_kv":
                        if i == 0:
                            dve.wait_ge(m["kl_out"], 4)
                            klm_mask(0)
                            dve.wait_ge(m["go_done"], 1)
                        if i + 1 < NB:
                            klm_mask(i + 1)
                        dve.wait_ge(m["gkv_done"], i + 1)
                        for pr in range(2):
                            ins = dve.scalar_tensor_tensor(
                                out=s0[:, i, pr, :], in0=s0[:, i, pr, :], scalar=ebl[:, pr, 8 + i:9 + i],
                                in1=ps[:, 2 + i % 2, pr * P:(pr + 1) * P], op0=ALU.mult, op1=ALU.add)
                        ins.then_inc(m["gkv_used"], 1)
                    elif step == "smix":
                        if i == 0:
                            dve.wait_ge(m["stored"], 64)
                            dve.wait_ge(m["s_root"], 1)
                            link(dve.reciprocal(rs[:, :], rs[:, :]))
                        link(dve.scalar_tensor_tensor(out=qS[:, i, :], in0=qS[:, i, :],
                                                      scalar=lp[:, SG + i:SG + i + 1], in1=rs[:, :],
                                                      op0=ALU.mult, op1=ALU.mult))
                        link(dve.tensor_copy(mix_hi[:, i, :], qS[:, i, :]))
                        dve.tensor_tensor(mix_lo[:, i, :], qS[:, i, :], mix_hi[:, i, :].bitcast(F32),
                                          ALU.subtract).then_inc(m["mix_ready"], 1)
                    elif step == "gmix":
                        dve.wait_ge(m["g_root"], i + 1)
                        dve.wait_ge(m["r_silu"], i + 1)
                        root = sq_tile(i)
                        link(dve.reciprocal(root, root))
                        link(dve.scalar_tensor_tensor(out=oG[:, i, :], in0=oG[:, i, :],
                                                      scalar=lp[:, GG + i:GG + i + 1], in1=root,
                                                      op0=ALU.mult, op1=ALU.mult))
                        dve.tensor_tensor(mix_hi[:, 4 + i, :], oG[:, i, :], rG[:, i, :], ALU.mult)
                        link(dve.tensor_tensor(a_buf[:, i % 2, :], oG[:, i, :], rG[:, i, :], ALU.mult))
                        dve.tensor_tensor(mix_lo[:, 4 + i, :], a_buf[:, i % 2, :],
                                          mix_hi[:, 4 + i, :].bitcast(F32),
                                          ALU.subtract).then_inc(m["mix_ready"], 1)

                def evacuate(n):
                    dve.wait_ge(chunk_done, cb + (CH_IN + n + 1 + RING))
                    dve.tensor_tensor(halves(x[:, n, :]), pair(n % 4), halves(x[:, n, :]),
                                      ALU.add).then_inc(x_ready, 1)

                boundary(l, 1, evacuate)
                dve.wait_ge(mixer_left, l + 1)
                link(dve.memset(st[:, 0, 0:1], 0.0))
                dve.sem_clear(m_range)

            dve.sem_inc(down_used, 4)
            dve.memset(eps[:, :], EPS).then_inc(eps_set, 1)
            dve.wait_ge(start_loaded, 48)
            dve.wait_ge(lp_loaded, 16)
            for n in range(KT):
                new_h(n, g_first[:, n:n + 1], 0, 0)
            with dve.Fori(0, DEPTH) as l:
                ffn_half(l, 0)
                mixer(l)
                ffn_half(l, 1)
            scale_ready(DEPTH * 3)
            dve.wait_ge(rs_ready, DEPTH * 3 + 1)
            for n in range(KT):
                g = LG + 2 * KT + n
                dve.scalar_tensor_tensor(out=x[:, n, :], in0=x[:, n, :], scalar=lp[:, g:g + 1],
                                         in1=rs[:, :], op0=ALU.mult, op1=ALU.mult).then_inc(y_ready, 1)


def constants():
    half = HD // 8
    inv = np.power(np.float32(500000.0), -np.arange(half, dtype=np.float32) * np.float32(2.0 / (2 * half)))
    pos = np.concatenate([np.arange(SEQ), np.tile(PAST + np.arange(NT), NB)]).astype(np.float32)
    ang = (pos[:, None] * inv[None, :].astype(np.float32)).astype(np.float32).T
    cos_t, sin_t = np.ones((2, HD, T), np.float32), np.zeros((2, HD, T), np.float32)
    cos_t[:, 0:half], cos_t[:, half:2 * half] = np.cos(ang), np.cos(ang)
    sin_t[:, 0:half], sin_t[:, half:2 * half] = -np.sin(ang), np.sin(ang)
    q, k = np.arange(P)[:, None], np.arange(P)[None, :]
    low = np.float32(-1e30)
    swa = np.where(np.concatenate([k > q, k <= q], 1), np.float32(0), low)
    b, t = np.arange(P)[:, None] // 16, np.arange(P)[:, None] % NT
    new = np.arange(SAMP)[None, :]
    samp = np.where(np.concatenate([k > t, (new // NT == b) & (new % NT <= t)], 1), np.float32(0), low)
    gla = ((q <= k) & (q // CHUNK == k // CHUNK)).astype(np.int32)
    glas = ((q // NT == new // NT) & (q <= new)).astype(np.int32)
    bm = (q // NT == np.arange(NB)[None, :]).astype(np.float32)
    return {"cos_t": cos_t.reshape(P, T), "sin_t": sin_t.reshape(P, T), "swa_mask": swa, "samp_mask": samp,
            "gla_mask": gla, "glas_mask": glas, "bmask": bm, "ident_d": np.eye(P, dtype=np.float32)}


def weight_stream(w):
    out = np.zeros((CH_ALL, P, KT * P), np.float32)

    def gate_up(a):
        return a.reshape(KT, P, 2, FT, P).transpose(3, 2, 1, 0, 4).reshape(CH_GU, P, KT * P)

    def down(a, dst):
        a = a.reshape(FT, P, KT, P).transpose(2, 1, 0, 3).reshape(KT, P, FT * P)
        for c in range(DN_CH):
            n = min(KT * P, FT * P - c * KT * P)
            dst[c::DN_CH, :, 0:n] = a[:, :, c * KT * P:c * KT * P + n]

    def tile(a):
        return a.reshape(KT, P, -1).transpose(1, 0, 2)

    starts = {"qG": 0, "kG": 256, "vG": 512, "rG": 1024, "a": 1536, "qS": 1552, "kS": 2064, "vS": 2192}
    for l in range(DEPTH):
        o = l * CH_LAYER
        for half, n in enumerate(("1", "2")):
            b = o + half * (CH_FFN + CH_MIX)
            out[b:b + CH_GU] = gate_up(w[f"w_ffn{n}_gu"][l])
            down(w[f"w_ffn{n}_down"][l], out[b + CH_GU:b + CH_FFN])
        b = o + CH_FFN
        w_in = w["w_in"][l]
        for name in IN_TILES:
            c = b + in_chunk(name)
            if name == "a":
                a = tile(w_in[:, 1536:1552])
                for part in range(2):
                    out[c + part].reshape(P, KT, P)[:, 0:4, 0:16] = a[:, 4 * part:4 * part + 4]
                continue
            if name[:2] == "qS":
                j = int(name[2])
                cols = [1552 + h * HD + d for h in (j, 4 + j) for d in range(HD)]
            else:
                s = starts[name[:2]] + (P * int(name[2]) if len(name) == 3 else 0)
                cols = list(range(s, s + P))
            out[c] = tile(w_in[:, cols]).reshape(P, KT * P)
        rows = [4 * P + h * HD + d for j in range(4) for h in (j, 4 + j) for d in range(HD)]
        rows += list(range(4 * P))
        w_out = w["w_out"][l][rows].reshape(KT, P, KT, P).transpose(2, 1, 0, 3)
        out[b + CH_IN:b + CH_MIX] = w_out.reshape(KT, P, KT * P)
    return out


def kernel(**inputs):
    import concourse.bacc as _bacc
    from concourse.bass_utils import run_bass_kernel_spmd as _run

    w = {k: np.asarray(v) for k, v in inputs.items()}

    def feat(v):
        return v.reshape(-1, P).T

    tokens = np.concatenate([w["x_prompt"].reshape(SEQ, D), w["x_sample"].reshape(SAMP, D)])
    nexts = [w["norm_ffn1"][l + 1] if l + 1 < DEPTH else w["norm_final"] for l in range(DEPTH)]
    lparams = np.zeros((DEPTH, P, 44), np.float32)
    for l in range(DEPTH):
        sinks = w["attn_sinks"][l].reshape(2, 4)
        lparams[l, :, 0:8] = feat(w["norm_mix"][l])
        lparams[l, :, 8:16] = feat(w["norm_ffn2"][l])
        lparams[l, :, 16:24] = feat(nexts[l])
        lparams[l, :, 24:26] = feat(w["b_gate"][l])
        lparams[l, :, 26:30] = feat(w["gla_norm"][l])
        lparams[l, :, 30:34] = w["swa_norm"][l].reshape(2, 4, HD).transpose(0, 2, 1).reshape(P, 4)
        lparams[l, :, 34:42] = sinks.reshape(2, 2, 2).transpose(1, 0, 2).reshape(8)
        lparams[l, :, 42:44] = np.broadcast_to(sinks.T[None, :, None, :], (NB, 4, NT, 2)).reshape(P, 2)
    arrays = {
        "xT": tokens.T.reshape(KT, P, T).transpose(1, 0, 2),
        "stream": weight_stream(w),
        "gains": feat(w["norm_ffn1"][0]),
        "lparams": lparams,
        "wa2": w["w_gate_up"],
        **constants(),
        "s0_d": w["state_gla"].reshape(DEPTH, NB, 2, 2, HD, P).transpose(0, 3, 4, 1, 2, 5).reshape(DEPTH, P, NB, 2, P),
        "kc_d": w["cache_swa_k"].reshape(DEPTH, NB, WIN, P).transpose(0, 3, 1, 2),
        "vc_d": w["cache_swa_v"].reshape(DEPTH, NB, WIN, P).transpose(0, 2, 1, 3),
    }
    arrays = {k: np.ascontiguousarray(v) for k, v in arrays.items()}
    outs = {"y_d": (P, KT, T), "s_p_d": (DEPTH, P, 2, P), "kv_p_d": (DEPTH, 2, P, WIN + SAMP),
            "s_s_d": (DEPTH, P, NB, 2, P), "k_s_d": (DEPTH, P, NB, WIN - NT), "v_s_d": (DEPTH, WIN - NT, NB, P)}
    nc = _bacc.Bacc("TRN2", target_bir_lowering=False, num_devices=1)
    aps = {k: nc.dram_tensor(k, v.shape, mybir.dt.from_np(v.dtype), kind="ExternalInput").ap()
           for k, v in arrays.items()}
    aps |= {k: nc.dram_tensor(k, v, F32, kind="ExternalOutput").ap() for k, v in outs.items()}
    trunk(nc, **aps)
    r = _run(nc, [arrays], core_ids=[0]).results[0]

    y = r["y_d"].transpose(2, 1, 0).reshape(T, D)
    kv = r["kv_p_d"].transpose(0, 1, 3, 2)
    kv_new = kv[:, :, WIN:].reshape(DEPTH, 2, NB, NT, P)
    k_s = np.concatenate([r["k_s_d"].transpose(0, 2, 3, 1), kv_new[:, 0]], 2)
    v_s = np.concatenate([r["v_s_d"].transpose(0, 2, 1, 3), kv_new[:, 1]], 2)
    s_p = r["s_p_d"].reshape(DEPTH, 1, 2, HD, 2, P).transpose(0, 1, 4, 2, 3, 5).reshape(DEPTH, 1, GH, HD, P)
    s_s = r["s_s_d"].reshape(DEPTH, 2, HD, NB, 2, P).transpose(0, 3, 4, 1, 2, 5).reshape(DEPTH, NB, GH, HD, P)
    return (y[:SEQ].reshape(1, SEQ, D), y[SEQ:].reshape(NB, NT, D), s_p,
            kv[:, 0, :WIN].reshape(DEPTH, 1, WIN, 2, HD), kv[:, 1, :WIN].reshape(DEPTH, 1, WIN, 2, HD),
            s_s, k_s.reshape(DEPTH, NB, WIN, 2, HD), v_s.reshape(DEPTH, NB, WIN, 2, HD))
```

```python
from contextlib import ExitStack

import numpy as np

import concourse.bass as bass
from concourse import mybir

F32 = mybir.dt.float32
F32R = mybir.dt.float32r
I32 = mybir.dt.int32
ALU = mybir.AluOpType
ACT = mybir.ActivationFunctionType
AX_X = mybir.AxisListType.X

P = 128
D = 1024
DEPTH = 2
SEQ = 512
NB = 8
NT = 4
SAMP = NB * NT
T = SEQ + SAMP
TH = T // 2
KT = D // P
D_FF = 2816
FT = D_FF // P
WIN = 128
HD = 64
PAST = 2048
EPS = 1e-6
CHUNK = 64
NCHK = SEQ // CHUNK
NBLK = SEQ // WIN
GH = 4
DN_CH = -(-FT // KT)

CH_GU = 2 * FT
CH_FFN = CH_GU + KT * DN_CH
RING = 4
RAW = 2
IN_TILES = ["kS", "vS", "qS0", "qS1", "qS2", "qS3", "a", "kG0", "kG1", "qG0", "qG1",
            "vG0", "vG1", "vG2", "vG3", "rG0", "rG1", "rG2", "rG3"]
CH_IN = len(IN_TILES) + 1
CH_MIX = CH_IN + KT
CH_LAYER = 2 * CH_FFN + CH_MIX
CH_ALL = DEPTH * CH_LAYER + RING
assert CH_LAYER % RING == 0 and CH_IN % RING == 0

JOBS_FFN = 2 * FT + KT

IN_JOBS = ["kS", "vS", "qS0", "qS1", "qS2", "qS3", "a", "kG0", "z0", "z1", "kG1", "qG0", "qG1",
           "vG0", "vG1", "vG2", "vG3", "rG0", "rG1", "rG2", "rG3"]
UNITS = [(b, jj) for jj in range(2) for b in range(NBLK)]


def in_chunk(name):
    c = 0
    for n in IN_TILES:
        if n == name:
            return c
        c += 2 if n == "a" else 1
    raise KeyError(name)


def mixer_steps():
    n = len(UNITS)
    slot = {1: [("rope", 0)],
            2: [("vstr", 0), ("rope", 1)],
            3: [("rope", 2)],
            4: [("rope", 3)],
            6: [("rope", 4), ("samp_q", 0)],
            10: [("gatef", 0)],
            12: [("gate", 0)],
            13: [("vtr", 0), ("gatef", 1)],
            14: [("vtr", 1), ("samp_s", 0), ("nrm", n), ("gate", 1)],
            15: [("vtr", 2), ("samp_t", 0), ("kltr", 0), ("load_s0", 0)],
            16: [("kltr", 1), ("kltr", 2), ("samp_o", 0), ("vtr", 3), ("vtr", 4), ("gs_att", 0)],
            17: [("gs_o", 0), ("att", 0), ("kv", 0), ("kv", 1)] + [("ssq", j) for j in range(4)],
            18: [("att", 1), ("o", 0), ("kv", 2), ("kv", 3), ("gs_kv", 0), ("gs_kv", 1), ("silu", 0)],
            19: [("att", 2), ("o", 1), ("kv", 4), ("kv", 5), ("gs_kv", 2), ("gs_kv", 3), ("silu", 1)],
            20: [("att", 3), ("o", 2), ("kv", 6), ("kv", 7), ("gs_kv", 4), ("gs_kv", 5), ("silu", 2),
                 ("o", 3), ("silu", 3)]}
    unit_slots = [5, 6, 7, 9, 10, 11, 12, 13, 14, 15]
    steps = [("load", 0)]
    for i in range(len(IN_JOBS)):
        steps.append(("in", i))
        if i == 0:
            steps.append(("norm", 0))
        steps.append(("evac", i))
        mine = slot.get(i, [])
        if i in unit_slots:
            u = unit_slots.index(i)
            steps += [("pv", u - 2)] * (0 <= u - 2 < n)
            steps += [x for x in mine if x[0] == "vtr" or x == ("rope", 4)]
            steps += [("score", u)] * (0 <= u < n)
            steps += [("ptr", u - 1)] * (0 <= u - 1 < n)
            steps += [("nrm", u)] * (0 <= u < n)
            mine = [x for x in mine if x not in steps]
        steps += mine
    steps += [("sss", 0), ("gs_kv", 6), ("gs_kv", 7), ("sbc", 0), ("store", 0)]
    steps += [("gsq", h) for h in range(GH)]
    steps += [("smix", j) for j in range(4)]
    steps += [("gss", 0)]
    steps += [("gbc", h) for h in range(3)]
    steps += [("gmix", 0), ("gbc", 3)]
    steps += [("gmix", h) for h in range(1, 4)]
    return steps


def trunk(nc, xT, stream, gains, lparams, wa2, cos_t, sin_t, swa_mask, samp_mask, gla_mask,
          glas_mask, bmask, ident_d, s0_d, kc_d, vc_d, y_d, s_p_d, kv_p_d, s_s_d, k_s_d, v_s_d):
    U = T * 4
    base = -(-nc.sbuf_base // 64) * 64
    plan = {"at": base}

    def sb(name, shape, dt=F32, at=None):
        size = int(np.prod(shape[1:])) * 4
        if at is None:
            at = plan["at"]
            plan["at"] += -(-size // 64) * 64
        return nc.alloc_sbuf_tensor_at(name, list(shape), dt, offset=at)

    ctx = ExitStack()
    with ctx:
        x = sb("x", [P, KT, T])
        h_hi = sb("h_hi", [P, KT, T], F32R)
        h_lo = sb("h_lo", [P, KT, T], F32R)
        arena = plan["at"]
        act_hi = sb("act_hi", [P, FT, T], F32R)
        act_lo = sb("act_lo", [P, FT, T], F32R)
        w_raw = sb("w_raw", [P, RAW, KT * P])
        w_hi = sb("w_hi", [P, RING, KT * P], F32R)
        w_lo = sb("w_lo", [P, RING, KT * P], F32R)
        rs = sb("rs", [P, T])
        g_buf = sb("g_buf", [P, 2, T])
        a_buf = sb("a_buf", [P, 2, T])
        sq_buf = sb("sq_buf", [P, 2, T])
        ssum = sb("ssum", [P, T])
        s_ring = sb("s_ring", [P, 4, 2, P])
        ones = sb("ones", [P, P])
        ident = sb("ident", [P, P])
        lp = sb("lp", [P, 44])
        st = sb("st", [P, 2, 24])
        nsk = sb("nsk", [P, 10])
        eps = sb("eps", [P, 1])
        rt = sb("rt", [P, 25])
        g_first = sb("g_first", [P, KT])
        ebl = sb("ebl", [P, 2, 16])
        bm = sb("bm", [P, NB])
        assert plan["at"] <= nc.sbuf_usable_end, plan["at"]
        LG, BG, GG, SG, SK, SKS = 0, 24, 26, 30, 34, 42

        def mx(name, shape, off, dt=F32):
            assert off + int(np.prod(shape[1:])) * 4 <= 2 * FT * U, name
            return sb(name, shape, dt, at=arena + off)

        mix_hi = mx("mix_hi", [P, KT, T], 0, F32R)
        mix_lo = mx("mix_lo", [P, KT, T], 8 * U, F32R)
        kG = mx("kG", [P, 2, T], 0)
        qG = mx("qG", [P, 2, T], 2 * U)
        aT = mx("aT", [P, T], 4 * U)
        kS = mx("kS", [P, T], 5 * U)
        vS = mx("vS", [P, T], 6 * U)
        cos_s = mx("cos_s", [P, T], 7 * U)
        sin_s = mx("sin_s", [P, T], 8 * U)
        shuf = mx("shuf", [P, T], 9 * U)
        klT = mx("klT", [P, 5, 2 * P], 7 * U)
        t1 = mx("t1", [P, T], 10 * U)
        t2 = mx("t2", [P, T], 11 * U)
        t3 = mx("t3", [P, T], 12 * U)
        kc = mx("kc", [P, NB, WIN], 13 * U)
        qz = mx("qz", [P, NB * (P + 16)], 15 * U)
        qc = mx("qc", [P, P], 15 * U + 4608)
        wa = mx("wa", [P, 2 * P], 15 * U + 5120)
        s0 = mx("s0", [P, NB, 2, P], 13 * U)
        qS = mx("qS", [P, 4, T], 18 * U)
        vG = mx("vG", [P, 4, T], 22 * U)
        oG = mx("oG", [P, 4, T], 22 * U)
        rG = mx("rG", [P, 4, T], 26 * U)
        off = 30 * U
        v_tok = mx("v_tok", [P, 5, 4 * P], off)
        off += 10240
        vs_tok = mx("vs_tok", [P, 5, P], off)
        off += 2560
        vc = mx("vc", [P, NB, P], off)
        attm = mx("attm", [P, 2, 2, 2, P], off)
        off += 4096
        m_swa = mx("m_swa", [P, 2 * WIN], off)
        off += 1024
        m_gla = mx("m_gla", [P, P], off, I32)
        off += 512
        m_samp = mx("m_samp", [P, WIN + SAMP], off)
        off += 640
        m_glas = mx("m_glas", [P, SAMP], off, I32)
        off += 128
        klm = mx("klm", [P, 2, 2 * P], off)
        off += 2048
        atts = mx("atts", [P, 2, 2, SAMP], off)
        off += 512

        ps = ctx.enter_context(nc.psum_tensor("ps", [P, 8, 512], F32))

        def pair(i):
            return ps[:, 2 * i:2 * i + 2, 0:TH]

        def halves(ap):
            return ap.rearrange("p (h n) -> p h n", h=2)

        def s_tile(u):
            return (g_buf, sq_buf)[u % 2][:, :, :].rearrange("p a n -> p (a n)")[:, 0:1024]

        def unit_rows(u):
            if u == len(UNITS):
                return [(g, slice(g * 512, g * 512 + WIN + SAMP)) for g in range(2)]
            return [(a, slice(a * 256 + (0 if UNITS[u][0] else WIN), (a + 1) * 256)) for a in range(4)]

        p_t = a_buf[:, :, :].rearrange("p a n -> p (a n)")

        def sq_tile(j):
            return (g_buf, sq_buf)[j // 2][:, j % 2, :]

        def sem(name):
            return ctx.enter_context(nc.semaphore(name))

        raw_loaded = [sem(f"raw_loaded{i}") for i in range(RAW)]
        hi_ready = sem("hi_ready")
        lo_ready = sem("lo_ready")
        chunk_done = sem("chunk_done")
        gate_scaled = sem("gate_scaled")
        silu_done = sem("silu_done")
        up_used = sem("up_used")
        act_ready = sem("act_ready")
        down_used = sem("down_used")
        x_ready = sem("x_ready")
        sq_ready = sem("sq_ready")
        h_ready = sem("h_ready")
        h_step = sem("h_step")
        ssum_ready = sem("ssum_ready")
        norm_summed = sem("norm_summed")
        norm_root = sem("norm_root")
        rs_ready = sem("rs_ready")
        lp_loaded = sem("lp_loaded")
        start_loaded = sem("start_loaded")
        ones_set = sem("ones_set")
        eps_set = sem("eps_set")
        y_ready = sem("y_ready")
        y_stored = sem("y_stored")
        caches_moved = sem("caches_moved")
        mixer_left = sem("mixer_left")
        m_names = ["loaded", "s0_loaded", "stored", "in_done", "in_used", "v_step", "a_step",
                   "roped", "vst_done", "vst_out", "score_done", "masked", "statted", "exped",
                   "normed", "ptr_done", "pt_out", "pv_done", "attn_out", "z_logged", "z_summed",
                   "z_exped", "kl_diff", "kl_exped", "kl_made", "kltr_done", "kl_out", "vtr_done",
                   "v_out", "ss_done", "q_set", "st_done", "st_out", "so_done", "so_out",
                   "att_done", "att_out", "kv_done", "state_made", "o_done", "o_out", "ga_done",
                   "ga_out", "go_done", "go_out", "klm_made", "gkv_done", "gkv_used", "r_silu",
                   "gsq", "gss_done", "g_root", "g_recip", "gbc_done", "ssq", "sss_done", "s_root",
                   "s_recip", "sbc_done", "mix_made", "mix_high", "mix_ready", "kb_made"]
        m = {n: sem("m_" + n) for n in m_names}
        first, last = m[m_names[0]].num, m[m_names[-1]].num
        m_range = range(min(first, last), max(first, last) + 1)
        assert len(m_range) == len(m_names)

        STEPS = mixer_steps()

        def earlier(pos, step):
            return sum(x[0] == step for x in STEPS[:pos])

        B_STEPS = 2 * KT - 2
        N_LOADS = 9

        block = ctx.enter_context(nc.Block())

        @block.sync
        def _(sp):
            sp.dma_start(x[:, :, :], xT).then_inc(start_loaded, 16)
            sp.dma_start(ident[:, :], ident_d).then_inc(start_loaded, 16)
            sp.dma_start(bm[:, :], bmask).then_inc(start_loaded, 16)
            with sp.Fori(0, CH_ALL // RING) as i:
                for q in range(RING):
                    sp.wait_ge(lo_ready, i * RING + (q + 1 - RAW + RING))
                    sp.dma_start(w_raw[:, q % RAW, :], stream[i * RING + q]).then_inc(raw_loaded[q % RAW], 16)
            sp.wait_ge(y_ready, KT)
            sp.dma_start(y_d, x[:, :, :]).then_inc(y_stored, 16)
            sp.wait_ge(y_stored, 16)
            sp.wait_ge(caches_moved, DEPTH * 32)

        @block.gpsimd
        def _(pool):
            pool.memset(ones[:, :], 1.0).then_inc(ones_set, 1)
            pool.sem_inc(lo_ready, RING)
            for l in range(DEPTH):
                pool.dma_start(k_s_d[l, :, :, 0:WIN - NT], kc_d[l, :, :, NT:WIN]).then_inc(caches_moved, 16)
                pool.dma_start(v_s_d[l, 0:WIN - NT, :, :], vc_d[l, NT:WIN, :, :]).then_inc(caches_moved, 16)
            with pool.Fori(0, CH_ALL // RING) as i:
                for q in range(RING):
                    pool.wait_ge(hi_ready, i * RING + (q + 1))
                    pool.tensor_tensor(w_lo[:, q, :], w_raw[:, q % RAW, :], w_hi[:, q, :].bitcast(F32),
                                       ALU.subtract).then_inc(lo_ready, 1)

        @block.tensor
        def _(pe):
            pe.sem_inc(chunk_done, RING)

            def product(dst, slot, col, rhs_hi, rhs_lo, first, last):
                cols = slice(col, col + P)
                for w, r in ((w_hi, rhs_hi), (w_lo, rhs_hi), (w_hi, rhs_lo)):
                    for hf in range(2):
                        ins = pe.matmul(dst[:, hf, :], w[:, slot, cols], r[:, hf * TH:(hf + 1) * TH],
                                        start=first and w is w_hi and r is rhs_hi,
                                        stop=last and r is rhs_lo)
                return ins

            def model_tile(dst, chunk, slot, hb=None):
                pe.wait_ge(lo_ready, chunk + (1 + RING))
                for k in range(KT):
                    if hb is not None and k >= 5:
                        pe.wait_ge(h_ready, hb + (k + 1))
                    ins = product(dst, slot, k * P, h_hi[:, k, :], h_lo[:, k, :], k == 0, k == KT - 1)
                return ins

            def norm_sum(phase):
                pe.wait_ge(ssum_ready, phase + 1)
                for hf in range(2):
                    ins = pe.matmul(pair(3)[:, hf, :], ones[:, :], ssum[:, hf * TH:(hf + 1) * TH],
                                    start=True, stop=True)
                ins.then_inc(norm_summed, 1)

            def ffn_half(l, half):
                ch = l * CH_LAYER + half * (CH_FFN + CH_MIX)
                fb = l * (2 * FT) + half * FT
                hb = l * (3 * KT) + half * 2 * KT
                pe.wait_ge(h_ready, hb + 5)
                for q in range(4):
                    if q == 3:
                        pe.wait_ge(norm_root, l * 3 + (half * 2 + 1))
                    model_tile(pair(q), ch + q, q, hb if q == 0 else None).then_inc(chunk_done, 1)
                    if q == 0:
                        norm_sum(l * 3 + half * 2)
                with pe.Fori(1, FT // 2) as i:
                    for q in range(4):
                        pe.wait_ge(up_used if q % 2 else gate_scaled, i * 2 + (fb + (q // 2 - 1)))
                        model_tile(pair(q), i * 4 + (ch + q), q).then_inc(chunk_done, 1)
                with pe.Fori(0, KT // 4) as i:
                    for q in range(4):
                        pe.wait_ge(up_used if q % 2 else gate_scaled, fb + (FT - 1 + q // 2))
                        pe.wait_ge(down_used, i * 4 + (l * (2 * KT) + (half * KT + q + 1)))
                        for c in range(DN_CH):
                            s = (q * DN_CH + c) % RING
                            pe.wait_ge(lo_ready, i * (4 * DN_CH) + (ch + (CH_GU + q * DN_CH + c + 1 + RING)))
                            for k in range(c * KT, min(FT, (c + 1) * KT)):
                                if q == 0 and k >= FT - 4:
                                    pe.wait_ge(act_ready, fb + (k + 1))
                                ins = product(pair(q), s, (k - c * KT) * P, act_hi[:, k, :],
                                              act_lo[:, k, :], k == 0, k == FT - 1)
                            ins.then_inc(chunk_done, 1)

            def spread(p, col, samp_col):
                for tb in range(5):
                    w, c = (P, col + tb) if tb < 4 else (SAMP, samp_col)
                    ins = pe.matmul(ps[:, 2 * p + tb // 4, (tb % 4) * P:(tb % 4) * P + w],
                                    rt[0:w, c:c + 1].to_broadcast([w, P]), ident[0:w, 0:w],
                                    start=True, stop=True)
                return ins

            def mixer(l):
                ch = l * CH_LAYER + CH_FFN
                hb = l * (3 * KT) + KT
                for pos, (step, i) in enumerate(STEPS):
                    if step == "in":
                        name = IN_JOBS[i]
                        if i == 0:
                            pe.wait_ge(h_ready, hb + 6)
                        if i >= 2:
                            pe.wait_ge(m["in_used"], i - 1)
                        dst = pair(i % 2)
                        if name[0] == "z":
                            pr = int(name[1])
                            pe.wait_ge(m["loaded"], 16 * N_LOADS)
                            pe.wait_ge(m["in_used"], IN_JOBS.index("a") + 1)
                            for hf in range(2):
                                ins = pe.matmul(dst[:, hf, :], wa[0:16, pr * P:(pr + 1) * P],
                                                aT[0:16, hf * TH:(hf + 1) * TH], start=True, stop=True)
                            ins.then_inc(m["in_done"], 1)
                            continue
                        c = in_chunk(name)
                        if name == "a":
                            for part in range(2):
                                pe.wait_ge(lo_ready, ch + (c + part + 1 + RING))
                                for k in range(4 * part, 4 * part + 4):
                                    ins = product(dst, (c + part) % RING, (k % 4) * P, h_hi[:, k, :],
                                                  h_lo[:, k, :], k == 0, k == KT - 1)
                                if part == 0:
                                    ins.then_inc(chunk_done, 1)
                        else:
                            ins = model_tile(dst, ch + c, c % RING, hb if i == 0 else None)
                        ins.then_inc(chunk_done, 1)
                    elif step == "norm":
                        norm_sum(l * 3 + 1)
                    elif step == "vstr":
                        pe.wait_ge(m["in_used"], 2)
                        pe.wait_ge(norm_root, l * 3 + 2)
                        for tb in range(5):
                            w = P if tb < 4 else SAMP
                            dst = ps[0:w, 6, tb * P:(tb + 1) * P] if tb < 4 else ps[0:w, 7, 0:P]
                            ins = pe.transpose(dst, vS[:, tb * P:tb * P + w], ident[:, :])
                        ins.then_inc(m["vst_done"], 1)
                    elif step == "score":
                        b, jj = UNITS[i]
                        pe.wait_ge(m["roped"], 2 * jj + 3)
                        if i >= 1:
                            pe.wait_ge(m["masked"], i)
                        k0 = max(b - 1, 0) * WIN
                        o = 0 if b else WIN
                        for g in range(2):
                            rows = slice(g * HD, (g + 1) * HD)
                            for uu in range(2):
                                ins = pe.matmul(ps[:, 4 + g, uu * 256 + o:(uu + 1) * 256],
                                                qS[rows, 2 * jj + uu, b * WIN:(b + 1) * WIN],
                                                kS[rows, k0:(b + 1) * WIN], start=True, stop=True)
                        ins.then_inc(m["score_done"], 1)
                    elif step == "ptr":
                        b, jj = UNITS[i]
                        pe.wait_ge(m["normed"], i + 1)
                        if i >= 1:
                            pe.wait_ge(m["attn_out"], i)
                        else:
                            pe.wait_ge(m["vst_out"], 2)
                        if earlier(pos, "vtr"):
                            pe.wait_ge(m["v_out"], earlier(pos, "vtr"))
                        for a in range(4):
                            for kb in range(0 if b else 1, 2):
                                o = (a % 2) * 256 + kb * WIN
                                ins = pe.transpose(ps[:, 6 + a // 2, o:o + WIN],
                                                   s_tile(i)[:, a * 256 + kb * WIN:a * 256 + (kb + 1) * WIN],
                                                   ident[:, :])
                        ins.then_inc(m["ptr_done"], 1)
                    elif step == "pv":
                        b, jj = UNITS[i]
                        pe.wait_ge(m["pt_out"], i + 1)
                        for a in range(4):
                            g, uu = divmod(a, 2)
                            for kb in range(0 if b else 1, 2):
                                o = a * 256 + kb * WIN
                                ins = pe.matmul(ps[g * HD:(g + 1) * HD, 6, uu * WIN:(uu + 1) * WIN],
                                                vs_tok[:, b - 1 + kb, g * HD:(g + 1) * HD], p_t[:, o:o + WIN],
                                                start=kb == (0 if b else 1), stop=kb == 1)
                        ins.then_inc(m["pv_done"], 1)
                    elif step == "samp_s":
                        pe.wait_ge(m["loaded"], 16 * N_LOADS)
                        pe.wait_ge(m["masked"], len(UNITS))
                        pe.wait_ge(m["q_set"], 1)
                        for g in range(2):
                            rows = slice(g * HD, (g + 1) * HD)
                            for b in range(NB):
                                pe.matmul(ps[:, 4 + g, 0:WIN], qz[rows, b * P:(b + 1) * P], kc[rows, b, :],
                                          start=b == 0, stop=b == NB - 1)
                            ins = pe.matmul(ps[:, 4 + g, WIN:WIN + SAMP], qc[rows, :],
                                            kS[rows, SEQ:T], start=True, stop=True)
                        ins.then_inc(m["ss_done"], 1)
                    elif step == "samp_t":
                        pe.wait_ge(m["normed"], len(UNITS) + 1)
                        pe.wait_ge(m["attn_out"], len(UNITS))
                        src = s_tile(0)
                        for g in range(2):
                            pe.transpose(ps[:, 6, g * P:(g + 1) * P], src[:, g * 512:g * 512 + WIN],
                                         ident[:, :])
                            ins = pe.transpose(ps[0:SAMP, 6, (2 + g) * P:(3 + g) * P],
                                               src[:, g * 512 + WIN:g * 512 + WIN + SAMP], ident[:, :])
                        ins.then_inc(m["st_done"], 1)
                    elif step == "samp_o":
                        pe.wait_ge(m["st_out"], 2)
                        pe.wait_ge(m["v_out"], earlier(pos, "vtr"))
                        for g in range(2):
                            rows = slice(g * HD, (g + 1) * HD)
                            pe.matmul(ps[rows, 7, 0:P], vs_tok[0:SAMP, 4, rows],
                                      p_t[0:SAMP, (2 + g) * P:(3 + g) * P], start=True, stop=False)
                            for b in range(NB):
                                ins = pe.matmul(ps[rows, 7, b * 16:(b + 1) * 16], vc[:, b, rows],
                                                p_t[:, g * P + b * 16:g * P + b * 16 + 16],
                                                start=False, stop=b == NB - 1)
                        ins.then_inc(m["so_done"], 1)
                    elif step == "kltr":
                        pe.wait_ge(m["kl_made"], min(i + 1, 2))
                        pe.wait_ge(m["masked"], len(UNITS) + 1)
                        if i < 2:
                            for tb in range(4):
                                ins = pe.transpose(ps[:, 4 + i, tb * P:(tb + 1) * P],
                                                   (aT, t1)[i][:, tb * P:(tb + 1) * P], ident[:, :])
                        else:
                            pe.wait_ge(m["kl_out"], 1)
                            for pr in range(2):
                                ins = pe.transpose(ps[0:SAMP, 4, pr * P:(pr + 1) * P],
                                                   (aT, t1)[pr][:, SEQ:T], ident[:, :])
                        ins.then_inc(m["kltr_done"], 1)
                    elif step == "vtr":
                        if i < 3:
                            pe.wait_ge(m["pt_out"], earlier(pos, "ptr"))
                            if i:
                                pe.wait_ge(m["v_out"], i)
                        elif i == 3:
                            pe.wait_ge(m["st_out"], 2)
                        else:
                            pe.wait_ge(m["so_out"], 1)
                        if i < 4:
                            pe.wait_ge(m["in_used"], IN_JOBS.index(f"vG{i}") + 1)
                            for tb in range(4):
                                ins = pe.transpose(ps[:, 6 if i == 3 else 7, tb * P:(tb + 1) * P],
                                                   vG[:, i, tb * P:(tb + 1) * P], ident[:, :])
                        else:
                            for h in range(GH):
                                ins = pe.transpose(ps[0:SAMP, 7, h * P:(h + 1) * P], vG[:, h, SEQ:T],
                                                   ident[:, :])
                        ins.then_inc(m["vtr_done"], 1)
                    elif step == "kv":
                        pe.wait_ge(m["att_out"], i // 2 + 1)
                        rows = slice((i % 2) * CHUNK, (i % 2 + 1) * CHUNK)
                        for h in range(GH):
                            pr, hh = divmod(h, 2)
                            ins = pe.matmul(ps[hh * HD:(hh + 1) * HD, 4 + i % 2, pr * P:(pr + 1) * P],
                                            klT[rows, i // 2, h * HD:(h + 1) * HD],
                                            v_tok[rows, i // 2, h * P:(h + 1) * P], start=True, stop=True)
                        ins.then_inc(m["kv_done"], 1)
                    elif step == "att":
                        if i == 0:
                            pe.wait_ge(m["ga_out"], 1)
                        else:
                            pe.wait_ge(m["state_made"], 2 * i)
                        for h in range(GH):
                            pr, hh = divmod(h, 2)
                            rows = slice(hh * HD, (hh + 1) * HD)
                            ins = pe.matmul(ps[:, 4 + hh, pr * P:(pr + 1) * P], kG[rows, pr, i * P:(i + 1) * P],
                                            qG[rows, pr, i * P:(i + 1) * P], start=True, stop=True)
                        ins.then_inc(m["att_done"], 1)
                    elif step == "o":
                        pe.wait_ge(m["att_out"], i + 1)
                        pe.wait_ge(m["state_made"], 2 * i + 1)
                        if i == 0:
                            pe.wait_ge(m["go_out"], 1)
                        else:
                            pe.wait_ge(m["o_out"], i)
                        if earlier(pos, "gs_kv"):
                            pe.wait_ge(m["gkv_used"], earlier(pos, "gs_kv"))
                        for h in range(GH):
                            pr, hh = divmod(h, 2)
                            at, bank = pr * P, 6 + hh
                            pe.matmul(ps[:, bank, at:at + P], v_tok[:, i, h * P:(h + 1) * P],
                                      attm[:, i % 2, hh, pr, :], start=True, stop=False)
                            for c in (2 * i, 2 * i + 1):
                                if c == 0:
                                    continue
                                o = at + (c % 2) * CHUNK
                                ins = pe.matmul(ps[:, bank, o:o + CHUNK],
                                                s_ring[hh * HD:(hh + 1) * HD, c % 4, pr, :],
                                                qG[hh * HD:(hh + 1) * HD, pr, c * CHUNK:(c + 1) * CHUNK],
                                                start=False, stop=c == 2 * i + 1)
                        ins.then_inc(m["o_done"], 1)
                    elif step == "gs_att":
                        pe.wait_ge(m["kb_made"], 2)
                        pe.wait_ge(m["kl_out"], 3)
                        for h in range(GH):
                            pr, hh = divmod(h, 2)
                            rows = slice(hh * HD, (hh + 1) * HD)
                            ins = pe.matmul(ps[0:SAMP, 4 + hh, pr * SAMP:(pr + 1) * SAMP], kG[rows, pr, SEQ:T],
                                            qG[rows, pr, SEQ:T], start=True, stop=True)
                        ins.then_inc(m["ga_done"], 1)
                    elif step == "gs_o":
                        pe.wait_ge(m["ga_out"], 1)
                        pe.wait_ge(m["s0_loaded"], 16)
                        pe.wait_ge(m["v_out"], 5)
                        for h in range(GH):
                            pr, hh = divmod(h, 2)
                            rows = slice(hh * HD, (hh + 1) * HD)
                            pe.matmul(ps[:, 6 + hh, pr * SAMP:(pr + 1) * SAMP],
                                      v_tok[0:SAMP, 4, h * P:(h + 1) * P], atts[0:SAMP, hh, pr, :],
                                      start=True, stop=False)
                            for b in range(NB):
                                o = pr * SAMP + b * NT
                                ins = pe.matmul(ps[:, 6 + hh, o:o + NT], s0[rows, b, pr, :],
                                                qG[rows, pr, SEQ + b * NT:SEQ + (b + 1) * NT],
                                                start=False, stop=b == NB - 1)
                        ins.then_inc(m["go_done"], 1)
                    elif step == "gs_kv":
                        pe.wait_ge(m["klm_made"], i + 1)
                        pe.wait_ge(m["o_out"], earlier(pos, "o"))
                        if i >= 2:
                            pe.wait_ge(m["gkv_used"], i - 1)
                        for h in range(GH):
                            pr, hh = divmod(h, 2)
                            ins = pe.matmul(ps[hh * HD:(hh + 1) * HD, 6 + i % 2, pr * P:(pr + 1) * P],
                                            klm[0:SAMP, i % 2, h * HD:(h + 1) * HD],
                                            v_tok[0:SAMP, 4, h * P:(h + 1) * P], start=True, stop=True)
                        ins.then_inc(m["gkv_done"], 1)
                    elif step == "sss":
                        pe.wait_ge(m["in_used"], len(IN_JOBS))
                        pe.wait_ge(m["ssq"], 4)
                        for tb in range(5):
                            w = P if tb < 4 else SAMP
                            for j in range(4):
                                ins = pe.matmul(ps[0:w, 0, tb:tb + 1], sq_tile(j)[:, tb * P:tb * P + w],
                                                ones[:, 0:1], start=j == 0, stop=j == 3)
                        ins.then_inc(m["sss_done"], 1)
                    elif step == "gss":
                        pe.wait_ge(m["gsq"], GH)
                        for h in range(GH):
                            for tb in range(5):
                                w = P if tb < 4 else SAMP
                                c = h * 4 + tb if tb < 4 else 16 + h
                                ins = pe.matmul(ps[0:w, 2, c:c + 1], sq_tile(h)[:, tb * P:tb * P + w],
                                                ones[:, 0:1], start=True, stop=True)
                        ins.then_inc(m["gss_done"], 1)
                    elif step == "sbc":
                        pe.wait_ge(m["s_recip"], 2)
                        spread(0, 20, 24).then_inc(m["sbc_done"], 1)
                    elif step == "gbc":
                        pe.wait_ge(m["g_recip"], 2)
                        if i == 1:
                            pe.wait_ge(m["state_made"], NCHK)
                        elif i == 2:
                            pe.wait_ge(m["gkv_used"], NB)
                            pe.wait_ge(m["o_out"], NBLK)
                        elif i == 3:
                            pe.wait_ge(m["mix_made"], 5)
                        spread((1, 2, 3, 1)[i], 4 * i, 16 + i).then_inc(m["gbc_done"], 1)
                pe.wait_ge(m["mix_made"], 4)
                for n in range(KT):
                    c = CH_IN + n
                    pe.wait_ge(lo_ready, ch + (c + 1 + RING))
                    if n >= 4:
                        pe.wait_ge(x_ready, l * (3 * KT) + (KT + n - 3))
                    for k in range(KT):
                        if n == 0:
                            pe.wait_ge(m["mix_ready"], k + 1)
                        ins = product(pair(n % 4), c % RING, k * P, mix_hi[:, k, :], mix_lo[:, k, :],
                                      k == 0, k == KT - 1)
                    ins.then_inc(chunk_done, 1)

            pe.wait_ge(ones_set, 1)
            pe.wait_ge(start_loaded, 48)
            with pe.Fori(0, DEPTH) as l:
                ffn_half(l, 0)
                mixer(l)
                ffn_half(l, 1)
            pe.wait_ge(h_ready, DEPTH * 3 * KT + KT)
            norm_sum(DEPTH * 3)

        @block.scalar
        def _(act):
            def high_part(g, q):
                act.wait_ge(raw_loaded[q % RAW], g[1])
                act.wait_ge(chunk_done, g[0] + 1)
                act.activation(w_hi[:, q % RING, :], w_raw[:, q % RAW, :], ACT.Copy).then_inc(hi_ready, 1)

            def chunk(l, c, i=None, per=0):
                n, r = l * CH_LAYER + c, l * (CH_LAYER // RAW * 16) + (c // RAW + 1) * 16
                if i is not None:
                    n, r = n + i * per, r + i * (per // RAW * 16)
                return n, r

            def square(l, p, n):
                act.wait_ge(x_ready, l * (3 * KT) + (p * KT + n + 1))
                dst = ssum[:, :] if n == 0 else sq_buf[:, n % 2, :]
                act.activation(dst, x[:, n, :], ACT.Square).then_inc(sq_ready, 1)

            def root(phase):
                act.wait_ge(norm_summed, phase + 1)
                act.activation(halves(rs[:, :]), pair(3), ACT.Sqrt, bias=eps[:, :],
                               scale=1.0 / D).then_inc(norm_root, 1)

            def ffn_half(l, half):
                c0 = half * (CH_FFN + CH_MIX)
                fb = l * (2 * FT) + half * FT
                high_part(chunk(l, c0 + RING), 0)
                root(l * 3 + half * 2)
                for q in range(1, 4):
                    high_part(chunk(l, c0 + RING + q), q)
                    if q % 2:
                        silu(fb + q // 2, q // 2)
                with act.Fori(1, FT // 2) as i:
                    for q in range(4):
                        high_part(chunk(l, c0 + RING + q, i, 4), q)
                        if q % 2:
                            silu(i * 2 + (fb + q // 2), q // 2)
                for n in range(KT):
                    for c in range(DN_CH):
                        high_part(chunk(l, c0 + CH_GU + n * DN_CH + c + RING), n * DN_CH + c)
                    square(l, half * 2, n)

            def silu(f, q):
                act.wait_ge(gate_scaled, f + 1)
                act.activation(g_buf[:, q, :], g_buf[:, q, :], ACT.Silu).then_inc(silu_done, 1)

            def mixer(l):
                c0 = CH_FFN
                steps = [0]

                def link(ins):
                    steps[0] += 1
                    ins.then_inc(m["a_step"], 1)
                    act.wait_ge(m["a_step"], steps[0])

                for pos, (step, i) in enumerate(STEPS):
                    if step == "load":
                        act.wait_ge(chunk_done, l * CH_LAYER + (CH_FFN + RING))
                        act.dma_start(cos_s[:, :], cos_t).then_inc(m["loaded"], 16)
                        act.dma_start(sin_s[:, :], sin_t).then_inc(m["loaded"], 16)
                        act.dma_start(m_swa[:, :], swa_mask).then_inc(m["loaded"], 16)
                        act.dma_start(m_samp[:, :], samp_mask).then_inc(m["loaded"], 16)
                        act.dma_start(m_gla[:, :], gla_mask).then_inc(m["loaded"], 16)
                        act.dma_start(m_glas[:, :], glas_mask).then_inc(m["loaded"], 16)
                        act.dma_start(wa[0:16, :], wa2[l]).then_inc(m["loaded"], 16)
                        act.dma_start(kc[:, :, :], kc_d[l]).then_inc(m["loaded"], 16)
                        act.dma_start(vc[:, :, :], vc_d[l]).then_inc(m["loaded"], 16)
                    elif step == "in":
                        name = IN_JOBS[i]
                        if name[0] != "z":
                            for part in range(2 if name == "a" else 1):
                                c = in_chunk(name) + part
                                high_part(chunk(l, c0 + c + RING), c)
                    elif step == "norm":
                        root(l * 3 + 1)
                    elif step == "vstr":
                        act.wait_ge(m["vst_done"], 1)
                        act.activation(vs_tok[:, 0:4, :], ps[:, 6, :].rearrange("p (b n) -> p b n", b=4),
                                       ACT.Copy).then_inc(m["vst_out"], 1)
                        act.activation(vs_tok[0:SAMP, 4, :], ps[0:SAMP, 7, 0:P],
                                       ACT.Copy).then_inc(m["vst_out"], 1)
                    elif step in ("score", "samp_s"):
                        u = i if step == "score" else len(UNITS)
                        act.wait_ge(m["statted"], u + 1)
                        for a, cols in unit_rows(u):
                            ap = s_tile(u)[:, cols]
                            act.activation(ap, ap, ACT.Exp, bias=st[:, u % 2, 4 + a:5 + a],
                                           accum_out=st[:, u % 2, 16 + a:17 + a])
                        n = len(unit_rows(u))
                        act.activation(st[:, u % 2, 12:12 + n], st[:, u % 2, 8:8 + n],
                                       ACT.Exp).then_inc(m["exped"], 1)
                    elif step == "ptr":
                        act.wait_ge(m["ptr_done"], i + 1)
                        if i >= 1:
                            act.wait_ge(m["pv_done"], i)
                        o = 0 if UNITS[i][0] else WIN
                        act.activation(p_t[:, 0:1024].rearrange("p (a n) -> p a n", a=4)[:, :, o:256],
                                       ps[:, 6:8, :].rearrange("p b n -> p (b n)")
                                       .rearrange("p (a n) -> p a n", a=4)[:, :, o:256],
                                       ACT.Copy).then_inc(m["pt_out"], 1)
                    elif step == "samp_t":
                        act.wait_ge(m["st_done"], 1)
                        act.wait_ge(m["pv_done"], len(UNITS))
                        act.activation(p_t[:, 0:256], ps[:, 6, 0:256], ACT.Copy).then_inc(m["st_out"], 1)
                        act.activation(p_t[0:SAMP, 256:512], ps[0:SAMP, 6, 256:512],
                                       ACT.Copy).then_inc(m["st_out"], 1)
                    elif step == "gatef":
                        z = (t1, shuf)[i]
                        act.wait_ge(m["in_used"], IN_JOBS.index(f"z{i}") + 1)
                        if i:
                            act.wait_ge(m["kb_made"], 1)
                        link(act.activation(t2[:, :], z[:, :], ACT.Abs))
                        link(act.activation(t2[:, :], t2[:, :], ACT.Exp, scale=-1.0))
                        act.activation(t2[:, :], t2[:, :], ACT.Ln, bias=1.0).then_inc(m["z_logged"], 1)
                    elif step == "gate":
                        z = (t1, shuf)[i]
                        act.wait_ge(m["z_summed"], i + 1)
                        act.activation(z[:, :], t3[:, :], ACT.Exp, scale=1.0 / 16)
                        act.activation(t2[:, :], t3[:, :], ACT.Exp, scale=-1.0 / 16).then_inc(m["z_exped"], 1)
                        act.wait_ge(m["kl_diff"], i + 1)
                        act.activation(z[:, :], z[:, :], ACT.Exp, scale=1.0 / 16).then_inc(m["kl_exped"], 1)
                    elif step == "vtr":
                        act.wait_ge(m["vtr_done"], i + 1)
                        if i < 4:
                            act.activation(v_tok[:, 0:4, i * P:(i + 1) * P],
                                           ps[:, 6 if i == 3 else 7, :].rearrange("p (b n) -> p b n", b=4),
                                           ACT.Copy).then_inc(m["v_out"], 1)
                        else:
                            act.activation(v_tok[0:SAMP, 4, :], ps[0:SAMP, 7, :],
                                           ACT.Copy).then_inc(m["v_out"], 1)
                    elif step == "kltr":
                        act.wait_ge(m["kltr_done"], i + 1)
                        if i < 2:
                            act.activation(klT[:, 0:4, i * P:(i + 1) * P],
                                           ps[:, 4 + i, :].rearrange("p (b n) -> p b n", b=4),
                                           ACT.Copy).then_inc(m["kl_out"], 1)
                        else:
                            act.activation(klT[0:SAMP, 4, :], ps[0:SAMP, 4, 0:2 * P],
                                           ACT.Copy).then_inc(m["kl_out"], 1)
                    elif step == "load_s0":
                        act.wait_ge(m["ss_done"], 1)
                        act.dma_start(s0[:, :, :, :], s0_d[l]).then_inc(m["s0_loaded"], 16)
                    elif step == "silu":
                        act.wait_ge(m["in_used"], IN_JOBS.index(f"rG{i}") + 1)
                        act.activation(rG[:, i, :], rG[:, i, :], ACT.Silu).then_inc(m["r_silu"], 1)
                    elif step == "ssq":
                        act.wait_ge(m["so_out"], 1)
                        act.activation(sq_tile(i), qS[:, i, :], ACT.Square).then_inc(m["ssq"], 1)
                    elif step == "sss":
                        act.wait_ge(m["sss_done"], 1)
                        act.activation(rt[:, 20:24], ps[:, 0, 0:4], ACT.Sqrt, bias=eps[:, :],
                                       scale=1.0 / (4 * P)).then_inc(m["s_root"], 1)
                        act.activation(rt[0:SAMP, 24:25], ps[0:SAMP, 0, 4:5], ACT.Sqrt, bias=eps[0:SAMP, :],
                                       scale=1.0 / (4 * P)).then_inc(m["s_root"], 1)
                    elif step == "gss":
                        act.wait_ge(m["gss_done"], 1)
                        act.activation(rt[:, 0:16], ps[:, 2, 0:16], ACT.Sqrt, bias=eps[:, :],
                                       scale=1.0 / P).then_inc(m["g_root"], 1)
                        act.activation(rt[0:SAMP, 16:20], ps[0:SAMP, 2, 16:20], ACT.Sqrt,
                                       bias=eps[0:SAMP, :], scale=1.0 / P).then_inc(m["g_root"], 1)
                    elif step in ("smix", "gmix"):
                        k = i + (4 if step == "gmix" else 0)
                        act.wait_ge(m["mix_made"], k + 1)
                        if k == 0:
                            act.wait_ge(m["stored"], 64)
                        src = qS[:, i, :] if step == "smix" else a_buf[:, i % 2, :]
                        act.activation(mix_hi[:, k, :], src, ACT.Copy).then_inc(m["mix_high"], 1)
                    elif step == "o":
                        act.wait_ge(m["o_done"], i + 1)
                        for hh in range(2):
                            ins = act.activation(
                                oG[:, hh:4:2, i * P:(i + 1) * P],
                                ps[:, 6 + hh, 0:256].rearrange("p (h n) -> p h n", h=2),
                                ACT.Copy)
                        ins.then_inc(m["o_out"], 1)
                    elif step == "gs_o":
                        act.wait_ge(m["go_done"], 1)
                        for hh in range(2):
                            ins = act.activation(oG[:, hh:4:2, SEQ:T],
                                                 ps[:, 6 + hh, 0:64].rearrange("p (h n) -> p h n", h=2),
                                                 ACT.Copy)
                        ins.then_inc(m["go_out"], 1)
                    elif step == "store":
                        act.wait_ge(m["roped"], 1)
                        act.dma_start(kv_p_d[l, 0], kS[:, SEQ - WIN:T]).then_inc(m["stored"], 16)
                        act.dma_start(kv_p_d[l, 1], vS[:, SEQ - WIN:T]).then_inc(m["stored"], 16)
                        act.wait_ge(m["state_made"], NCHK)
                        act.dma_start(s_p_d[l], s_ring[:, NCHK % 4, :, :]).then_inc(m["stored"], 16)
                        act.wait_ge(m["gkv_used"], NB)
                        act.dma_start(s_s_d[l], s0[:, :, :, :]).then_inc(m["stored"], 16)
                    elif step == "gsq":
                        act.wait_ge(m["o_out"], NBLK)
                        act.wait_ge(m["go_out"], 1)
                        act.wait_ge(m["sss_done"], 1)
                        act.activation(sq_tile(i), oG[:, i, :], ACT.Square).then_inc(m["gsq"], 1)
                for n in range(KT):
                    high_part(chunk(l, c0 + CH_IN + n + RING), n)
                    if n == KT - 1:
                        act.sem_inc(mixer_left, 1)
                    square(l, 1, n)

            for q in range(RING):
                act.wait_ge(raw_loaded[q % RAW], (q // RAW + 1) * 16)
                act.wait_ge(chunk_done, q + 1)
                act.activation(w_hi[:, q, :], w_raw[:, q % RAW, :], ACT.Copy).then_inc(hi_ready, 1)
            act.dma_start(g_first[:, :], gains).then_inc(lp_loaded, 16)
            act.wait_ge(start_loaded, 48)
            act.wait_ge(eps_set, 1)
            for n in range(KT):
                dst = ssum[:, :] if n == 0 else sq_buf[:, n % 2, :]
                if n >= 3:
                    act.wait_ge(h_step, 2 * n - 2)
                act.activation(dst, x[:, n, :], ACT.Square).then_inc(sq_ready, 1)
            with act.Fori(0, DEPTH) as l:
                act.wait_ge(h_ready, l * (3 * KT) + KT)
                act.dma_start(lp[:, :], lparams[l]).then_inc(lp_loaded, 16)
                ffn_half(l, 0)
                mixer(l)
                ffn_half(l, 1)
            root(DEPTH * 3)

        @block.vector
        def _(dve):
            def rope_swap():
                return [8 + i if i < 8 else i - 8 if i < 16 else i for i in range(32)]

            def new_h(n, gain, step, squares):
                dve.tensor_scalar(h_hi[:, n, :], x[:, n, :], gain, None, ALU.mult).then_inc(h_step, 1)
                k = n + max(n - 2, 0) + 1
                dve.wait_ge(h_step, step + k)
                dve.scalar_tensor_tensor(out=h_lo[:, n, :], in0=x[:, n, :], scalar=gain,
                                         in1=h_hi[:, n, :].bitcast(F32), op0=ALU.mult,
                                         op1=ALU.subtract).then_inc(h_ready, 1)
                if n >= 2:
                    add_square(n - 1, squares + n, h_step)
                if n == KT - 1:
                    dve.wait_ge(h_step, step + (k + 1))
                    add_square(n, squares + KT, ssum_ready)

            def add_square(n, squares, out_sem):
                dve.wait_ge(sq_ready, squares)
                dve.tensor_tensor(ssum[:, :], ssum[:, :], sq_buf[:, n % 2, :], ALU.add).then_inc(out_sem, 1)

            def scale_ready(phase):
                dve.wait_ge(norm_root, phase + 1)
                dve.reciprocal(rs[:, :], rs[:, :]).then_inc(rs_ready, 1)

            def boundary(l, p, evacuate):
                for n in range(KT):
                    evacuate(n)
                    dve.wait_ge(x_ready, l * (3 * KT) + (p * KT + n + 1))
                    if n == 0:
                        dve.wait_ge(lp_loaded, l * 16 + 32)
                    new_h(n, lp[:, LG + p * KT + n:LG + p * KT + n + 1], l * (3 * B_STEPS) + (p + 1) * B_STEPS,
                          l * (3 * KT) + (p + 1) * KT)

            def ffn_half(l, half):
                cb = l * CH_LAYER + half * (CH_FFN + CH_MIX)
                fb = l * (2 * FT) + half * FT
                scale_ready(l * 3 + half * 2)
                with dve.Fori(0, FT // 2) as i:
                    for q in range(2):
                        if q == 0:
                            dve.wait_ge(rs_ready, l * 3 + (half * 2 + 1))
                        dve.wait_ge(chunk_done, i * 4 + (cb + 2 * q + 1 + RING))
                        dve.tensor_tensor(halves(g_buf[:, q, :]), pair(2 * q), halves(rs[:, :]),
                                          ALU.mult).then_inc(gate_scaled, 1)
                        dve.wait_ge(chunk_done, i * 4 + (cb + 2 * q + 2 + RING))
                        dve.wait_ge(silu_done, i * 2 + (fb + q + 1))
                        dve.tensor_tensor(halves(act_hi[:, i * 2 + q, :]), pair(2 * q + 1),
                                          halves(g_buf[:, q, :]), ALU.mult)
                        dve.tensor_tensor(halves(a_buf[:, q, :]), pair(2 * q + 1),
                                          halves(g_buf[:, q, :]), ALU.mult).then_inc(up_used, 1)
                        dve.wait_ge(up_used, i * 2 + (fb + q + 1))
                        dve.tensor_tensor(act_lo[:, i * 2 + q, :], a_buf[:, q, :],
                                          act_hi[:, i * 2 + q, :].bitcast(F32),
                                          ALU.subtract).then_inc(act_ready, 1)

                def evacuate(n):
                    dve.wait_ge(chunk_done, cb + (CH_GU + DN_CH * (n + 1) + RING))
                    dve.scalar_tensor_tensor(out=halves(a_buf[:, n % 2, :]), in0=pair(n % 4), scalar=0.5,
                                             in1=halves(rs[:, :]), op0=ALU.mult,
                                             op1=ALU.mult).then_inc(down_used, 1)
                    dve.wait_ge(down_used, l * (2 * KT) + (half * KT + n + 1 + 4))
                    dve.tensor_tensor(x[:, n, :], x[:, n, :], a_buf[:, n % 2, :], ALU.add).then_inc(x_ready, 1)

                boundary(l, half * 2, evacuate)

            def mixer(l):
                cb = l * CH_LAYER + CH_FFN
                steps = [0]

                def link(ins):
                    steps[0] += 1
                    ins.then_inc(m["v_step"], 1)
                    dve.wait_ge(m["v_step"], steps[0])

                def stats(u, src, mask, n, w, o, sink):
                    s = s_tile(u).rearrange("p (a n) -> p a n", a=n)[:, :, o:o + w]
                    dve.scalar_tensor_tensor(out=s, in0=src, scalar=HD ** -0.5,
                                             in1=mask.unsqueeze(1).to_broadcast([P, n, w]),
                                             op0=ALU.mult, op1=ALU.add).then_inc(m["masked"], 1)
                    dve.wait_ge(m["masked"], u + 1)
                    q = st[:, u % 2, :]
                    link(dve.tensor_reduce(q[:, 0:n], s, AX_X, ALU.max, negate=True))
                    link(dve.tensor_tensor(q[:, 4:4 + n], q[:, 0:n], nsk[:, sink:sink + n], ALU.min))
                    dve.tensor_tensor(q[:, 8:8 + n], q[:, 4:4 + n], lp[:, SK + sink:SK + sink + n],
                                      ALU.add).then_inc(m["statted"], 1)

                def spread_tile(p):
                    return ps[:, 2 * p:2 * p + 2, :].rearrange("p b n -> p (b n)")[:, 0:T]

                def low_part(k, full):
                    dve.wait_ge(m["mix_high"], k + 1)
                    if k == 0:
                        dve.wait_ge(m["stored"], 64)
                    dve.tensor_tensor(mix_lo[:, k, :], full, mix_hi[:, k, :].bitcast(F32),
                                      ALU.subtract).then_inc(m["mix_ready"], 1)

                def klm_mask(b):
                    if b >= 2:
                        dve.wait_ge(m["gkv_done"], b - 1)
                    dve.tensor_scalar(klm[0:SAMP, b % 2, :], klT[0:SAMP, 4, :], bm[0:SAMP, b:b + 1], None,
                                      ALU.mult).then_inc(m["klm_made"], 1)

                for pos, (step, i) in enumerate(STEPS):
                    if step == "load":
                        link(dve.tensor_scalar(nsk[:, :], lp[:, SK:SK + 10], -1.0, None, ALU.mult))
                        link(dve.memset(qz[:, :], 0.0))
                        link(dve.memset(atts[:, :, :, :], 0.0))
                    elif step == "norm":
                        scale_ready(l * 3 + 1)
                        dve.wait_ge(rs_ready, l * 3 + 2)
                        link(dve.memset(ssum[:, :], 1.0))
                        link(dve.memset(ssum[:, 0:SEQ].rearrange("p (c n) -> p c n", n=CHUNK)[:, :, 0:1], 0.0))
                        link(dve.memset(ssum[:, SEQ:T].rearrange("p (c n) -> p c n", n=NT)[:, :, 0:1], 0.0))
                    elif step == "evac":
                        name = IN_JOBS[i]
                        src = pair(i % 2)
                        if name[0] == "z":
                            pr = int(name[1])
                            dve.wait_ge(m["in_done"], pr + 1)
                            dve.tensor_scalar(halves((t1, shuf)[pr][:, :]), src, lp[:, BG + pr:BG + pr + 1],
                                              None, ALU.add).then_inc(m["in_used"], 1)
                            continue
                        c = in_chunk(name) + (1 if name == "a" else 0)
                        dst = {"kS": kS, "vS": vS, "a": aT}.get(name)
                        if dst is None:
                            t = {"kG": kG, "qG": qG, "vG": vG, "rG": rG, "qS": qS}[name[:2]]
                            dst = t[:, int(name[2]), :]
                        else:
                            dst = dst[:, :]
                        dve.wait_ge(chunk_done, cb + (c + 1 + RING))
                        dve.tensor_tensor(halves(dst), src, halves(rs[:, :]), ALU.mult)\
                           .then_inc(m["in_used"], 1)
                    elif step == "rope":
                        t = kS[:, :] if i == 0 else qS[:, i - 1, :]
                        dve.wait_ge(m["loaded"], 16 * N_LOADS)
                        dve.wait_ge(m["in_used"], (1, 3, 4, 5, 6)[i])
                        link(dve.stream_shuffle(shuf[:, :], t, rope_swap()))
                        link(dve.tensor_tensor(shuf[:, :], shuf[:, :], sin_s[:, :], ALU.mult))
                        link(dve.tensor_tensor(t, t, cos_s[:, :], ALU.mult))
                        dve.tensor_tensor(t, t, shuf[:, :], ALU.add).then_inc(m["roped"], 1)
                        dve.wait_ge(m["roped"], i + 1)
                    elif step == "samp_q":
                        for j in range(4):
                            src = qS[:, j, SEQ:T].rearrange("p (b t) -> p b t", t=NT)
                            dve.tensor_copy(qc[:, :].rearrange("p (b n) -> p b n", n=16)[:, :, j * NT:(j + 1) * NT], src)
                            ins = dve.tensor_copy(
                                qz[:, :].rearrange("p (b n) -> p b n", n=P + 16)[:, :, j * NT:(j + 1) * NT], src)
                        ins.then_inc(m["q_set"], 1)
                    elif step == "score":
                        b, jj = UNITS[i]
                        o = 0 if b else WIN
                        if i >= 2:
                            dve.wait_ge(m["ptr_done"], i - 1)
                        elif i == 0:
                            dve.wait_ge(m["loaded"], 16 * N_LOADS)
                        dve.wait_ge(m["score_done"], i + 1)
                        src = ps[:, 4:6, :].rearrange("p b n -> p (b n)").rearrange("p (a n) -> p a n", a=4)
                        stats(i, src[:, :, o:256], m_swa[:, o:256], 4, 256 - o, o, 4 * jj)
                    elif step == "samp_s":
                        dve.wait_ge(m["ptr_done"], len(UNITS) - 1)
                        dve.wait_ge(m["ss_done"], 1)
                        stats(len(UNITS), ps[:, 4:6, 0:WIN + SAMP], m_samp[:, :], 2, WIN + SAMP, 0, 8)
                    elif step == "nrm":
                        dve.wait_ge(m["exped"], i + 1)
                        s = st[:, i % 2, :]
                        rows = unit_rows(i)
                        n = len(rows)
                        link(dve.tensor_tensor(s[:, 20:20 + n], s[:, 16:16 + n], s[:, 12:12 + n], ALU.add))
                        link(dve.reciprocal(s[:, 20:20 + n], s[:, 20:20 + n]))
                        for a, cols in rows:
                            ap = s_tile(i)[:, cols]
                            ins = dve.tensor_scalar(ap, ap, s[:, 20 + a:21 + a], None, ALU.mult)
                        ins.then_inc(m["normed"], 1)
                    elif step == "pv":
                        b, jj = UNITS[i]
                        dve.wait_ge(m["pv_done"], i + 1)
                        dve.tensor_copy(qS[:, 2 * jj:2 * jj + 2, b * WIN:(b + 1) * WIN],
                                        ps[:, 6, 0:256].rearrange("p (u n) -> p u n", u=2))\
                           .then_inc(m["attn_out"], 1)
                    elif step == "samp_o":
                        dve.wait_ge(m["so_done"], 1)
                        for j in range(4):
                            ins = dve.tensor_copy(
                                qS[:, j, SEQ:T].rearrange("p (b t) -> p b t", t=NT),
                                ps[:, 7, 0:P].rearrange("p (b n) -> p b n", n=16)[:, :, j * NT:(j + 1) * NT])
                        ins.then_inc(m["so_out"], 1)
                    elif step == "gate":
                        z = (t1, shuf)[i]
                        chunks = ((z[:, 0:SEQ], t3[:, 0:SEQ], CHUNK, 0), (z[:, SEQ:T], t3[:, SEQ:T], NT, 8))
                        dve.wait_ge(m["z_logged"], i + 1)
                        link(dve.scalar_tensor_tensor(out=z[:, :], in0=z[:, :], scalar=0.0, in1=t2[:, :],
                                                      op0=ALU.min, op1=ALU.subtract))
                        dve.tensor_tensor_scan(t3[:, :], ssum[:, :], z[:, :], 0.0, ALU.mult, ALU.add)\
                           .then_inc(m["z_summed"], 1)
                        dve.wait_ge(m["z_summed"], i + 1)
                        dve.wait_ge(m["z_exped"], i + 1)
                        for zz, _, n, o in chunks:
                            dve.tensor_copy(ebl[:, i, o:o + 8].unsqueeze(2),
                                            zz.rearrange("p (c n) -> p c n", n=n)[:, :, n - 1:n])
                        link(dve.scalar_tensor_tensor(out=qG[:, i, :], in0=qG[:, i, :], scalar=HD ** -0.5,
                                                      in1=z[:, :], op0=ALU.mult, op1=ALU.mult))
                        for zz, bb, n, o in chunks:
                            b3 = bb.rearrange("p (c n) -> p c n", n=n)
                            ins = dve.tensor_tensor(zz.rearrange("p (c n) -> p c n", n=n),
                                                    b3[:, :, n - 1:n].to_broadcast([P, 8, n]), b3,
                                                    ALU.subtract)
                        ins.then_inc(m["kl_diff"], 1)
                        dve.wait_ge(m["kl_exped"], i + 1)
                        dve.tensor_tensor((aT, t1)[i][:, :], kG[:, i, :], z[:, :], ALU.mult)\
                           .then_inc(m["kl_made"], 1)
                        dve.wait_ge(m["kl_made"], i + 1)
                        dve.tensor_tensor(kG[:, i, :], kG[:, i, :], t2[:, :], ALU.mult).then_inc(m["kb_made"], 1)
                    elif step == "kv":
                        dve.wait_ge(m["kv_done"], i + 1)
                        if i >= 3:
                            dve.wait_ge(m["o_done"], (i - 3) // 2 + 1)
                        if i == 0:
                            ins = dve.tensor_copy(s_ring[:, 1, :, :].rearrange("p a b -> p (a b)"),
                                                  ps[:, 4, 0:256])
                        else:
                            dve.wait_ge(m["state_made"], i)
                            for pr in range(2):
                                ins = dve.scalar_tensor_tensor(
                                    out=s_ring[:, (i + 1) % 4, pr, :], in0=s_ring[:, i % 4, pr, :],
                                    scalar=ebl[:, pr, i:i + 1], in1=ps[:, 4 + i % 2, pr * P:(pr + 1) * P],
                                    op0=ALU.mult, op1=ALU.add)
                        ins.then_inc(m["state_made"], 1)
                    elif step == "att":
                        if i == 0:
                            dve.wait_ge(m["so_done"], 1)
                            link(dve.memset(attm[:, :, :, :, :], 0.0))
                        if i >= 2:
                            dve.wait_ge(m["o_done"], i - 1)
                        dve.wait_ge(m["att_done"], i + 1)
                        for hh in range(2):
                            ins = dve.copy_predicated(attm[:, i % 2, hh, :, :],
                                                      m_gla[:, :].unsqueeze(1).to_broadcast([P, 2, P]),
                                                      ps[:, 4 + hh, 0:256].rearrange("p (h n) -> p h n", h=2))
                        ins.then_inc(m["att_out"], 1)
                    elif step == "gs_att":
                        dve.wait_ge(m["ga_done"], 1)
                        for hh in range(2):
                            ins = dve.copy_predicated(
                                atts[0:SAMP, hh, :, :],
                                m_glas[0:SAMP, :].unsqueeze(1).to_broadcast([SAMP, 2, SAMP]),
                                ps[0:SAMP, 4 + hh, 0:64].rearrange("p (h n) -> p h n", h=2))
                        ins.then_inc(m["ga_out"], 1)
                    elif step == "gs_kv":
                        if i == 0:
                            dve.wait_ge(m["kl_out"], 3)
                            klm_mask(0)
                            dve.wait_ge(m["go_done"], 1)
                        if i + 1 < NB:
                            klm_mask(i + 1)
                        dve.wait_ge(m["gkv_done"], i + 1)
                        for pr in range(2):
                            ins = dve.scalar_tensor_tensor(
                                out=s0[:, i, pr, :], in0=s0[:, i, pr, :], scalar=ebl[:, pr, 8 + i:9 + i],
                                in1=ps[:, 6 + i % 2, pr * P:(pr + 1) * P], op0=ALU.mult, op1=ALU.add)
                        ins.then_inc(m["gkv_used"], 1)
                    elif step in ("sss", "gss"):
                        k, cols, samp = ("s", slice(20, 24), slice(24, 25)) if step == "sss" else \
                            ("g", slice(0, 16), slice(16, 20))
                        dve.wait_ge(m[k + "_root"], 2)
                        dve.reciprocal(rt[:, cols], rt[:, cols]).then_inc(m[k + "_recip"], 1)
                        dve.reciprocal(rt[0:SAMP, samp], rt[0:SAMP, samp]).then_inc(m[k + "_recip"], 1)
                    elif step == "smix":
                        dve.wait_ge(m["sbc_done"], 1)
                        dve.scalar_tensor_tensor(out=qS[:, i, :], in0=qS[:, i, :],
                                                 scalar=lp[:, SG + i:SG + i + 1], in1=spread_tile(0),
                                                 op0=ALU.mult, op1=ALU.mult).then_inc(m["mix_made"], 1)
                        if i:
                            low_part(i - 1, qS[:, i - 1, :])
                    elif step == "gmix":
                        dve.wait_ge(m["gbc_done"], i + 1)
                        link(dve.scalar_tensor_tensor(out=oG[:, i, :], in0=oG[:, i, :],
                                                      scalar=lp[:, GG + i:GG + i + 1],
                                                      in1=spread_tile((1, 2, 3, 1)[i]),
                                                      op0=ALU.mult, op1=ALU.mult))
                        if i == 0:
                            low_part(3, qS[:, 3, :])
                        dve.wait_ge(m["r_silu"], i + 1)
                        dve.tensor_tensor(a_buf[:, i % 2, :], oG[:, i, :], rG[:, i, :],
                                          ALU.mult).then_inc(m["mix_made"], 1)
                        if i:
                            low_part(3 + i, a_buf[:, (i - 1) % 2, :])
                        if i == GH - 1:
                            low_part(7, a_buf[:, i % 2, :])

                def evacuate(n):
                    dve.wait_ge(chunk_done, cb + (CH_IN + n + 1 + RING))
                    dve.tensor_tensor(halves(x[:, n, :]), pair(n % 4), halves(x[:, n, :]),
                                      ALU.add).then_inc(x_ready, 1)

                boundary(l, 1, evacuate)
                dve.wait_ge(mixer_left, l + 1)
                link(dve.memset(st[:, 0, 0:1], 0.0))
                dve.sem_clear(m_range)

            dve.sem_inc(down_used, 4)
            dve.memset(eps[:, :], EPS).then_inc(eps_set, 1)
            dve.wait_ge(start_loaded, 48)
            dve.wait_ge(lp_loaded, 16)
            for n in range(KT):
                new_h(n, g_first[:, n:n + 1], 0, 0)
            with dve.Fori(0, DEPTH) as l:
                ffn_half(l, 0)
                mixer(l)
                ffn_half(l, 1)
            scale_ready(DEPTH * 3)
            dve.wait_ge(rs_ready, DEPTH * 3 + 1)
            for n in range(KT):
                g = LG + 2 * KT + n
                dve.scalar_tensor_tensor(out=x[:, n, :], in0=x[:, n, :], scalar=lp[:, g:g + 1],
                                         in1=rs[:, :], op0=ALU.mult, op1=ALU.mult).then_inc(y_ready, 1)


def constants():
    half = HD // 8
    inv = np.power(np.float32(500000.0), -np.arange(half, dtype=np.float32) * np.float32(2.0 / (2 * half)))
    pos = np.concatenate([np.arange(SEQ), np.tile(PAST + np.arange(NT), NB)]).astype(np.float32)
    ang = (pos[:, None] * inv[None, :].astype(np.float32)).astype(np.float32).T
    cos_t, sin_t = np.ones((2, HD, T), np.float32), np.zeros((2, HD, T), np.float32)
    cos_t[:, 0:half], cos_t[:, half:2 * half] = np.cos(ang), np.cos(ang)
    sin_t[:, 0:half], sin_t[:, half:2 * half] = -np.sin(ang), np.sin(ang)
    q, k = np.arange(P)[:, None], np.arange(P)[None, :]
    low = np.float32(-1e30)
    swa = np.where(np.concatenate([k > q, k <= q], 1), np.float32(0), low)
    b, t = np.arange(P)[:, None] // 16, np.arange(P)[:, None] % NT
    new = np.arange(SAMP)[None, :]
    samp = np.where(np.concatenate([k > t, (new // NT == b) & (new % NT <= t)], 1), np.float32(0), low)
    gla = ((q <= k) & (q // CHUNK == k // CHUNK)).astype(np.int32)
    glas = ((q // NT == new // NT) & (q <= new)).astype(np.int32)
    bm = (q // NT == np.arange(NB)[None, :]).astype(np.float32)
    return {"cos_t": cos_t.reshape(P, T), "sin_t": sin_t.reshape(P, T), "swa_mask": swa, "samp_mask": samp,
            "gla_mask": gla, "glas_mask": glas, "bmask": bm, "ident_d": np.eye(P, dtype=np.float32)}


def weight_stream(w):
    out = np.zeros((CH_ALL, P, KT * P), np.float32)

    def gate_up(a):
        return a.reshape(KT, P, 2, FT, P).transpose(3, 2, 1, 0, 4).reshape(CH_GU, P, KT * P)

    def down(a, dst):
        a = a.reshape(FT, P, KT, P).transpose(2, 1, 0, 3).reshape(KT, P, FT * P)
        for c in range(DN_CH):
            n = min(KT * P, FT * P - c * KT * P)
            dst[c::DN_CH, :, 0:n] = a[:, :, c * KT * P:c * KT * P + n]

    def tile(a):
        return a.reshape(KT, P, -1).transpose(1, 0, 2)

    starts = {"qG": 0, "kG": 256, "vG": 512, "rG": 1024, "a": 1536, "qS": 1552, "kS": 2064, "vS": 2192}
    for l in range(DEPTH):
        o = l * CH_LAYER
        for half, n in enumerate(("1", "2")):
            b = o + half * (CH_FFN + CH_MIX)
            out[b:b + CH_GU] = gate_up(w[f"w_ffn{n}_gu"][l])
            down(w[f"w_ffn{n}_down"][l], out[b + CH_GU:b + CH_FFN])
        b = o + CH_FFN
        w_in = w["w_in"][l]
        for name in IN_TILES:
            c = b + in_chunk(name)
            if name == "a":
                a = tile(w_in[:, 1536:1552])
                for part in range(2):
                    out[c + part].reshape(P, KT, P)[:, 0:4, 0:16] = a[:, 4 * part:4 * part + 4]
                continue
            if name[:2] == "qS":
                j = int(name[2])
                cols = [1552 + h * HD + d for h in (j, 4 + j) for d in range(HD)]
            else:
                s = starts[name[:2]] + (P * int(name[2]) if len(name) == 3 else 0)
                cols = list(range(s, s + P))
            out[c] = tile(w_in[:, cols]).reshape(P, KT * P)
        rows = [4 * P + h * HD + d for j in range(4) for h in (j, 4 + j) for d in range(HD)]
        rows += list(range(4 * P))
        w_out = w["w_out"][l][rows].reshape(KT, P, KT, P).transpose(2, 1, 0, 3)
        out[b + CH_IN:b + CH_MIX] = w_out.reshape(KT, P, KT * P)
    return out


def kernel(**inputs):
    import concourse.bacc as _bacc
    from concourse.bass_utils import run_bass_kernel_spmd as _run

    w = {k: np.asarray(v) for k, v in inputs.items()}

    def feat(v):
        return v.reshape(-1, P).T

    tokens = np.concatenate([w["x_prompt"].reshape(SEQ, D), w["x_sample"].reshape(SAMP, D)])
    nexts = [w["norm_ffn1"][l + 1] if l + 1 < DEPTH else w["norm_final"] for l in range(DEPTH)]
    lparams = np.zeros((DEPTH, P, 44), np.float32)
    for l in range(DEPTH):
        sinks = w["attn_sinks"][l].reshape(2, 4)
        lparams[l, :, 0:8] = feat(w["norm_mix"][l])
        lparams[l, :, 8:16] = feat(w["norm_ffn2"][l])
        lparams[l, :, 16:24] = feat(nexts[l])
        lparams[l, :, 24:26] = feat(w["b_gate"][l])
        lparams[l, :, 26:30] = feat(w["gla_norm"][l])
        lparams[l, :, 30:34] = w["swa_norm"][l].reshape(2, 4, HD).transpose(0, 2, 1).reshape(P, 4)
        lparams[l, :, 34:42] = sinks.reshape(2, 2, 2).transpose(1, 0, 2).reshape(8)
        lparams[l, :, 42:44] = np.broadcast_to(sinks.T[None, :, None, :], (NB, 4, NT, 2)).reshape(P, 2)
    arrays = {
        "xT": tokens.T.reshape(KT, P, T).transpose(1, 0, 2),
        "stream": weight_stream(w),
        "gains": feat(w["norm_ffn1"][0]),
        "lparams": lparams,
        "wa2": w["w_gate_up"],
        **constants(),
        "s0_d": w["state_gla"].reshape(DEPTH, NB, 2, 2, HD, P).transpose(0, 3, 4, 1, 2, 5).reshape(DEPTH, P, NB, 2, P),
        "kc_d": w["cache_swa_k"].reshape(DEPTH, NB, WIN, P).transpose(0, 3, 1, 2),
        "vc_d": w["cache_swa_v"].reshape(DEPTH, NB, WIN, P).transpose(0, 2, 1, 3),
    }
    arrays = {k: np.ascontiguousarray(v) for k, v in arrays.items()}
    outs = {"y_d": (P, KT, T), "s_p_d": (DEPTH, P, 2, P), "kv_p_d": (DEPTH, 2, P, WIN + SAMP),
            "s_s_d": (DEPTH, P, NB, 2, P), "k_s_d": (DEPTH, P, NB, WIN - NT), "v_s_d": (DEPTH, WIN - NT, NB, P)}
    nc = _bacc.Bacc("TRN2", target_bir_lowering=False, num_devices=1)
    aps = {k: nc.dram_tensor(k, v.shape, mybir.dt.from_np(v.dtype), kind="ExternalInput").ap()
           for k, v in arrays.items()}
    aps |= {k: nc.dram_tensor(k, v, F32, kind="ExternalOutput").ap() for k, v in outs.items()}
    trunk(nc, **aps)
    r = _run(nc, [arrays], core_ids=[0]).results[0]

    y = r["y_d"].transpose(2, 1, 0).reshape(T, D)
    kv = r["kv_p_d"].transpose(0, 1, 3, 2)
    kv_new = kv[:, :, WIN:].reshape(DEPTH, 2, NB, NT, P)
    k_s = np.concatenate([r["k_s_d"].transpose(0, 2, 3, 1), kv_new[:, 0]], 2)
    v_s = np.concatenate([r["v_s_d"].transpose(0, 2, 1, 3), kv_new[:, 1]], 2)
    s_p = r["s_p_d"].reshape(DEPTH, 1, 2, HD, 2, P).transpose(0, 1, 4, 2, 3, 5).reshape(DEPTH, 1, GH, HD, P)
    s_s = r["s_s_d"].reshape(DEPTH, 2, HD, NB, 2, P).transpose(0, 3, 4, 1, 2, 5).reshape(DEPTH, NB, GH, HD, P)
    return (y[:SEQ].reshape(1, SEQ, D), y[SEQ:].reshape(NB, NT, D), s_p,
            kv[:, 0, :WIN].reshape(DEPTH, 1, WIN, 2, HD), kv[:, 1, :WIN].reshape(DEPTH, 1, WIN, 2, HD),
            s_s, k_s.reshape(DEPTH, NB, WIN, 2, HD), v_s.reshape(DEPTH, NB, WIN, 2, HD))
```

```python
from contextlib import ExitStack

import numpy as np

import concourse.bass as bass
from concourse import mybir

F32 = mybir.dt.float32
F32R = mybir.dt.float32r
I32 = mybir.dt.int32
ALU = mybir.AluOpType
ACT = mybir.ActivationFunctionType
AX_X = mybir.AxisListType.X

P = 128
D = 1024
DEPTH = 2
SEQ = 512
NB = 8
NT = 4
SAMP = NB * NT
T = SEQ + SAMP
TH = T // 2
KT = D // P
D_FF = 2816
FT = D_FF // P
WIN = 128
HD = 64
PAST = 2048
EPS = 1e-6
CHUNK = 64
NCHK = SEQ // CHUNK
NBLK = SEQ // WIN
GH = 4
DN_CH = -(-FT // KT)

CH_GU = 2 * FT
CH_FFN = CH_GU + KT * DN_CH
RING = 4
RAW = 2
IN_TILES = ["kS", "vS", "qS0", "qS1", "qS2", "qS3", "a", "kG0", "kG1", "qG0", "qG1",
            "vG0", "vG1", "vG2", "vG3", "rG0", "rG1", "rG2", "rG3"]
CH_IN = len(IN_TILES) + 1
CH_MIX = CH_IN + KT
CH_LAYER = 2 * CH_FFN + CH_MIX
CH_ALL = DEPTH * CH_LAYER + RING
assert CH_LAYER % RING == 0 and CH_IN % RING == 0

JOBS = ["kS", "vS", "qS0", "qS1", "qS2", "qS3", "a", "kG0", "z0", "kG1", "z1", "qG0", "qG1",
        "vG0", "vG1", "vG2", "vG3", "rG0", "rG1", "rG2", "squares", "rG3"] + [f"out{n}" for n in range(KT)]
UNITS = [(b, jj) for jj in range(2) for b in range(NBLK)]


def in_chunk(name):
    c = 0
    for n in IN_TILES:
        if n == name:
            return c
        c += 2 if n == "a" else 1
    raise KeyError(name)


def job_pair(i):
    return 2 if i == 2 else i % 2


def mixer_steps():
    n = len(UNITS)
    slot = {1: [("rope", 0)],
            2: [("vstr", 0), ("rope", 1), ("scan", 0)],
            3: [("rope", 2)],
            4: [("rope", 3)],
            6: [("rope", 4)],
            7: [("samp_q", 0)],
            10: [("gatef", 0), ("gatef", 1)],
            11: [("gate", 0)],
            12: [("decay", 0)],
            13: [("vtr", 0), ("keys", 0), ("gate", 1)],
            14: [("vtr", 1), ("decay", 1), ("samp_s", 0), ("nrm", n)],
            15: [("vtr", 2), ("keys", 1), ("samp_t", 0), ("kltr", 0), ("load_s0", 0)],
            16: [("samp_o", 0), ("store_kv", 0), ("kltr", 1), ("kltr", 2), ("vtr", 3),
                 ("vtr", 4), ("gs_att", 0)],
            17: [("gs_o", 0), ("att", 0), ("kv", 0), ("kv", 1)] + [("ssq", j) for j in range(4)],
            18: [("att", 1), ("o", 0), ("kv", 2), ("kv", 3), ("gs_kv", 0), ("gs_kv", 1), ("s_add", 0)],
            19: [("att", 2), ("o", 1), ("kv", 4), ("kv", 5), ("gs_kv", 2), ("gs_kv", 3)],
            20: [("s_norm", 0), ("smix", 0), ("smix", 1)],
            21: [("att", 3), ("smix", 2), ("o", 2), ("kv", 6), ("kv", 7), ("smix", 3)] +
                [("silu", j) for j in range(4)] + [("gs_kv", 4)],
            22: [("o", 3)] + [("gsq", h) for h in range(GH)] + [("gs_kv", 5), ("gs_kv", 6)],
            23: [("gss", 0), ("gs_kv", 7), ("store", 0)],
            24: [("gbc", 0), ("gbc", 1), ("gmix", 0)],
            25: [("gmix", 1), ("gbc", 2)],
            26: [("gbc", 3), ("gmix", 2)],
            27: [("gmix", 3)]}
    unit_slots = [4, 5, 6, 7, 9, 11, 12, 13, 14, 15]
    steps = [("load", 0)]
    for i, name in enumerate(JOBS):
        steps.append(("in", i))
        if i == 0:
            steps.append(("norm", 0))
        if name != "squares":
            steps.append(("evac", i))
        mine = slot.get(i, [])
        if i in unit_slots:
            u = unit_slots.index(i)
            steps += [("pv", u - 2)] * (0 <= u - 2 < n)
            steps += [x for x in mine if x[0] == "vtr"]
            steps += [("score", u)] * (0 <= u < n)
            steps += [("ptr", u - 1)] * (0 <= u - 1 < n)
            steps += [x for x in mine if x[0] in ("rope", "samp_q", "gate", "decay", "keys")]
            steps += [("nrm", u)] * (0 <= u < n)
            mine = [x for x in mine if x not in steps]
        steps += mine
    return steps


def trunk(nc, xT, stream, gains, lparams, wa2, cos_t, sin_t, swa_mask, samp_mask, gla_mask,
          glas_mask, bmask, ident_d, s0_d, kc_d, vc_d, y_d, s_p_d, kv_p_d, s_s_d, k_s_d, v_s_d):
    U = T * 4
    base = -(-nc.sbuf_base // 64) * 64
    plan = {"at": base}

    def sb(name, shape, dt=F32, at=None):
        size = int(np.prod(shape[1:])) * 4
        if at is None:
            at = plan["at"]
            plan["at"] += -(-size // 64) * 64
        return nc.alloc_sbuf_tensor_at(name, list(shape), dt, offset=at)

    ctx = ExitStack()
    with ctx:
        x = sb("x", [P, KT, T])
        h_hi = sb("h_hi", [P, KT, T], F32R)
        h_lo = sb("h_lo", [P, KT, T], F32R)
        arena = plan["at"]
        act_hi = sb("act_hi", [P, FT, T], F32R)
        act_lo = sb("act_lo", [P, FT, T], F32R)
        w_raw = sb("w_raw", [P, RAW, KT * P])
        w_hi = sb("w_hi", [P, RING, KT * P], F32R)
        w_lo = sb("w_lo", [P, RING, KT * P], F32R)
        rs = sb("rs", [P, T])
        g_buf = sb("g_buf", [P, 2, T])
        a_buf = sb("a_buf", [P, 2, T])
        sq_buf = sb("sq_buf", [P, 2, T])
        ssum = sb("ssum", [P, T])
        s_ring = sb("s_ring", [P, 4, 2, P])
        ones = sb("ones", [P, P])
        ident = sb("ident", [P, P])
        lp = sb("lp", [P, 44])
        st = sb("st", [P, 2, 24])
        nsk = sb("nsk", [P, 10])
        eps = sb("eps", [P, 1])
        rt = sb("rt", [P, 5 * GH])
        g_first = sb("g_first", [P, KT])
        ebl = sb("ebl", [P, 2, 16])
        bm = sb("bm", [P, NB])
        assert plan["at"] <= nc.sbuf_usable_end, plan["at"]
        LG, BG, GG, SG, SK, SKS = 0, 24, 26, 30, 34, 42

        def mx(name, shape, off, dt=F32):
            assert off + int(np.prod(shape[1:])) * 4 <= 2 * FT * U, name
            return sb(name, shape, dt, at=arena + off)

        kG = mx("kG", [P, 2, T], 0)
        qG = mx("qG", [P, 2, T], 2 * U)
        aT = mx("aT", [P, T], 4 * U)
        kS = mx("kS", [P, T], 5 * U)
        vS = mx("vS", [P, T], 6 * U)
        cos_s = mx("cos_s", [P, T], 7 * U)
        sin_s = mx("sin_s", [P, T], 8 * U)
        shuf = mx("shuf", [P, T], 9 * U)
        t1 = mx("t1", [P, T], 10 * U)
        t2 = mx("t2", [P, T], 11 * U)
        t3 = mx("t3", [P, T], 12 * U)
        kc = mx("kc", [P, NB, WIN], 13 * U)
        qz = mx("qz", [P, NB * (P + 16)], 15 * U)
        qc = mx("qc", [P, P], 15 * U + 4608)
        qd = mx("qd", [P, 2, NB, 2, NT], 15 * U + 4608)
        wa = mx("wa", [P, 2 * P], 15 * U + 5120)
        s0 = mx("s0", [P, NB, 2, P], 13 * U)
        qS = mx("qS", [P, 4, T], 18 * U)
        vG = mx("vG", [P, 4, T], 22 * U)
        oG = mx("oG", [P, 4, T], 22 * U)
        rG = mx("rG", [P, 4, T], 26 * U)
        mixS_hi = mx("mixS_hi", [P, 4, T], 9 * U, F32R)
        mixS_lo = mx("mixS_lo", [P, 4, T], 4 * U, F32R)
        mixG_hi = mx("mixG_hi", [P, 4, T], 0, F32R)
        mixG_lo = mx("mixG_lo", [P, 4, T], 26 * U, F32R)
        off = 30 * U
        v_tok = mx("v_tok", [P, 5, 4 * P], off)
        off += 10240
        vs_tok = mx("vs_tok", [P, 5, P], off)
        off += 2560
        vc = mx("vc", [P, NB, P], off)
        attm = mx("attm", [P, 2, 2, 2, P], off)
        off += 4096
        m_swa = mx("m_swa", [P, 2 * WIN], off)
        off += 1024
        m_gla = mx("m_gla", [P, P], off, I32)
        off += 512
        m_samp = mx("m_samp", [P, WIN + SAMP], off)
        off += 640
        m_glas = mx("m_glas", [P, SAMP], off, I32)
        off += 128
        klm = mx("klm", [P, 2, 2 * P], off)
        off += 2048
        atts = mx("atts", [P, 2, 2, SAMP], off)
        off += 512
        klT = mx("klT", [P, 5, 2 * P], off)
        off += 5120
        t4 = mx("t4", [P, T], off)

        ps = ctx.enter_context(nc.psum_tensor("ps", [P, 8, 512], F32))

        def pair(i):
            return ps[:, 2 * i:2 * i + 2, 0:TH]

        def halves(ap):
            return ap.rearrange("p (h n) -> p h n", h=2)

        def s_tile(u):
            return (g_buf, sq_buf)[u % 2][:, :, :].rearrange("p a n -> p (a n)")[:, 0:1024]

        def unit_rows(u):
            if u == len(UNITS):
                return [(g, slice(g * 512, g * 512 + WIN + SAMP)) for g in range(2)]
            return [(a, slice(a * 256 + (0 if UNITS[u][0] else WIN), (a + 1) * 256)) for a in range(4)]

        p_t = a_buf[:, :, :].rearrange("p a n -> p (a n)")

        def sq_tile(j):
            return (g_buf, sq_buf)[j // 2][:, j % 2, :]

        def go_out():
            return ps[:, 6, 0:4 * SAMP].rearrange("p (h b g t) -> p h b g t", h=2, b=NB, g=2)

        def mixed(k):
            hi, lo = (mixS_hi, mixS_lo) if k < 4 else (mixG_hi, mixG_lo)
            return hi[:, k % 4, :], lo[:, k % 4, :]

        def sem(name):
            return ctx.enter_context(nc.semaphore(name))

        raw_loaded = [sem(f"raw_loaded{i}") for i in range(RAW)]
        hi_ready = sem("hi_ready")
        lo_ready = sem("lo_ready")
        chunk_done = sem("chunk_done")
        gate_scaled = sem("gate_scaled")
        silu_done = sem("silu_done")
        up_used = sem("up_used")
        act_ready = sem("act_ready")
        down_used = sem("down_used")
        x_ready = sem("x_ready")
        sq_ready = sem("sq_ready")
        h_ready = sem("h_ready")
        h_step = sem("h_step")
        ssum_ready = sem("ssum_ready")
        norm_summed = sem("norm_summed")
        norm_root = sem("norm_root")
        rs_ready = sem("rs_ready")
        lp_loaded = sem("lp_loaded")
        x_loaded = [sem(f"x_loaded{n}") for n in range(KT)]
        start_loaded = sem("start_loaded")
        ones_set = sem("ones_set")
        eps_set = sem("eps_set")
        y_ready = sem("y_ready")
        y_stored = sem("y_stored")
        caches_moved = sem("caches_moved")
        mixer_left = sem("mixer_left")
        m_names = ["loaded", "s0_loaded", "stored", "kv_stored", "in_done", "in_used", "v_step", "a_step",
                   "roped", "vst_done", "vst_out", "score_done", "masked", "statted", "exped",
                   "normed", "ptr_done", "pt_out", "pv_done", "attn_out", "z_logged", "z_summed",
                   "z_exped", "kl_diff", "kl_exped", "kl_made", "kltr_done", "kl_out", "vtr_done",
                   "v_out", "ss_done", "q_set", "st_done", "st_out", "so_done", "so_out",
                   "att_done", "att_out", "kv_done", "state_made", "o_done", "o_out", "ga_done",
                   "ga_out", "go_done", "go_out", "klm_made", "gkv_done", "gkv_used", "r_silu",
                   "gsq", "gss_done", "g_root", "g_recip", "gbc_done", "ssq", "s_added", "ssum_done", "s_root", "q_paired",
                   "mix_made", "mix_high", "mix_ready", "kb_made"]
        m = {n: sem("m_" + n) for n in m_names}
        first, last = m[m_names[0]].num, m[m_names[-1]].num
        m_range = range(min(first, last), max(first, last) + 1)
        assert len(m_range) == len(m_names)

        STEPS = mixer_steps()

        def earlier(pos, step):
            return sum(x[0] == step for x in STEPS[:pos])

        B_STEPS = 2 * KT - 2
        N_LOADS = 9

        block = ctx.enter_context(nc.Block())

        @block.sync
        def _(sp):
            with sp.Fori(0, CH_ALL // RING) as i:
                for q in range(RING):
                    sp.wait_ge(lo_ready, i * RING + (q + 1 - RAW + RING))
                    sp.dma_start(w_raw[:, q % RAW, :], stream[i * RING + q]).then_inc(raw_loaded[q % RAW], 16)
            for n in range(KT):
                sp.wait_ge(y_ready, n + 1)
                sp.dma_start(y_d[:, n, :], x[:, n, :]).then_inc(y_stored, 16)
            sp.wait_ge(y_stored, KT * 16)
            sp.wait_ge(caches_moved, DEPTH * 32)

        @block.gpsimd
        def _(pool):
            pool.memset(ones[:, :], 1.0).then_inc(ones_set, 1)
            pool.sem_inc(lo_ready, RING)
            with pool.Fori(0, CH_ALL // RING) as i:
                for q in range(RING):
                    pool.wait_ge(hi_ready, i * RING + (q + 1))
                    pool.tensor_tensor(w_lo[:, q, :], w_raw[:, q % RAW, :], w_hi[:, q, :].bitcast(F32),
                                       ALU.subtract).then_inc(lo_ready, 1)

        @block.tensor
        def _(pe):
            pe.sem_inc(chunk_done, RING)

            def product(dst, slot, col, rhs_hi, rhs_lo, first, last):
                cols = slice(col, col + P)
                for w, r in ((w_hi, rhs_hi), (w_lo, rhs_hi), (w_hi, rhs_lo)):
                    for hf in range(2):
                        ins = pe.matmul(dst[:, hf, :], w[:, slot, cols], r[:, hf * TH:(hf + 1) * TH],
                                        start=first and w is w_hi and r is rhs_hi,
                                        stop=last and r is rhs_lo)
                return ins

            def model_tile(dst, chunk, slot, hb=None):
                pe.wait_ge(lo_ready, chunk + (1 + RING))
                for k in range(KT):
                    if hb is not None and k >= 5:
                        pe.wait_ge(h_ready, hb + (k + 1))
                    ins = product(dst, slot, k * P, h_hi[:, k, :], h_lo[:, k, :], k == 0, k == KT - 1)
                return ins

            def norm_sum(phase):
                pe.wait_ge(ssum_ready, phase + 1)
                square_sum(pair(3), ssum).then_inc(norm_summed, 1)

            def ffn_half(l, half):
                ch = l * CH_LAYER + half * (CH_FFN + CH_MIX)
                fb = l * (2 * FT) + half * FT
                hb = l * (3 * KT) + half * 2 * KT
                pe.wait_ge(h_ready, hb + 5)
                for q in range(4):
                    if q == 3:
                        pe.wait_ge(norm_root, l * 3 + (half * 2 + 1))
                    model_tile(pair(q), ch + q, q, hb if q == 0 else None).then_inc(chunk_done, 1)
                    if q == 0:
                        norm_sum(l * 3 + half * 2)
                with pe.Fori(1, FT // 2) as i:
                    for q in range(4):
                        pe.wait_ge(up_used if q % 2 else gate_scaled, i * 2 + (fb + (q // 2 - 1)))
                        model_tile(pair(q), i * 4 + (ch + q), q).then_inc(chunk_done, 1)
                with pe.Fori(0, KT // 4) as i:
                    for q in range(4):
                        pe.wait_ge(up_used if q % 2 else gate_scaled, fb + (FT - 1 + q // 2))
                        pe.wait_ge(down_used, i * 4 + (l * (2 * KT) + (half * KT + q + 1)))
                        for c in range(DN_CH):
                            s = (q * DN_CH + c) % RING
                            pe.wait_ge(lo_ready, i * (4 * DN_CH) + (ch + (CH_GU + q * DN_CH + c + 1 + RING)))
                            for k in range(c * KT, min(FT, (c + 1) * KT)):
                                if q == 0 and k >= FT - 4:
                                    pe.wait_ge(act_ready, fb + (k + 1))
                                ins = product(pair(q), s, (k - c * KT) * P, act_hi[:, k, :],
                                              act_lo[:, k, :], k == 0, k == FT - 1)
                            ins.then_inc(chunk_done, 1)

            def output_half(ch, half, n, dst):
                c = CH_IN + half * 4 + n // 2
                pe.wait_ge(lo_ready, ch + (c + 1 + RING))
                for k in range(4):
                    if n == 0:
                        pe.wait_ge(m["mix_ready"], half * 4 + k + 1)
                    ins = product(dst, c % RING, (n % 2 * 4 + k) * P, *mixed(half * 4 + k),
                                  k == 0, k == 3)
                ins.then_inc(chunk_done if n % 2 else m["in_done"], 1)

            def square_sum(dst, squares):
                for hf in range(2):
                    ins = pe.matmul(dst[:, hf, :], ones[:, :], squares[:, hf * TH:(hf + 1) * TH],
                                    start=True, stop=True)
                return ins

            def mixer(l):
                ch = l * CH_LAYER + CH_FFN
                hb = l * (3 * KT) + KT
                for pos, (step, i) in enumerate(STEPS):
                    if step == "in":
                        name = JOBS[i]
                        if i == 0:
                            pe.wait_ge(h_ready, hb + 6)
                        if i >= 3:
                            pe.wait_ge(m["in_used"], i - 1)
                        dst = pair(job_pair(i))
                        if name == "squares":
                            pe.wait_ge(m["s_added"], 1)
                            ins = square_sum(dst, sq_tile(0))
                            ins.then_inc(m["ssum_done"], 1)
                            continue
                        if name[:3] == "out":
                            output_half(ch, 0, int(name[3]), dst)
                            continue
                        if name[0] == "z":
                            pr = int(name[1])
                            pe.wait_ge(m["loaded"], 16 * N_LOADS)
                            pe.wait_ge(m["in_used"], JOBS.index("a") + 1)
                            for hf in range(2):
                                ins = pe.matmul(dst[:, hf, :], wa[0:16, pr * P:(pr + 1) * P],
                                                aT[0:16, hf * TH:(hf + 1) * TH], start=True, stop=True)
                            ins.then_inc(m["in_done"], 1)
                            continue
                        c = in_chunk(name)
                        if name == "a":
                            for part in range(2):
                                pe.wait_ge(lo_ready, ch + (c + part + 1 + RING))
                                for k in range(4 * part, 4 * part + 4):
                                    ins = product(dst, (c + part) % RING, (k % 4) * P, h_hi[:, k, :],
                                                  h_lo[:, k, :], k == 0, k == KT - 1)
                                if part == 0:
                                    ins.then_inc(chunk_done, 1)
                        else:
                            ins = model_tile(dst, ch + c, c % RING, hb if i == 0 else None)
                        ins.then_inc(chunk_done, 1)
                    elif step == "norm":
                        norm_sum(l * 3 + 1)
                    elif step == "vstr":
                        pe.wait_ge(m["in_used"], 2)
                        pe.wait_ge(norm_root, l * 3 + 2)
                        for tb in range(5):
                            w = P if tb < 4 else SAMP
                            dst = ps[0:w, 6, tb * P:(tb + 1) * P] if tb < 4 else ps[0:w, 7, 0:P]
                            ins = pe.transpose(dst, vS[:, tb * P:tb * P + w], ident[:, :])
                        ins.then_inc(m["vst_done"], 1)
                    elif step == "score":
                        b, jj = UNITS[i]
                        pe.wait_ge(m["roped"], 2 * jj + 3)
                        if i >= 1:
                            pe.wait_ge(m["masked"], i)
                        k0 = max(b - 1, 0) * WIN
                        o = 0 if b else WIN
                        for g in range(2):
                            rows = slice(g * HD, (g + 1) * HD)
                            for uu in range(2):
                                ins = pe.matmul(ps[:, 4 + g, uu * 256 + o:(uu + 1) * 256],
                                                qS[rows, 2 * jj + uu, b * WIN:(b + 1) * WIN],
                                                kS[rows, k0:(b + 1) * WIN], start=True, stop=True)
                        ins.then_inc(m["score_done"], 1)
                    elif step == "ptr":
                        b, jj = UNITS[i]
                        pe.wait_ge(m["normed"], i + 1)
                        if i >= 1:
                            pe.wait_ge(m["attn_out"], i)
                        else:
                            pe.wait_ge(m["vst_out"], 2)
                        if earlier(pos, "vtr"):
                            pe.wait_ge(m["v_out"], earlier(pos, "vtr"))
                        for a in range(4):
                            for kb in range(0 if b else 1, 2):
                                o = (a % 2) * 256 + kb * WIN
                                ins = pe.transpose(ps[:, 6 + a // 2, o:o + WIN],
                                                   s_tile(i)[:, a * 256 + kb * WIN:a * 256 + (kb + 1) * WIN],
                                                   ident[:, :])
                        ins.then_inc(m["ptr_done"], 1)
                    elif step == "pv":
                        b, jj = UNITS[i]
                        pe.wait_ge(m["pt_out"], i + 1)
                        for a in range(4):
                            g, uu = divmod(a, 2)
                            for kb in range(0 if b else 1, 2):
                                o = a * 256 + kb * WIN
                                ins = pe.matmul(ps[g * HD:(g + 1) * HD, 6, uu * WIN:(uu + 1) * WIN],
                                                vs_tok[:, b - 1 + kb, g * HD:(g + 1) * HD], p_t[:, o:o + WIN],
                                                start=kb == (0 if b else 1), stop=kb == 1)
                        ins.then_inc(m["pv_done"], 1)
                    elif step == "samp_s":
                        pe.wait_ge(m["loaded"], 16 * N_LOADS)
                        pe.wait_ge(m["masked"], len(UNITS))
                        pe.wait_ge(m["q_set"], 1)
                        for g in range(2):
                            rows = slice(g * HD, (g + 1) * HD)
                            for b in range(NB):
                                pe.matmul(ps[:, 4 + g, 0:WIN], qz[rows, b * P:(b + 1) * P], kc[rows, b, :],
                                          start=b == 0, stop=b == NB - 1)
                            ins = pe.matmul(ps[:, 4 + g, WIN:WIN + SAMP], qc[rows, :],
                                            kS[rows, SEQ:T], start=True, stop=True)
                        ins.then_inc(m["ss_done"], 1)
                    elif step == "samp_t":
                        pe.wait_ge(m["normed"], len(UNITS) + 1)
                        pe.wait_ge(m["attn_out"], len(UNITS))
                        src = s_tile(0)
                        for g in range(2):
                            pe.transpose(ps[:, 6, g * P:(g + 1) * P], src[:, g * 512:g * 512 + WIN],
                                         ident[:, :])
                            ins = pe.transpose(ps[0:SAMP, 6, (2 + g) * P:(3 + g) * P],
                                               src[:, g * 512 + WIN:g * 512 + WIN + SAMP], ident[:, :])
                        ins.then_inc(m["st_done"], 1)
                    elif step == "samp_o":
                        pe.wait_ge(m["st_out"], 2)
                        pe.wait_ge(m["v_out"], earlier(pos, "vtr"))
                        pe.matmul(ps[:, 7, 0:2 * P], vs_tok[0:SAMP, 4, :], p_t[0:SAMP, 2 * P:4 * P],
                                  start=True, stop=False)
                        for b in range(NB):
                            ins = pe.matmul(ps[:, 7, 0:2 * P].rearrange("p (g n) -> p g n", g=2)
                                            [:, :, b * 16:(b + 1) * 16], vc[:, b, :],
                                            p_t[:, 0:2 * P].rearrange("p (g n) -> p g n", g=2)
                                            [:, :, b * 16:(b + 1) * 16], start=False, stop=b == NB - 1)
                        ins.then_inc(m["so_done"], 1)
                    elif step == "kltr":
                        pe.wait_ge(m["kl_made"], min(i + 1, 2))
                        pe.wait_ge(m["masked"], len(UNITS) + 1)
                        if i < 2:
                            for tb in range(4):
                                ins = pe.transpose(ps[:, 4 + i, tb * P:(tb + 1) * P],
                                                   (aT, t1)[i][:, tb * P:(tb + 1) * P], ident[:, :])
                        else:
                            pe.wait_ge(m["kl_out"], 1)
                            for pr in range(2):
                                ins = pe.transpose(ps[0:SAMP, 4, pr * P:(pr + 1) * P],
                                                   (aT, t1)[pr][:, SEQ:T], ident[:, :])
                        ins.then_inc(m["kltr_done"], 1)
                    elif step == "vtr":
                        if i < 3:
                            pe.wait_ge(m["pt_out"], earlier(pos, "ptr"))
                            if i:
                                pe.wait_ge(m["v_out"], i)
                        elif i == 3:
                            pe.wait_ge(m["st_out"], 2)
                        else:
                            pe.wait_ge(m["so_out"], 1)
                        if i < 4:
                            pe.wait_ge(m["in_used"], JOBS.index(f"vG{i}") + 1)
                            for tb in range(4):
                                ins = pe.transpose(ps[:, 6 if i == 3 else 7, tb * P:(tb + 1) * P],
                                                   vG[:, i, tb * P:(tb + 1) * P], ident[:, :])
                        else:
                            for h in range(GH):
                                ins = pe.transpose(ps[0:SAMP, 7, h * P:(h + 1) * P], vG[:, h, SEQ:T],
                                                   ident[:, :])
                        ins.then_inc(m["vtr_done"], 1)
                    elif step == "kv":
                        pe.wait_ge(m["att_out"], i // 2 + 1)
                        rows = slice((i % 2) * CHUNK, (i % 2 + 1) * CHUNK)
                        for h in range(GH):
                            pr, hh = divmod(h, 2)
                            ins = pe.matmul(ps[hh * HD:(hh + 1) * HD, 4 + i % 2, pr * P:(pr + 1) * P],
                                            klT[rows, i // 2, h * HD:(h + 1) * HD],
                                            v_tok[rows, i // 2, h * P:(h + 1) * P], start=True, stop=True)
                        ins.then_inc(m["kv_done"], 1)
                    elif step == "att":
                        if i == 0:
                            pe.wait_ge(m["ga_out"], 1)
                        else:
                            pe.wait_ge(m["state_made"], 2 * i)
                        for h in range(GH):
                            pr, hh = divmod(h, 2)
                            rows = slice(hh * HD, (hh + 1) * HD)
                            ins = pe.matmul(ps[:, 4 + hh, pr * P:(pr + 1) * P], kG[rows, pr, i * P:(i + 1) * P],
                                            qG[rows, pr, i * P:(i + 1) * P], start=True, stop=True)
                        ins.then_inc(m["att_done"], 1)
                    elif step == "o":
                        pe.wait_ge(m["att_out"], i + 1)
                        pe.wait_ge(m["state_made"], 2 * i + 1)
                        if i == 0:
                            pe.wait_ge(m["go_out"], 1)
                        else:
                            pe.wait_ge(m["o_out"], i)
                        if earlier(pos, "gs_kv"):
                            pe.wait_ge(m["gkv_used"], earlier(pos, "gs_kv"))
                        for h in range(GH):
                            pr, hh = divmod(h, 2)
                            at, bank = pr * P, 6 + hh
                            pe.matmul(ps[:, bank, at:at + P], v_tok[:, i, h * P:(h + 1) * P],
                                      attm[:, i % 2, hh, pr, :], start=True, stop=False)
                            for c in (2 * i, 2 * i + 1):
                                if c == 0:
                                    continue
                                o = at + (c % 2) * CHUNK
                                ins = pe.matmul(ps[:, bank, o:o + CHUNK],
                                                s_ring[hh * HD:(hh + 1) * HD, c % 4, pr, :],
                                                qG[hh * HD:(hh + 1) * HD, pr, c * CHUNK:(c + 1) * CHUNK],
                                                start=False, stop=c == 2 * i + 1)
                        ins.then_inc(m["o_done"], 1)
                    elif step == "gs_att":
                        pe.wait_ge(m["kb_made"], 2)
                        pe.wait_ge(m["kl_out"], 3)
                        for h in range(GH):
                            pr, hh = divmod(h, 2)
                            rows = slice(hh * HD, (hh + 1) * HD)
                            ins = pe.matmul(ps[0:SAMP, 4 + hh, pr * SAMP:(pr + 1) * SAMP], kG[rows, pr, SEQ:T],
                                            qG[rows, pr, SEQ:T], start=True, stop=True)
                        ins.then_inc(m["ga_done"], 1)
                    elif step == "gs_o":
                        pe.wait_ge(m["ga_out"], 1)
                        pe.wait_ge(m["s0_loaded"], 16)
                        pe.wait_ge(m["v_out"], 5)
                        pe.wait_ge(m["q_paired"], 1)
                        for h in range(GH):
                            pr, hh = divmod(h, 2)
                            pe.matmul(go_out()[:, pr, :, hh, :], v_tok[0:SAMP, 4, h * P:(h + 1) * P],
                                      atts[0:SAMP, hh, pr, :].rearrange("p (b t) -> p b t", t=NT),
                                      start=h == 0, stop=False)
                        for pr in range(2):
                            for b in range(NB):
                                ins = pe.matmul(go_out()[:, pr, b, :, :], s0[:, b, pr, :], qd[:, pr, b, :, :],
                                                start=False, stop=pr == 1 and b == NB - 1)
                        ins.then_inc(m["go_done"], 1)
                    elif step == "gs_kv":
                        pe.wait_ge(m["klm_made"], i + 1)
                        pe.wait_ge(m["o_out"], earlier(pos, "o"))
                        if i >= 2:
                            pe.wait_ge(m["gkv_used"], i - 1)
                        for h in range(GH):
                            pr, hh = divmod(h, 2)
                            ins = pe.matmul(ps[hh * HD:(hh + 1) * HD, 6 + i % 2, pr * P:(pr + 1) * P],
                                            klm[0:SAMP, i % 2, h * HD:(h + 1) * HD],
                                            v_tok[0:SAMP, 4, h * P:(h + 1) * P], start=True, stop=True)
                        ins.then_inc(m["gkv_done"], 1)
                    elif step == "gss":
                        pe.wait_ge(m["gsq"], GH)
                        pe.wait_ge(m["att_out"], NBLK)
                        pe.wait_ge(m["state_made"], NCHK)
                        for h in range(GH):
                            for tb in range(5):
                                w = P if tb < 4 else SAMP
                                c = h * 4 + tb if tb < 4 else 16 + h
                                ins = pe.matmul(ps[0:w, 4, c:c + 1], sq_tile(h)[:, tb * P:tb * P + w],
                                                ones[:, 0:1], start=True, stop=True)
                        ins.then_inc(m["gss_done"], 1)
                    elif step == "gbc":
                        pe.wait_ge(m["g_recip"], 2)
                        if i == 1:
                            pe.wait_ge(m["gkv_used"], NB)
                            pe.wait_ge(m["o_out"], NBLK)
                        elif i >= 2:
                            pe.wait_ge(m["mix_made"], 4 + i - 1)
                        for tb in range(5):
                            w, c = (P, 4 * i + tb) if tb < 4 else (SAMP, 16 + i)
                            ins = pe.matmul(ps[:, 4 + 2 * (i % 2) + tb // 4, (tb % 4) * P:(tb % 4) * P + w],
                                            rt[0:w, c:c + 1].to_broadcast([w, P]), ident[0:w, 0:w],
                                            start=True, stop=True)
                        ins.then_inc(m["gbc_done"], 1)
                pe.wait_ge(m["in_used"], len(JOBS))
                for n in range(KT):
                    if n >= 4:
                        pe.wait_ge(x_ready, l * (3 * KT) + (KT + n - 3))
                    output_half(ch, 1, n, pair(n % 4))

            pe.wait_ge(ones_set, 1)
            pe.wait_ge(start_loaded, 32)
            with pe.Fori(0, DEPTH) as l:
                ffn_half(l, 0)
                mixer(l)
                ffn_half(l, 1)
            pe.wait_ge(h_ready, DEPTH * 3 * KT + KT)
            norm_sum(DEPTH * 3)

        @block.scalar
        def _(act):
            def high_part(g, q):
                act.wait_ge(raw_loaded[q % RAW], g[1])
                act.wait_ge(chunk_done, g[0] + 1)
                act.activation(w_hi[:, q % RING, :], w_raw[:, q % RAW, :], ACT.Copy).then_inc(hi_ready, 1)

            def chunk(l, c, i=None, per=0):
                n, r = l * CH_LAYER + c, l * (CH_LAYER // RAW * 16) + (c // RAW + 1) * 16
                if i is not None:
                    n, r = n + i * per, r + i * (per // RAW * 16)
                return n, r

            def square(l, p, n):
                act.wait_ge(x_ready, l * (3 * KT) + (p * KT + n + 1))
                dst = ssum[:, :] if n == 0 else sq_buf[:, n % 2, :]
                act.activation(dst, x[:, n, :], ACT.Square).then_inc(sq_ready, 1)

            def root(phase):
                act.wait_ge(norm_summed, phase + 1)
                act.activation(halves(rs[:, :]), pair(3), ACT.Sqrt, bias=eps[:, :],
                               scale=1.0 / D).then_inc(norm_root, 1)

            def ffn_half(l, half):
                c0 = half * (CH_FFN + CH_MIX)
                fb = l * (2 * FT) + half * FT
                high_part(chunk(l, c0 + RING), 0)
                root(l * 3 + half * 2)
                for q in range(1, 4):
                    high_part(chunk(l, c0 + RING + q), q)
                    if q % 2:
                        silu(fb + q // 2, q // 2)
                with act.Fori(1, FT // 2) as i:
                    for q in range(4):
                        high_part(chunk(l, c0 + RING + q, i, 4), q)
                        if q % 2:
                            silu(i * 2 + (fb + q // 2), q // 2)
                for n in range(KT):
                    for c in range(DN_CH):
                        high_part(chunk(l, c0 + CH_GU + n * DN_CH + c + RING), n * DN_CH + c)
                    square(l, half * 2, n)

            def silu(f, q):
                act.wait_ge(gate_scaled, f + 1)
                act.activation(g_buf[:, q, :], g_buf[:, q, :], ACT.Silu).then_inc(silu_done, 1)

            def mixer(l):
                c0 = CH_FFN
                steps = [0]

                def link(ins):
                    steps[0] += 1
                    ins.then_inc(m["a_step"], 1)
                    act.wait_ge(m["a_step"], steps[0])

                for pos, (step, i) in enumerate(STEPS):
                    if step == "load":
                        act.wait_ge(chunk_done, l * CH_LAYER + (CH_FFN + RING))
                        act.dma_start(cos_s[:, :], cos_t).then_inc(m["loaded"], 16)
                        act.dma_start(sin_s[:, :], sin_t).then_inc(m["loaded"], 16)
                        act.dma_start(m_swa[:, :], swa_mask).then_inc(m["loaded"], 16)
                        act.dma_start(m_samp[:, :], samp_mask).then_inc(m["loaded"], 16)
                        act.dma_start(m_gla[:, :], gla_mask).then_inc(m["loaded"], 16)
                        act.dma_start(m_glas[:, :], glas_mask).then_inc(m["loaded"], 16)
                        act.dma_start(wa[0:16, :], wa2[l]).then_inc(m["loaded"], 16)
                        act.dma_start(kc[:, :, :], kc_d[l]).then_inc(m["loaded"], 16)
                        act.dma_start(vc[:, :, :], vc_d[l]).then_inc(m["loaded"], 16)
                    elif step == "in":
                        name = JOBS[i]
                        if name[:3] == "out":
                            n = int(name[3])
                            if n % 2:
                                high_part(chunk(l, c0 + CH_IN + n // 2 + RING), n // 2)
                        elif name[0] != "z" and name != "squares":
                            for part in range(2 if name == "a" else 1):
                                c = in_chunk(name) + part
                                high_part(chunk(l, c0 + c + RING), c)
                    elif step == "norm":
                        root(l * 3 + 1)
                    elif step == "vstr":
                        act.wait_ge(m["vst_done"], 1)
                        act.activation(vs_tok[:, 0:4, :], ps[:, 6, :].rearrange("p (b n) -> p b n", b=4),
                                       ACT.Copy).then_inc(m["vst_out"], 1)
                        act.activation(vs_tok[0:SAMP, 4, :], ps[0:SAMP, 7, 0:P],
                                       ACT.Copy).then_inc(m["vst_out"], 1)
                    elif step in ("score", "samp_s"):
                        u = i if step == "score" else len(UNITS)
                        act.wait_ge(m["statted"], u + 1)
                        for a, cols in unit_rows(u):
                            ap = s_tile(u)[:, cols]
                            act.activation(ap, ap, ACT.Exp, bias=st[:, u % 2, 4 + a:5 + a],
                                           accum_out=st[:, u % 2, 16 + a:17 + a])
                        n = len(unit_rows(u))
                        act.activation(st[:, u % 2, 12:12 + n], st[:, u % 2, 8:8 + n],
                                       ACT.Exp).then_inc(m["exped"], 1)
                    elif step == "ptr":
                        act.wait_ge(m["ptr_done"], i + 1)
                        if i >= 1:
                            act.wait_ge(m["pv_done"], i)
                        o = 0 if UNITS[i][0] else WIN
                        act.activation(p_t[:, 0:1024].rearrange("p (a n) -> p a n", a=4)[:, :, o:256],
                                       ps[:, 6:8, :].rearrange("p b n -> p (b n)")
                                       .rearrange("p (a n) -> p a n", a=4)[:, :, o:256],
                                       ACT.Copy).then_inc(m["pt_out"], 1)
                    elif step == "samp_t":
                        act.wait_ge(m["st_done"], 1)
                        act.wait_ge(m["pv_done"], len(UNITS))
                        act.activation(p_t[:, 0:256], ps[:, 6, 0:256], ACT.Copy).then_inc(m["st_out"], 1)
                        act.activation(p_t[0:SAMP, 256:512], ps[0:SAMP, 6, 256:512],
                                       ACT.Copy).then_inc(m["st_out"], 1)
                    elif step == "gatef":
                        z = (t1, shuf)[i]
                        act.wait_ge(m["in_used"], JOBS.index(f"z{i}") + 1)
                        log = (t2, t4)[i]
                        link(act.activation(log[:, :], z[:, :], ACT.Abs))
                        link(act.activation(log[:, :], log[:, :], ACT.Exp, scale=-1.0))
                        act.activation(log[:, :], log[:, :], ACT.Ln, bias=1.0).then_inc(m["z_logged"], 1)
                    elif step == "gate":
                        act.wait_ge(m["z_summed"], i + 1)
                        act.activation((t1, shuf)[i][:, :], t3[:, :], ACT.Exp, scale=1.0 / 16)
                        act.activation((t2, t4)[i][:, :], t3[:, :], ACT.Exp, scale=-1.0 / 16).then_inc(m["z_exped"], 1)
                    elif step == "decay":
                        z = (t1, shuf)[i]
                        act.wait_ge(m["kl_diff"], i + 1)
                        act.activation(z[:, :], z[:, :], ACT.Exp, scale=1.0 / 16).then_inc(m["kl_exped"], 1)
                    elif step == "vtr":
                        act.wait_ge(m["vtr_done"], i + 1)
                        if i < 4:
                            act.activation(v_tok[:, 0:4, i * P:(i + 1) * P],
                                           ps[:, 6 if i == 3 else 7, :].rearrange("p (b n) -> p b n", b=4),
                                           ACT.Copy).then_inc(m["v_out"], 1)
                        else:
                            act.activation(v_tok[0:SAMP, 4, :], ps[0:SAMP, 7, :],
                                           ACT.Copy).then_inc(m["v_out"], 1)
                    elif step == "kltr":
                        act.wait_ge(m["kltr_done"], i + 1)
                        if i < 2:
                            act.activation(klT[:, 0:4, i * P:(i + 1) * P],
                                           ps[:, 4 + i, :].rearrange("p (b n) -> p b n", b=4),
                                           ACT.Copy).then_inc(m["kl_out"], 1)
                        else:
                            act.activation(klT[0:SAMP, 4, :], ps[0:SAMP, 4, 0:2 * P],
                                           ACT.Copy).then_inc(m["kl_out"], 1)
                    elif step == "load_s0":
                        act.wait_ge(m["ss_done"], 1)
                        act.dma_start(s0[:, :, :, :], s0_d[l]).then_inc(m["s0_loaded"], 16)
                        act.dma_start(k_s_d[l, :, :, 0:WIN - NT], kc_d[l, :, :, NT:WIN])\
                           .then_inc(caches_moved, 16)
                        act.dma_start(v_s_d[l, 0:WIN - NT, :, :], vc_d[l, NT:WIN, :, :])\
                           .then_inc(caches_moved, 16)
                    elif step == "silu":
                        act.wait_ge(m["in_used"], JOBS.index(f"rG{i}") + 1)
                        act.activation(rG[:, i, :], rG[:, i, :], ACT.Silu).then_inc(m["r_silu"], 1)
                    elif step == "ssq":
                        act.wait_ge(m["so_out"], 1)
                        act.activation(sq_tile(i), qS[:, i, :], ACT.Square).then_inc(m["ssq"], 1)
                    elif step == "s_norm":
                        act.wait_ge(m["ssum_done"], 1)
                        act.activation(halves(sq_tile(0)), pair(job_pair(JOBS.index("squares"))), ACT.Sqrt,
                                       bias=eps[:, :], scale=1.0 / (4 * P)).then_inc(m["s_root"], 1)
                    elif step == "gss":
                        act.wait_ge(m["gss_done"], 1)
                        act.activation(rt[:, 0:16], ps[:, 4, 0:16], ACT.Sqrt, bias=eps[:, :],
                                       scale=1.0 / P).then_inc(m["g_root"], 1)
                        act.activation(rt[0:SAMP, 16:20], ps[0:SAMP, 4, 16:20], ACT.Sqrt,
                                       bias=eps[0:SAMP, :], scale=1.0 / P).then_inc(m["g_root"], 1)
                    elif step in ("smix", "gmix"):
                        k = i + (4 if step == "gmix" else 0)
                        act.wait_ge(m["mix_made"], k + 1)
                        src = qS[:, i, :] if step == "smix" else a_buf[:, i % 2, :]
                        act.activation(mixed(k)[0], src, ACT.Copy).then_inc(m["mix_high"], 1)
                    elif step == "o":
                        act.wait_ge(m["o_done"], i + 1)
                        for hh in range(2):
                            ins = act.activation(
                                oG[:, hh:4:2, i * P:(i + 1) * P],
                                ps[:, 6 + hh, 0:256].rearrange("p (h n) -> p h n", h=2),
                                ACT.Copy)
                        ins.then_inc(m["o_out"], 1)
                    elif step == "gs_o":
                        act.wait_ge(m["go_done"], 1)
                        for hh in range(2):
                            ins = act.activation(oG[:, hh:4:2, SEQ:T].rearrange("p h (b t) -> p h b t", t=NT),
                                                 go_out()[:, :, :, hh, :], ACT.Copy)
                        ins.then_inc(m["go_out"], 1)
                    elif step == "store_kv":
                        act.wait_ge(m["roped"], 1)
                        act.dma_start(kv_p_d[l, 0], kS[:, SEQ - WIN:T]).then_inc(m["kv_stored"], 16)
                        act.dma_start(kv_p_d[l, 1], vS[:, SEQ - WIN:T]).then_inc(m["kv_stored"], 16)
                    elif step == "store":
                        act.wait_ge(m["state_made"], NCHK)
                        act.dma_start(s_p_d[l], s_ring[:, NCHK % 4, :, :]).then_inc(m["stored"], 16)
                        act.wait_ge(m["gkv_used"], NB)
                        act.dma_start(s_s_d[l], s0[:, :, :, :]).then_inc(m["stored"], 16)
                    elif step == "gsq":
                        act.wait_ge(m["o_out"], NBLK)
                        act.wait_ge(m["go_out"], 1)
                        act.wait_ge(m["mix_made"], 4)
                        act.activation(sq_tile(i), oG[:, i, :], ACT.Square).then_inc(m["gsq"], 1)
                for n in range(KT):
                    if n % 2:
                        high_part(chunk(l, c0 + CH_IN + 4 + n // 2 + RING), n // 2)
                    if n == KT - 1:
                        act.wait_ge(m["stored"], 32)
                        act.sem_inc(mixer_left, 1)
                    square(l, 1, n)

            act.dma_start(g_first[:, :], gains).then_inc(lp_loaded, 16)
            for n in range(KT):
                act.dma_start(x[:, n, :], xT[:, n, :]).then_inc(x_loaded[n], 16)
            act.dma_start(ident[:, :], ident_d).then_inc(start_loaded, 16)
            act.dma_start(bm[:, :], bmask).then_inc(start_loaded, 16)
            for n in range(KT):
                if n % 2 == 0:
                    q = n // 2
                    act.wait_ge(raw_loaded[q % RAW], (q // RAW + 1) * 16)
                    act.wait_ge(chunk_done, q + 1)
                    act.activation(w_hi[:, q, :], w_raw[:, q % RAW, :], ACT.Copy).then_inc(hi_ready, 1)
                dst = ssum[:, :] if n == 0 else sq_buf[:, n % 2, :]
                if n >= 3:
                    act.wait_ge(h_step, 2 * n - 2)
                act.wait_ge(x_loaded[n], 16)
                act.activation(dst, x[:, n, :], ACT.Square).then_inc(sq_ready, 1)
            act.wait_ge(eps_set, 1)
            with act.Fori(0, DEPTH) as l:
                act.wait_ge(h_ready, l * (3 * KT) + KT)
                act.dma_start(lp[:, :], lparams[l]).then_inc(lp_loaded, 16)
                ffn_half(l, 0)
                mixer(l)
                ffn_half(l, 1)
            root(DEPTH * 3)

        @block.vector
        def _(dve):
            def rope_swap():
                return [8 + i if i < 8 else i - 8 if i < 16 else i for i in range(32)]

            def new_h(n, gain, step, squares):
                dve.tensor_scalar(h_hi[:, n, :], x[:, n, :], gain, None, ALU.mult).then_inc(h_step, 1)
                k = n + max(n - 2, 0) + 1
                dve.wait_ge(h_step, step + k)
                dve.scalar_tensor_tensor(out=h_lo[:, n, :], in0=x[:, n, :], scalar=gain,
                                         in1=h_hi[:, n, :].bitcast(F32), op0=ALU.mult,
                                         op1=ALU.subtract).then_inc(h_ready, 1)
                if n >= 2:
                    add_square(n - 1, squares + n, h_step)
                if n == KT - 1:
                    dve.wait_ge(h_step, step + (k + 1))
                    add_square(n, squares + KT, ssum_ready)

            def add_square(n, squares, out_sem):
                dve.wait_ge(sq_ready, squares)
                dve.tensor_tensor(ssum[:, :], ssum[:, :], sq_buf[:, n % 2, :], ALU.add).then_inc(out_sem, 1)

            def scale_ready(phase):
                dve.wait_ge(norm_root, phase + 1)
                dve.reciprocal(rs[:, :], rs[:, :]).then_inc(rs_ready, 1)

            def boundary(l, p, evacuate):
                for n in range(KT):
                    evacuate(n)
                    dve.wait_ge(x_ready, l * (3 * KT) + (p * KT + n + 1))
                    if n == 0:
                        dve.wait_ge(lp_loaded, l * 16 + 32)
                    new_h(n, lp[:, LG + p * KT + n:LG + p * KT + n + 1], l * (3 * B_STEPS) + (p + 1) * B_STEPS,
                          l * (3 * KT) + (p + 1) * KT)

            def ffn_half(l, half):
                cb = l * CH_LAYER + half * (CH_FFN + CH_MIX)
                fb = l * (2 * FT) + half * FT
                scale_ready(l * 3 + half * 2)
                with dve.Fori(0, FT // 2) as i:
                    for q in range(2):
                        if q == 0:
                            dve.wait_ge(rs_ready, l * 3 + (half * 2 + 1))
                        dve.wait_ge(chunk_done, i * 4 + (cb + 2 * q + 1 + RING))
                        dve.tensor_tensor(halves(g_buf[:, q, :]), pair(2 * q), halves(rs[:, :]),
                                          ALU.mult).then_inc(gate_scaled, 1)
                        dve.wait_ge(chunk_done, i * 4 + (cb + 2 * q + 2 + RING))
                        dve.wait_ge(silu_done, i * 2 + (fb + q + 1))
                        dve.tensor_tensor(halves(act_hi[:, i * 2 + q, :]), pair(2 * q + 1),
                                          halves(g_buf[:, q, :]), ALU.mult)
                        dve.tensor_tensor(halves(a_buf[:, q, :]), pair(2 * q + 1),
                                          halves(g_buf[:, q, :]), ALU.mult).then_inc(up_used, 1)
                        dve.wait_ge(up_used, i * 2 + (fb + q + 1))
                        dve.tensor_tensor(act_lo[:, i * 2 + q, :], a_buf[:, q, :],
                                          act_hi[:, i * 2 + q, :].bitcast(F32),
                                          ALU.subtract).then_inc(act_ready, 1)

                def evacuate(n):
                    dve.wait_ge(chunk_done, cb + (CH_GU + DN_CH * (n + 1) + RING))
                    dve.scalar_tensor_tensor(out=halves(a_buf[:, n % 2, :]), in0=pair(n % 4), scalar=0.5,
                                             in1=halves(rs[:, :]), op0=ALU.mult,
                                             op1=ALU.mult).then_inc(down_used, 1)
                    dve.wait_ge(down_used, l * (2 * KT) + (half * KT + n + 1 + 4))
                    dve.tensor_tensor(x[:, n, :], x[:, n, :], a_buf[:, n % 2, :], ALU.add).then_inc(x_ready, 1)

                boundary(l, half * 2, evacuate)

            def mixer(l):
                cb = l * CH_LAYER + CH_FFN
                steps = [0]

                def link(ins):
                    steps[0] += 1
                    ins.then_inc(m["v_step"], 1)
                    dve.wait_ge(m["v_step"], steps[0])

                def stats(u, src, mask, n, w, o, sink):
                    s = s_tile(u).rearrange("p (a n) -> p a n", a=n)[:, :, o:o + w]
                    dve.scalar_tensor_tensor(out=s, in0=src, scalar=HD ** -0.5,
                                             in1=mask.unsqueeze(1).to_broadcast([P, n, w]),
                                             op0=ALU.mult, op1=ALU.add).then_inc(m["masked"], 1)
                    dve.wait_ge(m["masked"], u + 1)
                    q = st[:, u % 2, :]
                    link(dve.tensor_reduce(q[:, 0:n], s, AX_X, ALU.max, negate=True))
                    link(dve.tensor_tensor(q[:, 4:4 + n], q[:, 0:n], nsk[:, sink:sink + n], ALU.min))
                    dve.tensor_tensor(q[:, 8:8 + n], q[:, 4:4 + n], lp[:, SK + sink:SK + sink + n],
                                      ALU.add).then_inc(m["statted"], 1)

                def out_done(half, n):
                    if n % 2:
                        dve.wait_ge(chunk_done, cb + (CH_IN + half * 4 + n // 2 + 1 + RING))
                    else:
                        dve.wait_ge(m["in_done"], 2 + half * 4 + n // 2 + 1)

                def low_part(k, full):
                    dve.wait_ge(m["mix_high"], k + 1)
                    if k == 0:
                        dve.wait_ge(m["kv_stored"], 32)
                    hi, lo = mixed(k)
                    dve.tensor_tensor(lo, full, hi.bitcast(F32),
                                      ALU.subtract).then_inc(m["mix_ready"], 1)

                def klm_mask(b):
                    if b >= 2:
                        dve.wait_ge(m["gkv_done"], b - 1)
                    dve.tensor_scalar(klm[0:SAMP, b % 2, :], klT[0:SAMP, 4, :], bm[0:SAMP, b:b + 1], None,
                                      ALU.mult).then_inc(m["klm_made"], 1)

                for pos, (step, i) in enumerate(STEPS):
                    if step == "load":
                        link(dve.tensor_scalar(nsk[:, :], lp[:, SK:SK + 10], -1.0, None, ALU.mult))
                        link(dve.memset(qz[:, :], 0.0))
                        link(dve.memset(atts[:, :, :, :], 0.0))
                    elif step == "norm":
                        scale_ready(l * 3 + 1)
                        dve.wait_ge(rs_ready, l * 3 + 2)
                    elif step == "scan":
                        link(dve.memset(ssum[:, :], 1.0))
                        link(dve.memset(ssum[:, 0:SEQ].rearrange("p (c n) -> p c n", n=CHUNK)[:, :, 0:1], 0.0))
                        link(dve.memset(ssum[:, SEQ:T].rearrange("p (c n) -> p c n", n=NT)[:, :, 0:1], 0.0))
                    elif step == "evac":
                        name = JOBS[i]
                        src = pair(job_pair(i))
                        if name[:3] == "out":
                            n = int(name[3])
                            out_done(0, n)
                            dve.tensor_tensor(halves(x[:, n, :]), src, halves(x[:, n, :]),
                                              ALU.add).then_inc(m["in_used"], 1)
                            continue
                        if name[0] == "z":
                            pr = int(name[1])
                            dve.wait_ge(m["in_done"], pr + 1)
                            dve.tensor_scalar(halves((t1, shuf)[pr][:, :]), src, lp[:, BG + pr:BG + pr + 1],
                                              None, ALU.add).then_inc(m["in_used"], 1)
                            continue
                        c = in_chunk(name) + (1 if name == "a" else 0)
                        dst = {"kS": kS, "vS": vS, "a": aT}.get(name)
                        if dst is None:
                            t = {"kG": kG, "qG": qG, "vG": vG, "rG": rG, "qS": qS}[name[:2]]
                            dst = t[:, int(name[2]), :]
                        else:
                            dst = dst[:, :]
                        dve.wait_ge(chunk_done, cb + (c + 1 + RING))
                        dve.tensor_tensor(halves(dst), src, halves(rs[:, :]), ALU.mult)\
                           .then_inc(m["in_used"], 1)
                    elif step == "rope":
                        t = kS[:, :] if i == 0 else qS[:, i - 1, :]
                        dve.wait_ge(m["loaded"], 16 * N_LOADS)
                        dve.wait_ge(m["in_used"], (1, 3, 4, 5, 6)[i])
                        link(dve.stream_shuffle(shuf[:, :], t, rope_swap()))
                        link(dve.tensor_tensor(shuf[:, :], shuf[:, :], sin_s[:, :], ALU.mult))
                        link(dve.tensor_tensor(t, t, cos_s[:, :], ALU.mult))
                        dve.tensor_tensor(t, t, shuf[:, :], ALU.add).then_inc(m["roped"], 1)
                        dve.wait_ge(m["roped"], i + 1)
                    elif step == "samp_q":
                        src = qS[:, :, SEQ:T].rearrange("p j (b t) -> p j b t", t=NT)
                        dve.tensor_copy(qc[:, :].rearrange("p (b j t) -> p j b t", b=NB, t=NT), src)
                        ins = dve.tensor_copy(qz[:, :].rearrange("p (b n) -> p b n", n=P + 16)[:, :, 0:16]
                                              .rearrange("p b (j t) -> p j b t", t=NT), src)
                        ins.then_inc(m["q_set"], 1)
                    elif step == "score":
                        b, jj = UNITS[i]
                        o = 0 if b else WIN
                        if i >= 2:
                            dve.wait_ge(m["ptr_done"], i - 1)
                        elif i == 0:
                            dve.wait_ge(m["loaded"], 16 * N_LOADS)
                        dve.wait_ge(m["score_done"], i + 1)
                        src = ps[:, 4:6, :].rearrange("p b n -> p (b n)").rearrange("p (a n) -> p a n", a=4)
                        stats(i, src[:, :, o:256], m_swa[:, o:256], 4, 256 - o, o, 4 * jj)
                    elif step == "samp_s":
                        dve.wait_ge(m["ptr_done"], len(UNITS) - 1)
                        dve.wait_ge(m["ss_done"], 1)
                        stats(len(UNITS), ps[:, 4:6, 0:WIN + SAMP], m_samp[:, :], 2, WIN + SAMP, 0, 8)
                    elif step == "nrm":
                        dve.wait_ge(m["exped"], i + 1)
                        s = st[:, i % 2, :]
                        rows = unit_rows(i)
                        n = len(rows)
                        link(dve.tensor_tensor(s[:, 20:20 + n], s[:, 16:16 + n], s[:, 12:12 + n], ALU.add))
                        link(dve.reciprocal(s[:, 20:20 + n], s[:, 20:20 + n]))
                        for a, cols in rows:
                            ap = s_tile(i)[:, cols]
                            ins = dve.tensor_scalar(ap, ap, s[:, 20 + a:21 + a], None, ALU.mult)
                        ins.then_inc(m["normed"], 1)
                    elif step == "pv":
                        b, jj = UNITS[i]
                        dve.wait_ge(m["pv_done"], i + 1)
                        dve.tensor_copy(qS[:, 2 * jj:2 * jj + 2, b * WIN:(b + 1) * WIN],
                                        ps[:, 6, 0:256].rearrange("p (u n) -> p u n", u=2))\
                           .then_inc(m["attn_out"], 1)
                    elif step == "samp_o":
                        dve.wait_ge(m["so_done"], 1)
                        for g in range(2):
                            rows = slice(g * HD, (g + 1) * HD)
                            ins = dve.tensor_copy(
                                qS[rows, :, SEQ:T].rearrange("p j (b t) -> p j b t", t=NT),
                                ps[rows, 7, g * P:(g + 1) * P].rearrange("p (b j t) -> p j b t", b=NB, t=NT))
                        ins.then_inc(m["so_out"], 1)
                    elif step == "gate":
                        z = (t1, shuf)[i]
                        dve.wait_ge(m["z_logged"], i + 1)
                        link(dve.scalar_tensor_tensor(out=z[:, :], in0=z[:, :], scalar=0.0, in1=(t2, t4)[i][:, :],
                                                      op0=ALU.min, op1=ALU.subtract))
                        dve.tensor_tensor_scan(t3[:, :], ssum[:, :], z[:, :], 0.0, ALU.mult, ALU.add)\
                           .then_inc(m["z_summed"], 1)
                    elif step == "decay":
                        z = (t1, shuf)[i]
                        chunks = ((z[:, 0:SEQ], t3[:, 0:SEQ], CHUNK, 0), (z[:, SEQ:T], t3[:, SEQ:T], NT, 8))
                        dve.wait_ge(m["z_summed"], i + 1)
                        dve.wait_ge(m["z_exped"], i + 1)
                        for zz, _, n, o in chunks:
                            dve.tensor_copy(ebl[:, i, o:o + 8].unsqueeze(2),
                                            zz.rearrange("p (c n) -> p c n", n=n)[:, :, n - 1:n])
                        link(dve.scalar_tensor_tensor(out=qG[:, i, :], in0=qG[:, i, :], scalar=HD ** -0.5,
                                                      in1=z[:, :], op0=ALU.mult, op1=ALU.mult))
                        for zz, bb, n, o in chunks:
                            b3 = bb.rearrange("p (c n) -> p c n", n=n)
                            ins = dve.tensor_tensor(zz.rearrange("p (c n) -> p c n", n=n),
                                                    b3[:, :, n - 1:n].to_broadcast([P, 8, n]), b3,
                                                    ALU.subtract)
                        ins.then_inc(m["kl_diff"], 1)
                    elif step == "keys":
                        z = (t1, shuf)[i]
                        dve.wait_ge(m["kl_exped"], i + 1)
                        dve.tensor_tensor((aT, t1)[i][:, :], kG[:, i, :], z[:, :], ALU.mult)\
                           .then_inc(m["kl_made"], 1)
                        dve.wait_ge(m["kl_made"], i + 1)
                        dve.tensor_tensor(kG[:, i, :], kG[:, i, :], (t2, t4)[i][:, :], ALU.mult).then_inc(m["kb_made"], 1)
                    elif step == "kv":
                        dve.wait_ge(m["kv_done"], i + 1)
                        if i >= 3:
                            dve.wait_ge(m["o_done"], (i - 3) // 2 + 1)
                        if i == 0:
                            ins = dve.tensor_copy(s_ring[:, 1, :, :].rearrange("p a b -> p (a b)"),
                                                  ps[:, 4, 0:256])
                        else:
                            dve.wait_ge(m["state_made"], i)
                            for pr in range(2):
                                ins = dve.scalar_tensor_tensor(
                                    out=s_ring[:, (i + 1) % 4, pr, :], in0=s_ring[:, i % 4, pr, :],
                                    scalar=ebl[:, pr, i:i + 1], in1=ps[:, 4 + i % 2, pr * P:(pr + 1) * P],
                                    op0=ALU.mult, op1=ALU.add)
                        ins.then_inc(m["state_made"], 1)
                    elif step == "att":
                        if i == 0:
                            dve.wait_ge(m["so_done"], 1)
                            link(dve.memset(attm[:, :, :, :, :], 0.0))
                        if i >= 2:
                            dve.wait_ge(m["o_done"], i - 1)
                        dve.wait_ge(m["att_done"], i + 1)
                        for hh in range(2):
                            ins = dve.copy_predicated(attm[:, i % 2, hh, :, :],
                                                      m_gla[:, :].unsqueeze(1).to_broadcast([P, 2, P]),
                                                      ps[:, 4 + hh, 0:256].rearrange("p (h n) -> p h n", h=2))
                        ins.then_inc(m["att_out"], 1)
                    elif step == "gs_att":
                        dve.wait_ge(m["ss_done"], 1)
                        link(dve.memset(qd[:, :, :, :, :], 0.0))
                        for hh in range(2):
                            rows = slice(hh * HD, (hh + 1) * HD)
                            ins = dve.tensor_copy(qd[rows, :, :, hh, :], qG[rows, :, SEQ:T]
                                                  .rearrange("p h (b t) -> p h b t", t=NT))
                        ins.then_inc(m["q_paired"], 1)
                        dve.wait_ge(m["ga_done"], 1)
                        for hh in range(2):
                            ins = dve.copy_predicated(
                                atts[0:SAMP, hh, :, :],
                                m_glas[0:SAMP, :].unsqueeze(1).to_broadcast([SAMP, 2, SAMP]),
                                ps[0:SAMP, 4 + hh, 0:64].rearrange("p (h n) -> p h n", h=2))
                        ins.then_inc(m["ga_out"], 1)
                    elif step == "gs_kv":
                        if i == 0:
                            dve.wait_ge(m["kl_out"], 3)
                            klm_mask(0)
                            dve.wait_ge(m["go_done"], 1)
                        if i + 1 < NB:
                            klm_mask(i + 1)
                        dve.wait_ge(m["gkv_done"], i + 1)
                        for pr in range(2):
                            ins = dve.scalar_tensor_tensor(
                                out=s0[:, i, pr, :], in0=s0[:, i, pr, :], scalar=ebl[:, pr, 8 + i:9 + i],
                                in1=ps[:, 6 + i % 2, pr * P:(pr + 1) * P], op0=ALU.mult, op1=ALU.add)
                        ins.then_inc(m["gkv_used"], 1)
                    elif step == "gss":
                        dve.wait_ge(m["g_root"], 2)
                        dve.reciprocal(rt[:, 0:16], rt[:, 0:16]).then_inc(m["g_recip"], 1)
                        dve.reciprocal(rt[0:SAMP, 16:20], rt[0:SAMP, 16:20]).then_inc(m["g_recip"], 1)
                    elif step == "s_add":
                        dve.wait_ge(m["ssq"], 4)
                        for j in range(1, 3):
                            link(dve.tensor_tensor(sq_tile(0), sq_tile(0), sq_tile(j), ALU.add))
                        dve.tensor_tensor(sq_tile(0), sq_tile(0), sq_tile(3), ALU.add).then_inc(m["s_added"], 1)
                    elif step == "s_norm":
                        dve.wait_ge(m["s_root"], 1)
                        dve.reciprocal(sq_tile(0), sq_tile(0)).then_inc(m["in_used"], 1)
                        dve.wait_ge(m["in_used"], JOBS.index("squares") + 1)
                    elif step == "smix":
                        dve.scalar_tensor_tensor(out=qS[:, i, :], in0=qS[:, i, :],
                                                 scalar=lp[:, SG + i:SG + i + 1], in1=sq_tile(0),
                                                 op0=ALU.mult, op1=ALU.mult).then_inc(m["mix_made"], 1)
                        if i:
                            low_part(i - 1, qS[:, i - 1, :])
                        if i == 3:
                            low_part(3, qS[:, 3, :])
                    elif step == "gmix":
                        dve.wait_ge(m["gbc_done"], i + 1)
                        link(dve.scalar_tensor_tensor(out=oG[:, i, :], in0=oG[:, i, :],
                                                      scalar=lp[:, GG + i:GG + i + 1],
                                                      in1=ps[:, 4 + 2 * (i % 2):6 + 2 * (i % 2), :]
                                                      .rearrange("p b n -> p (b n)")[:, 0:T],
                                                      op0=ALU.mult, op1=ALU.mult))
                        dve.wait_ge(m["r_silu"], i + 1)
                        dve.tensor_tensor(a_buf[:, i % 2, :], oG[:, i, :], rG[:, i, :],
                                          ALU.mult).then_inc(m["mix_made"], 1)
                        if i:
                            low_part(3 + i, a_buf[:, (i - 1) % 2, :])
                        if i == GH - 1:
                            low_part(7, a_buf[:, i % 2, :])

                dve.wait_ge(m["in_used"], len(JOBS))

                def evacuate(n):
                    out_done(1, n)
                    dve.tensor_tensor(halves(x[:, n, :]), pair(n % 4), halves(x[:, n, :]),
                                      ALU.add).then_inc(x_ready, 1)

                boundary(l, 1, evacuate)
                dve.wait_ge(mixer_left, l + 1)
                link(dve.memset(st[:, 0, 0:1], 0.0))
                dve.sem_clear(m_range)

            dve.sem_inc(down_used, 4)
            dve.memset(eps[:, :], EPS).then_inc(eps_set, 1)
            dve.wait_ge(lp_loaded, 16)
            for n in range(KT):
                dve.wait_ge(x_loaded[n], 16)
                new_h(n, g_first[:, n:n + 1], 0, 0)
            with dve.Fori(0, DEPTH) as l:
                ffn_half(l, 0)
                mixer(l)
                ffn_half(l, 1)
            scale_ready(DEPTH * 3)
            dve.wait_ge(rs_ready, DEPTH * 3 + 1)
            for n in range(KT):
                g = LG + 2 * KT + n
                dve.scalar_tensor_tensor(out=x[:, n, :], in0=x[:, n, :], scalar=lp[:, g:g + 1],
                                         in1=rs[:, :], op0=ALU.mult, op1=ALU.mult).then_inc(y_ready, 1)


def constants():
    half = HD // 8
    inv = np.power(np.float32(500000.0), -np.arange(half, dtype=np.float32) * np.float32(2.0 / (2 * half)))
    pos = np.concatenate([np.arange(SEQ), np.tile(PAST + np.arange(NT), NB)]).astype(np.float32)
    ang = (pos[:, None] * inv[None, :].astype(np.float32)).astype(np.float32).T
    cos_t, sin_t = np.ones((2, HD, T), np.float32), np.zeros((2, HD, T), np.float32)
    cos_t[:, 0:half], cos_t[:, half:2 * half] = np.cos(ang), np.cos(ang)
    sin_t[:, 0:half], sin_t[:, half:2 * half] = -np.sin(ang), np.sin(ang)
    q, k = np.arange(P)[:, None], np.arange(P)[None, :]
    low = np.float32(-1e30)
    swa = np.where(np.concatenate([k > q, k <= q], 1), np.float32(0), low)
    b, t = np.arange(P)[:, None] // 16, np.arange(P)[:, None] % NT
    new = np.arange(SAMP)[None, :]
    samp = np.where(np.concatenate([k > t, (new // NT == b) & (new % NT <= t)], 1), np.float32(0), low)
    gla = ((q <= k) & (q // CHUNK == k // CHUNK)).astype(np.int32)
    glas = ((q // NT == new // NT) & (q <= new)).astype(np.int32)
    bm = (q // NT == np.arange(NB)[None, :]).astype(np.float32)
    return {"cos_t": cos_t.reshape(P, T), "sin_t": sin_t.reshape(P, T), "swa_mask": swa, "samp_mask": samp,
            "gla_mask": gla, "glas_mask": glas, "bmask": bm, "ident_d": np.eye(P, dtype=np.float32)}


def weight_stream(w):
    out = np.zeros((CH_ALL, P, KT * P), np.float32)

    def gate_up(a):
        return a.reshape(KT, P, 2, FT, P).transpose(3, 2, 1, 0, 4).reshape(CH_GU, P, KT * P)

    def down(a, dst):
        a = a.reshape(FT, P, KT, P).transpose(2, 1, 0, 3).reshape(KT, P, FT * P)
        for c in range(DN_CH):
            n = min(KT * P, FT * P - c * KT * P)
            dst[c::DN_CH, :, 0:n] = a[:, :, c * KT * P:c * KT * P + n]

    def tile(a):
        return a.reshape(KT, P, -1).transpose(1, 0, 2)

    starts = {"qG": 0, "kG": 256, "vG": 512, "rG": 1024, "a": 1536, "qS": 1552, "kS": 2064, "vS": 2192}
    for l in range(DEPTH):
        o = l * CH_LAYER
        for half, n in enumerate(("1", "2")):
            b = o + half * (CH_FFN + CH_MIX)
            out[b:b + CH_GU] = gate_up(w[f"w_ffn{n}_gu"][l])
            down(w[f"w_ffn{n}_down"][l], out[b + CH_GU:b + CH_FFN])
        b = o + CH_FFN
        w_in = w["w_in"][l]
        for name in IN_TILES:
            c = b + in_chunk(name)
            if name == "a":
                a = tile(w_in[:, 1536:1552])
                for part in range(2):
                    out[c + part].reshape(P, KT, P)[:, 0:4, 0:16] = a[:, 4 * part:4 * part + 4]
                continue
            if name[:2] == "qS":
                j = int(name[2])
                cols = [1552 + h * HD + d for h in (j, 4 + j) for d in range(HD)]
            else:
                s = starts[name[:2]] + (P * int(name[2]) if len(name) == 3 else 0)
                cols = list(range(s, s + P))
            out[c] = tile(w_in[:, cols]).reshape(P, KT * P)
        rows = [4 * P + h * HD + d for j in range(4) for h in (j, 4 + j) for d in range(HD)]
        rows += list(range(4 * P))
        w_out = w["w_out"][l][rows].reshape(2, 4, P, KT // 2, 2, P).transpose(0, 3, 2, 4, 1, 5)
        out[b + CH_IN:b + CH_MIX] = w_out.reshape(KT, P, KT * P)
    return out


def kernel(**inputs):
    import concourse.bacc as _bacc
    from concourse.bass_utils import run_bass_kernel_spmd as _run

    w = {k: np.asarray(v) for k, v in inputs.items()}

    def feat(v):
        return v.reshape(-1, P).T

    tokens = np.concatenate([w["x_prompt"].reshape(SEQ, D), w["x_sample"].reshape(SAMP, D)])
    nexts = [w["norm_ffn1"][l + 1] if l + 1 < DEPTH else w["norm_final"] for l in range(DEPTH)]
    lparams = np.zeros((DEPTH, P, 44), np.float32)
    for l in range(DEPTH):
        sinks = w["attn_sinks"][l].reshape(2, 4)
        lparams[l, :, 0:8] = feat(w["norm_mix"][l])
        lparams[l, :, 8:16] = feat(w["norm_ffn2"][l])
        lparams[l, :, 16:24] = feat(nexts[l])
        lparams[l, :, 24:26] = feat(w["b_gate"][l])
        lparams[l, :, 26:30] = feat(w["gla_norm"][l])
        lparams[l, :, 30:34] = w["swa_norm"][l].reshape(2, 4, HD).transpose(0, 2, 1).reshape(P, 4)
        lparams[l, :, 34:42] = sinks.reshape(2, 2, 2).transpose(1, 0, 2).reshape(8)
        lparams[l, :, 42:44] = np.broadcast_to(sinks.T[None, :, None, :], (NB, 4, NT, 2)).reshape(P, 2)
    arrays = {
        "xT": tokens.T.reshape(KT, P, T).transpose(1, 0, 2),
        "stream": weight_stream(w),
        "gains": feat(w["norm_ffn1"][0]),
        "lparams": lparams,
        "wa2": w["w_gate_up"],
        **constants(),
        "s0_d": w["state_gla"].reshape(DEPTH, NB, 2, 2, HD, P).transpose(0, 3, 4, 1, 2, 5).reshape(DEPTH, P, NB, 2, P),
        "kc_d": w["cache_swa_k"].reshape(DEPTH, NB, WIN, P).transpose(0, 3, 1, 2),
        "vc_d": w["cache_swa_v"].reshape(DEPTH, NB, WIN, P).transpose(0, 2, 1, 3),
    }
    arrays = {k: np.ascontiguousarray(v) for k, v in arrays.items()}
    outs = {"y_d": (P, KT, T), "s_p_d": (DEPTH, P, 2, P), "kv_p_d": (DEPTH, 2, P, WIN + SAMP),
            "s_s_d": (DEPTH, P, NB, 2, P), "k_s_d": (DEPTH, P, NB, WIN - NT), "v_s_d": (DEPTH, WIN - NT, NB, P)}
    nc = _bacc.Bacc("TRN2", target_bir_lowering=False, num_devices=1)
    aps = {k: nc.dram_tensor(k, v.shape, mybir.dt.from_np(v.dtype), kind="ExternalInput").ap()
           for k, v in arrays.items()}
    aps |= {k: nc.dram_tensor(k, v, F32, kind="ExternalOutput").ap() for k, v in outs.items()}
    trunk(nc, **aps)
    r = _run(nc, [arrays], core_ids=[0]).results[0]

    y = r["y_d"].transpose(2, 1, 0).reshape(T, D)
    kv = r["kv_p_d"].transpose(0, 1, 3, 2)
    kv_new = kv[:, :, WIN:].reshape(DEPTH, 2, NB, NT, P)
    k_s = np.concatenate([r["k_s_d"].transpose(0, 2, 3, 1), kv_new[:, 0]], 2)
    v_s = np.concatenate([r["v_s_d"].transpose(0, 2, 1, 3), kv_new[:, 1]], 2)
    s_p = r["s_p_d"].reshape(DEPTH, 1, 2, HD, 2, P).transpose(0, 1, 4, 2, 3, 5).reshape(DEPTH, 1, GH, HD, P)
    s_s = r["s_s_d"].reshape(DEPTH, 2, HD, NB, 2, P).transpose(0, 3, 4, 1, 2, 5).reshape(DEPTH, NB, GH, HD, P)
    return (y[:SEQ].reshape(1, SEQ, D), y[SEQ:].reshape(NB, NT, D), s_p,
            kv[:, 0, :WIN].reshape(DEPTH, 1, WIN, 2, HD), kv[:, 1, :WIN].reshape(DEPTH, 1, WIN, 2, HD),
            s_s, k_s.reshape(DEPTH, NB, WIN, 2, HD), v_s.reshape(DEPTH, NB, WIN, 2, HD))
```
